# Optimizing a Trainium2 kernel written in Bass

```python
import math
import jax, jax.numpy as jnp
from jax import lax
import numpy as np

D_MODEL = 1024
BATCH = 1
SEQ = 2048
DEPTH = 1

N_META = 16
RWKV_WIDTH = D_MODEL // 2
HEAD_DIM = 64
RWKV_HEADS = RWKV_WIDTH // HEAD_DIM
W_LORA = 64
A_LORA = 64
G_LORA = 128
RWKV_PROJ = 3 * RWKV_WIDTH + W_LORA + A_LORA + G_LORA
RWKV_SPLITS = [RWKV_WIDTH, 2 * RWKV_WIDTH, 3 * RWKV_WIDTH, 3 * RWKV_WIDTH + W_LORA, 3 * RWKV_WIDTH + W_LORA + A_LORA]
GN_EPS = 64e-5
S5_WIDTH = D_MODEL // 2
S5_GROUP = 16
S5_GROUPS = S5_WIDTH // S5_GROUP
S5_STATE = 64
N_BRANCH = 2
PROJ_WIDTH = RWKV_PROJ + S5_WIDTH + N_BRANCH * D_MODEL
D_FF = 2816
CONV_W = 3
RMS_EPS = 1e-6

kernel_name = "rwkv7_s5_gated_hybrid_block"

def _rms_norm(x, g):
    xf = x.astype(jnp.float32)
    y = xf * lax.rsqrt(jnp.mean(xf * xf, axis=-1, keepdims=True) + RMS_EPS)
    return (y * g.astype(jnp.float32)).astype(x.dtype)

def _token_shift(p):
    return jnp.pad(p, ((0, 0), (1, 0), (0, 0)))[:, :-1, :]

def _rwkv7_step(S, inp):
    r_t, w_t, k_t, v_t, kk_t, b_t = inp
    sa = jnp.einsum('bhvk,bhk->bhv', S, -kk_t)
    S = S * w_t[:, :, None, :] + sa[..., None] * b_t[:, :, None, :] + v_t[..., None] * k_t[:, :, None, :]
    y = jnp.einsum('bhvk,bhk->bhv', S, r_t)
    return S, y

def _rwkv7_branch(p, mu, w0, w_up, a0, a_up, g_up, k_k, k_a, r_k, ln_g, ln_b, w_branch):
    f32 = jnp.float32
    bsz, t_len, _ = p.shape
    p = p + (_token_shift(p) - p) * mu
    r, k, v, wd, ad, gd = jnp.split(p, RWKV_SPLITS, axis=-1)
    w_log = -jax.nn.softplus(-(w0 + jnp.tanh(wd) @ w_up)) - 0.5
    decay = jnp.exp(-jnp.exp(w_log.astype(f32)))
    a = jax.nn.sigmoid(a0 + ad @ a_up)
    g = jax.nn.sigmoid(gd) @ g_up

    def heads(t):
        return t.astype(f32).reshape(bsz, t_len, RWKV_HEADS, HEAD_DIM)

    kk = heads(k * k_k)
    kk = kk / jnp.maximum(jnp.linalg.norm(kk, axis=-1, keepdims=True), 1e-12)
    k = k * (1 + (a - 1) * k_a)
    r_h, k_h, v_h, w_h, a_h = heads(r), heads(k), heads(v), heads(decay), heads(a)

    def tm(t):
        return jnp.moveaxis(t, 1, 0)

    s0 = jnp.zeros((bsz, RWKV_HEADS, HEAD_DIM, HEAD_DIM), f32)
    _, y = lax.scan(_rwkv7_step, s0, (tm(r_h), tm(w_h), tm(k_h), tm(v_h), tm(kk), tm(kk * a_h)))
    y = jnp.moveaxis(y, 0, 1)
    mean = jnp.mean(y, axis=-1, keepdims=True)
    var = jnp.mean(jnp.square(y - mean), axis=-1, keepdims=True)
    y = ((y - mean) * lax.rsqrt(var + GN_EPS)).reshape(bsz, t_len, RWKV_WIDTH)
    y = y * ln_g.astype(f32) + ln_b.astype(f32)
    bonus = jnp.sum(r_h * k_h * r_k.astype(f32), axis=-1, keepdims=True) * v_h
    y = (y + bonus.reshape(bsz, t_len, RWKV_WIDTH)) * g.astype(f32)
    return y.astype(p.dtype) @ w_branch

def _ssm_combine(e1, e2):
    a1, b1 = e1
    a2, b2 = e2
    return a1 * a2, a2 * b1 + b2

def _s5_branch(u, lam_re, lam_im, log_dt, b_re, b_im, c_re, c_im, d, w_glu):
    f32 = jnp.float32
    bsz, t_len, _ = u.shape
    ut = jnp.moveaxis(u.astype(f32).reshape(bsz, t_len, S5_GROUPS, S5_GROUP), 1, 0)
    lam = lax.complex(jnp.minimum(lam_re.astype(f32), -1e-4), lam_im.astype(f32))
    dt = jnp.exp(log_dt.astype(f32))[:, None]
    lam_bar = jnp.exp(lam * dt)
    b_bar = ((lam_bar - 1) / lam)[..., None] * lax.complex(b_re.astype(f32), b_im.astype(f32))
    bu = jnp.einsum('tbgh,gnh->tbgn', ut.astype(jnp.complex64), b_bar)
    a_el = jnp.broadcast_to(lam_bar, (t_len, 1) + lam_bar.shape)
    _, xs = lax.associative_scan(_ssm_combine, (a_el, bu), axis=0)
    c = lax.complex(c_re.astype(f32), c_im.astype(f32))
    y = jnp.einsum('tbgn,ghn->tbgh', xs, c).real + d.astype(f32).reshape(S5_GROUPS, S5_GROUP) * ut
    y = jnp.moveaxis(y, 0, 1).reshape(bsz, t_len, S5_WIDTH)
    y = jax.nn.gelu(y).astype(u.dtype)
    z = y @ w_glu
    return z[..., :D_MODEL] * jax.nn.sigmoid(z[..., D_MODEL:])

def _causal_dwconv(a, w, b):
    c = w.shape[-1]
    y = lax.conv_general_dilated(a, w[:, None, :].astype(a.dtype), window_strides=(1,),
                                 padding=[(CONV_W - 1, 0)], dimension_numbers=('NWC', 'WIO', 'NWC'),
                                 feature_group_count=c)
    return y + b

def setup_inputs(seed: int = 0) -> dict:
    key = jax.random.key(seed)
    ks = iter(jax.random.split(key, 40))
    L = DEPTH

    def nrm(shape, scale):
        return jax.random.normal(next(ks), shape, jnp.float32) * scale

    def unif(shape, lo, hi):
        return jax.random.uniform(next(ks), shape, jnp.float32, lo, hi)

    lam_im0 = jnp.broadcast_to(math.pi * jnp.arange(S5_STATE, dtype=jnp.float32), (L, S5_GROUPS, S5_STATE))
    return {
        "x": nrm((BATCH, SEQ, D_MODEL), 1.0),
        "meta_tokens": nrm((N_META, D_MODEL), 1.0),
        "norm_mix_pre": 1.0 + nrm((L, D_MODEL), 0.02),
        "norm_mix_post": 1.0 + nrm((L, D_MODEL), 0.02),
        "w_in": nrm((L, D_MODEL, PROJ_WIDTH), D_MODEL ** -0.5),
        "rwkv_shift_mu": unif((L, RWKV_PROJ), 0.0, 1.0),
        "rwkv_w0": unif((L, RWKV_WIDTH), -6.0, 1.0),
        "rwkv_w_up": nrm((L, W_LORA, RWKV_WIDTH), 0.1),
        "rwkv_a0": nrm((L, RWKV_WIDTH), 0.1),
        "rwkv_a_up": nrm((L, A_LORA, RWKV_WIDTH), 0.1),
        "rwkv_g_up": nrm((L, G_LORA, RWKV_WIDTH), G_LORA ** -0.5),
        "rwkv_k_k": 0.85 + nrm((L, RWKV_WIDTH), 0.02),
        "rwkv_k_a": 1.0 + nrm((L, RWKV_WIDTH), 0.02),
        "rwkv_r_k": nrm((L, RWKV_HEADS, HEAD_DIM), 0.1),
        "rwkv_ln_gain": 1.0 + nrm((L, RWKV_WIDTH), 0.02),
        "rwkv_ln_bias": nrm((L, RWKV_WIDTH), 0.02),
        "rwkv_w_branch": nrm((L, RWKV_WIDTH, D_MODEL), RWKV_WIDTH ** -0.5),
        "s5_lambda_re": -0.5 + nrm((L, S5_GROUPS, S5_STATE), 0.01),
        "s5_lambda_im": lam_im0 + nrm((L, S5_GROUPS, S5_STATE), 0.01),
        "s5_log_dt": unif((L, S5_GROUPS), math.log(1e-3), math.log(1e-1)),
        "s5_b_re": nrm((L, S5_GROUPS, S5_STATE, S5_GROUP), (2 * S5_GROUP) ** -0.5),
        "s5_b_im": nrm((L, S5_GROUPS, S5_STATE, S5_GROUP), (2 * S5_GROUP) ** -0.5),
        "s5_c_re": nrm((L, S5_GROUPS, S5_GROUP, S5_STATE), (2 * S5_STATE) ** -0.5),
        "s5_c_im": nrm((L, S5_GROUPS, S5_GROUP, S5_STATE), (2 * S5_STATE) ** -0.5),
        "s5_d": nrm((L, S5_WIDTH), 1.0),
        "s5_w_glu": nrm((L, S5_WIDTH, 2 * D_MODEL), S5_WIDTH ** -0.5),
        "w_out": nrm((L, D_MODEL, D_MODEL), D_MODEL ** -0.5),
        "norm_ffn_pre": 1.0 + nrm((L, D_MODEL), 0.02),
        "norm_ffn_post": 1.0 + nrm((L, D_MODEL), 0.02),
        "ffn_w_up": nrm((L, D_MODEL, 2 * D_FF), D_MODEL ** -0.5),
        "ffn_conv_w": nrm((L, CONV_W, D_FF), CONV_W ** -0.5),
        "ffn_conv_b": nrm((L, D_FF), 0.02),
        "ffn_w_down": nrm((L, D_FF, D_MODEL), D_FF ** -0.5),
    }

def reference(x, meta_tokens, norm_mix_pre, norm_mix_post, w_in, rwkv_shift_mu, rwkv_w0, rwkv_w_up,
              rwkv_a0, rwkv_a_up, rwkv_g_up, rwkv_k_k, rwkv_k_a, rwkv_r_k, rwkv_ln_gain, rwkv_ln_bias,
              rwkv_w_branch, s5_lambda_re, s5_lambda_im, s5_log_dt, s5_b_re, s5_b_im, s5_c_re, s5_c_im,
              s5_d, s5_w_glu, w_out, norm_ffn_pre, norm_ffn_post, ffn_w_up, ffn_conv_w, ffn_conv_b,
              ffn_w_down):
    bsz = x.shape[0]
    meta = jnp.broadcast_to(meta_tokens[None].astype(x.dtype), (bsz, N_META, D_MODEL))
    h = jnp.concatenate([meta, x], axis=1)
    for l in range(DEPTH):
        hn = _rms_norm(h, norm_mix_pre[l])
        proj = hn @ w_in[l]
        p_rwkv = proj[..., :RWKV_PROJ]
        u_s5 = proj[..., RWKV_PROJ:RWKV_PROJ + S5_WIDTH]
        gates = jax.nn.sigmoid(proj[..., RWKV_PROJ + S5_WIDTH:])
        y_a = _rwkv7_branch(p_rwkv, rwkv_shift_mu[l], rwkv_w0[l], rwkv_w_up[l], rwkv_a0[l], rwkv_a_up[l],
                            rwkv_g_up[l], rwkv_k_k[l], rwkv_k_a[l], rwkv_r_k[l], rwkv_ln_gain[l],
                            rwkv_ln_bias[l], rwkv_w_branch[l])
        y_b = _s5_branch(u_s5, s5_lambda_re[l], s5_lambda_im[l], s5_log_dt[l], s5_b_re[l], s5_b_im[l],
                         s5_c_re[l], s5_c_im[l], s5_d[l], s5_w_glu[l])
        mix = (gates[..., :D_MODEL] * y_a + gates[..., D_MODEL:] * y_b) @ w_out[l]
        h = h + _rms_norm(mix, norm_mix_post[l])
        hn = _rms_norm(h, norm_ffn_pre[l])
        up = hn @ ffn_w_up[l]
        a = _causal_dwconv(up[..., :D_FF], ffn_conv_w[l], ffn_conv_b[l])
        f = (jax.nn.gelu(a, approximate=True) * up[..., D_FF:]) @ ffn_w_down[l]
        h = h + _rms_norm(f, norm_ffn_post[l])
    return h[:, N_META:, :]


_drawn_inputs = setup_inputs


def setup_inputs(seed=0):
    import zlib

    import numpy as np

    out = dict(_drawn_inputs(seed))
    spreads = {}
    factors = {'norm_mix_post': 3.649,
     'rwkv_k_k': 4.097,
     'rwkv_k_a': 3.924,
     'rwkv_ln_gain': 4.059,
     'rwkv_ln_bias': 4.277,
     's5_lambda_re': 200.0,
     'norm_ffn_pre': 10.521,
     'norm_ffn_post': 46.655,
     'ffn_conv_b': 13.727,
     's5_lambda_im': 64.0,
     's5_log_dt': 64.0,
     's5_b_re': 64.0,
     's5_b_im': 64.0,
     's5_c_re': 64.0,
     's5_c_im': 64.0}
    for name, (base, spread) in spreads.items():
        noise = np.random.default_rng([zlib.crc32(name.encode()), seed]).standard_normal(out[name].shape)
        drawn = base * np.exp(spread * noise) if base else spread * noise
        out[name] = __import__('jax').numpy.asarray(drawn.astype(out[name].dtype))
    for name, factor in factors.items():
        out[name] = (out[name] * factor).astype(out[name].dtype)
    return out
```

```python
import math
from contextlib import ExitStack

import concourse.bass as bass
from concourse import mybir

F32 = mybir.dt.float32
F32R = mybir.dt.float32r
BF16 = mybir.dt.bfloat16
ALU = mybir.AluOpType
ACT = mybir.ActivationFunctionType

P = 128
D_MODEL, SEQ, N_META = 1024, 2048, 16
T = N_META + SEQ
KD = D_MODEL // P
SLOTS = 2
RMS_EPS, GN_EPS = 1e-6, 64e-5

RWKV_WIDTH, HEAD_DIM = D_MODEL // 2, 64
PAIRS = RWKV_WIDTH // P
RWKV_PROJ = 3 * RWKV_WIDTH + 256
CHUNK = 64
CHUNKS = -(-T // CHUNK)
ROLE_A, ROLE_B, ROLE_K, ROLE_R, ROLE_V = range(5)

S5_GROUPS, S5_GROUP, S5_STATE = 32, 16, 64
S5_CHUNK = P // S5_GROUP
S5_CHUNKS = T // S5_CHUNK
CT = 3
NT_ROWS = S5_CHUNKS // CT

M_RWKV, M_GATE = RWKV_PROJ // P, 2 * D_MODEL // P
D_FF, CONV_W = 2816, 3
M_FF = D_FF // P
K4 = RWKV_WIDTH // P
N_BLOCKS = 6
N_TOK = T // N_BLOCKS

COLUMNS = (("mu", M_RWKV), ("w0", PAIRS), ("a0", PAIRS), ("k_k", PAIRS), ("k_a", PAIRS), ("r_k", PAIRS), ("ln_g", PAIRS),
           ("ln_b", PAIRS), ("mix_pre", KD), ("ffn_pre", KD), ("conv_w", CONV_W * M_FF), ("conv_b", M_FF))
COL = {name: sum(n for _, n in COLUMNS[:j]) for j, (name, _) in enumerate(COLUMNS)}
N_COLS = sum(n for _, n in COLUMNS)

ROUNDER = 1.5 * 2.0 ** 23


def two_pi_parts():
    parts, rest = [], 2 * math.pi
    for bits in (8, 10):
        unit = 2.0 ** (math.floor(math.log2(rest)) - bits + 1)
        parts.append(math.floor(rest / unit) * unit)
        rest -= parts[-1]
    return parts + [rest]


TWO_PI_PARTS = two_pi_parts()


def norm_transpose(nc, name, sems, psum, src, x_hi, x_lo, gain, ident):
    rows_loaded, squares_done, std_ready, rstd_ready, rows_normed, turned, gained_ready, hi_ready, lo_ready, \
        eps_ready = sems(name, [("rows_loaded", 2), "squares_done", "std_ready", "rstd_ready", "rows_normed",
                                "turned", "gained_ready", "hi_ready", "lo_ready", "eps_ready"])
    with ExitStack() as ctx:
        sb = lambda n, shape, dt: ctx.enter_context(nc.sbuf_tensor(f"{name}_{n}", shape, dt))
        rows = sb("rows", [NT_ROWS, SLOTS, D_MODEL], F32)
        normed = sb("normed", [NT_ROWS, SLOTS, D_MODEL], F32)
        squares = sb("squares", [NT_ROWS, D_MODEL], F32)
        stat = sb("stat", [NT_ROWS, SLOTS, 3], F32)
        eps = sb("eps", [NT_ROWS, 1], F32)
        gained = sb("gained", [P, SLOTS, KD, NT_ROWS], F32)
        block = ctx.enter_context(nc.Block())
        PAIRS = T // NT_ROWS // SLOTS

        def turned_ps(u):
            return psum[:, 2 * u:2 * u + 2, 0:4 * NT_ROWS].rearrange("p b (k t) -> p b k t", k=4)

        @block.sync
        def _(sp):
            with sp.Fori(0, PAIRS) as i:
                for u in range(SLOTS):
                    sp.wait_ge(rows_normed, 2 * i + u + 1)
                    sp.dma_start(rows[:, u, :], src[bass.ds((2 * i + u) * NT_ROWS, NT_ROWS), :]).then_inc(rows_loaded[u], 16)

        @block.scalar
        def _(act):
            act.wait_ge(eps_ready, 1)
            with act.Fori(0, PAIRS) as i:
                for u in range(SLOTS):
                    act.wait_ge(rows_loaded[u], 16 * i + 16)
                    act.wait_ge(rows_normed, 2 * i + u + 1)
                    act.wait_ge(squares_done, 2 * i + u)
                    nc.scalar.activation(squares[:], rows[:, u, :], ACT.Square, accum_out=stat[:, u, 0:1]).then_inc(squares_done, 1)
                    act.wait_ge(squares_done, 2 * i + u + 1)
                    nc.scalar.activation(stat[:, u, 1:2], stat[:, u, 0:1], ACT.Sqrt, scale=1.0 / D_MODEL, bias=eps[:]).then_inc(std_ready, 1)
                    act.wait_ge(gained_ready, 2 * i + u + 1 + SLOTS)
                    nc.scalar.activation(x_hi[:, :, bass.ds((2 * i + u) * NT_ROWS, NT_ROWS)], gained[:, u], ACT.Copy).then_inc(hi_ready, 1)

        @block.vector
        def _(dve):
            dve.sem_inc(rows_normed, SLOTS)
            dve.sem_inc(gained_ready, SLOTS)
            dve.sem_inc(lo_ready, SLOTS)
            nc.vector.memset(eps[:], RMS_EPS).then_inc(eps_ready, 1)
            with dve.Fori(0, PAIRS) as i:
                for u in range(SLOTS):
                    dve.wait_ge(std_ready, 2 * i + u + 1)
                    nc.vector.reciprocal(stat[:, u, 2:3], stat[:, u, 1:2]).then_inc(rstd_ready, 1)
                    dve.wait_ge(rstd_ready, 2 * i + u + 1)
                    dve.wait_ge(turned, 2 * i + u + 1)
                    nc.vector.tensor_scalar(normed[:, u, :], rows[:, u, :], stat[:, u, 2:3], None, ALU.mult).then_inc(rows_normed, 1)
                    dve.wait_ge(turned, 2 * i + u + 1 + SLOTS)
                    dve.wait_ge(lo_ready, 2 * i + u + 1)
                    nc.vector.tensor_tensor(gained[:, u].rearrange("p (b k) t -> p b k t", b=2), turned_ps(u),
                                            gain.rearrange("p (b k) -> p b k", b=2).unsqueeze(3).broadcast_to([P, 2, 4, NT_ROWS]), ALU.mult).then_inc(gained_ready, 1)
                    dve.wait_ge(hi_ready, 2 * i + u + 1)
                    nc.vector.tensor_tensor(x_lo[:, :, bass.ds((2 * i + u) * NT_ROWS, NT_ROWS)], gained[:, u],
                                            x_hi[:, :, bass.ds((2 * i + u) * NT_ROWS, NT_ROWS)].bitcast(F32), ALU.subtract).then_inc(lo_ready, 1)

        @block.tensor
        def _(pe):
            pe.sem_inc(turned, SLOTS)
            with pe.Fori(0, PAIRS) as i:
                for u in range(SLOTS):
                    pe.wait_ge(rows_normed, 2 * i + u + 1 + SLOTS)
                    pe.wait_ge(gained_ready, 2 * i + u + 1)
                    for k in range(KD):
                        mm = nc.tensor.transpose(turned_ps(u)[:, k // 4, k % 4, :], normed[:, u, k * P:(k + 1) * P],
                                                 ident[0:NT_ROWS, 0:NT_ROWS])
                    mm.then_inc(turned, 1)


def in_projection(nc, name, sems, psum, x_hi, x_lo, w_tiles, mu, rwkv_out, gate_out):
    weight_loaded, split_hi, split_lo, products_done, evacuated, difference_ready, mixed_ready, stored, pad_ready = sems(name, [
        ("weight_loaded", 2), "split_hi", "split_lo", "products_done", "evacuated", "difference_ready", "mixed_ready",
        ("stored", 2), "pad_ready"])
    with ExitStack() as ctx:
        sb = lambda n, shape, dt: ctx.enter_context(nc.sbuf_tensor(f"{name}_{n}", shape, dt))
        weight = sb("weight", [P, SLOTS, KD, P], F32)
        w_hi = sb("w_hi", [P, SLOTS, KD, P], F32R)
        w_lo = sb("w_lo", [P, SLOTS, KD, P], F32R)
        pre = sb("pre", [P, SLOTS, 2 + T], F32)
        mixed = sb("mixed", [P, SLOTS, T], F32)
        block = ctx.enter_context(nc.Block())

        LAST = (M_RWKV + M_GATE) // 2 - 1

        def tile_loop(eng, body):
            with eng.Fori(0, M_RWKV // 2) as i:
                for u in range(SLOTS):
                    body(2 * i + u, i, u, True)
            with eng.Fori(M_RWKV // 2, LAST) as i:
                for u in range(SLOTS):
                    body(2 * i + u, i, u, False)
            for u in range(SLOTS):
                body(2 * LAST + u, LAST, u, False)

        @block.sync
        def _(sp):
            def load(m, u):
                sp.wait_ge(split_lo, m + 1)
                sp.dma_start(weight[:, u], w_tiles[bass.ds(m, 1)].rearrange("o p k c -> p (o k) c")).then_inc(weight_loaded[u], 16)

            def store_rwkv(m, u):
                sp.wait_ge(mixed_ready, m + 1 + SLOTS)
                sp.dma_start(rwkv_out[bass.ds(m, 1)].rearrange("o p t -> p (o t)"), mixed[:, u, :]).then_inc(stored[u], 16)

            def store_gate(m, u):
                sp.wait_ge(evacuated, m * N_BLOCKS + 2 * N_BLOCKS)
                sp.dma_start(gate_out[bass.ds(m - M_RWKV, 1)].rearrange("o p t -> p (o t)"), mixed[:, u, :]).then_inc(stored[u], 16)
            for u in range(SLOTS):
                load(u, u)
            for first, last, store in ((1, M_RWKV // 2 + 1, store_rwkv), (M_RWKV // 2 + 1, LAST + 1, store_gate)):
                with sp.Fori(first, last) as i:
                    for u in range(SLOTS):
                        load(2 * i + u, u)
                        store(2 * i - 2 + u, u)
            for u in range(SLOTS):
                store_gate(2 * LAST + u, u)
            for u in range(SLOTS):
                sp.wait_ge(stored[u], 16 * (M_RWKV + M_GATE) // 2)

        @block.tensor
        def _(pe):
            pe.sem_inc(products_done, SLOTS * N_BLOCKS)

            def tile(m, i, u, rwkv):
                pe.wait_ge(split_hi, m + 1)
                pe.wait_ge(split_lo, m + 1 + SLOTS)
                for n in range(N_BLOCKS):
                    pe.wait_ge(evacuated, m * N_BLOCKS + n + 1)
                    cols = slice(n * N_TOK, (n + 1) * N_TOK)
                    for k in range(KD):
                        for w, x in ((w_hi, x_hi), (w_hi, x_lo), (w_lo, x_hi)):
                            mm = nc.tensor.matmul(psum[:, n, 0:N_TOK], w[:, u, k, :], x[:, k, cols],
                                                  start=(k == 0 and w is w_hi and x is x_hi), stop=(k == KD - 1 and w is w_lo))
                    mm.then_inc(products_done, 1)
            tile_loop(pe, tile)

        @block.scalar
        def _(act):
            act.sem_inc(evacuated, N_BLOCKS)
            act.wait_ge(pad_ready, 1)

            def split(m, i, u):
                if u == 0 and isinstance(i, int) and i > LAST:
                    return
                act.wait_ge(weight_loaded[u], 16 * i + 16)
                act.wait_ge(products_done, (m + 1) * N_BLOCKS)
                nc.scalar.activation(w_hi[:, u], weight[:, u], ACT.Copy).then_inc(split_hi, 1)

            split(0, 0, 0)

            def tile(m, i, u, rwkv):
                split(m + 1, i + u, 1 - u)
                if rwkv:
                    act.wait_ge(mixed_ready, m + 1)
                else:
                    act.wait_ge(stored[u], 16 * i)
                for n in range(N_BLOCKS):
                    act.wait_ge(products_done, (m + SLOTS) * N_BLOCKS + n + 1)
                    if rwkv:
                        nc.scalar.activation(pre[:, u, 2 + n * N_TOK:2 + (n + 1) * N_TOK], psum[:, n, 0:N_TOK], ACT.Copy).then_inc(evacuated, 1)
                    else:
                        nc.scalar.activation(mixed[:, u, n * N_TOK:(n + 1) * N_TOK], psum[:, n, 0:N_TOK], ACT.Sigmoid).then_inc(evacuated, 1)
            tile_loop(act, tile)

        @block.vector
        def _(dve):
            nc.vector.memset(pre[:, :, 0:2], 0.0).then_inc(pad_ready, 1)
            dve.sem_inc(split_lo, SLOTS)
            dve.sem_inc(mixed_ready, SLOTS)

            def split(m, i, u):
                if u == 0 and isinstance(i, int) and i > LAST:
                    return
                dve.wait_ge(weight_loaded[u], 16 * i + 16)
                dve.wait_ge(split_hi, m + 1)
                nc.vector.tensor_tensor(w_lo[:, u], weight[:, u], w_hi[:, u].bitcast(F32), ALU.subtract).then_inc(split_lo, 1)

            split(0, 0, 0)

            def tile(m, i, u, rwkv):
                split(m + 1, i + u, 1 - u)
                if not rwkv:
                    return
                dve.wait_ge(evacuated, (m + 2) * N_BLOCKS)
                dve.wait_ge(stored[u], 16 * i)
                nc.vector.tensor_tensor(mixed[:, u, :], pre[:, u, 1:1 + T], pre[:, u, 2:2 + T], ALU.subtract).then_inc(difference_ready, 1)
                dve.wait_ge(difference_ready, m + 1)
                nc.vector.scalar_tensor_tensor(mixed[:, u, :], mixed[:, u, :], mu[:, bass.ds(m, 1)], pre[:, u, 2:2 + T],
                                               ALU.mult, ALU.add).then_inc(mixed_ready, 1)
            tile_loop(dve, tile)


def s5_inputs(nc, name, sems, psum, x_hi, x_lo, w_dram, u_out, ident):
    HG = S5_GROUPS // 2
    COLS = HG * S5_GROUP
    weight_loaded, split_hi, split_lo, products_done, evacuated, turned, turned_out, stored = sems(name, [
        "weight_loaded", "split_hi", "split_lo", "products_done", "evacuated", "turned", "turned_out", "stored"])
    with ExitStack() as ctx:
        sb = lambda n, shape, dt: ctx.enter_context(nc.sbuf_tensor(f"{name}_{n}", shape, dt))
        weight = sb("weight", [P, KD, COLS], F32)
        w_hi = sb("w_hi", [P, KD, COLS], F32R)
        w_lo = sb("w_lo", [P, KD, COLS], F32R)
        rows = sb("rows", [NT_ROWS, SLOTS, HG, S5_CHUNK, S5_GROUP], F32)
        cols = sb("cols", [P, HG, NT_ROWS], F32)
        block = ctx.enter_context(nc.Block())

        @block.sync
        def _(sp):
            with sp.Fori(0, 2) as half:
                sp.wait_ge(split_lo, half)
                sp.dma_start(weight[:], w_dram[bass.ds(half, 1)].rearrange("o p k n -> p (o k) n")).then_inc(weight_loaded, 16)
                for ct in range(CT):
                    sp.wait_ge(turned_out, half * CT + (ct + 1))
                    sp.dma_start(u_out[:, bass.ds(half * HG, HG), ct * NT_ROWS:(ct + 1) * NT_ROWS], cols[:]).then_inc(stored, 16)
            sp.wait_ge(stored, 16 * 2 * CT)

        @block.tensor
        def _(pe):
            with pe.Fori(0, 2) as half:
                def products(ct):
                    for tau in range(S5_CHUNK):
                        pe.wait_ge(evacuated, half * (CT * S5_CHUNK) + (ct * S5_CHUNK + tau + 1))
                        first = ct * NT_ROWS * S5_CHUNK + tau
                        for k in range(KD):
                            for x, w in ((x_hi, w_hi), (x_hi, w_lo), (x_lo, w_hi)):
                                mm = nc.tensor.matmul(psum[0:NT_ROWS, tau % 4, 0:COLS], x[:, k, first:first + (NT_ROWS - 1) * S5_CHUNK + 1:S5_CHUNK], w[:, k, :],
                                                      start=(k == 0 and x is x_hi and w is w_hi), stop=(k == KD - 1 and x is x_lo))
                        mm.then_inc(products_done, 1)

                def turn(ct):
                    pe.wait_ge(evacuated, half * (CT * S5_CHUNK) + ((ct + 1) * S5_CHUNK + 4))
                    pe.wait_ge(turned_out, half * CT + ct)
                    for g in range(HG):
                        mm = nc.tensor.transpose(psum[:, 4 + g // 4, (g % 4) * NT_ROWS:(g % 4 + 1) * NT_ROWS],
                                                 rows[:, ct % 2, g].rearrange("c t h -> c (t h)"), ident[0:NT_ROWS, 0:NT_ROWS])
                    mm.then_inc(turned, 1)
                pe.wait_ge(split_hi, half + 1)
                pe.wait_ge(split_lo, half + 1)
                products(0)
                for ct in range(1, CT):
                    products(ct)
                    turn(ct - 1)
                turn(CT - 1)

        @block.scalar
        def _(act):
            act.sem_inc(evacuated, 4)
            with act.Fori(0, 2) as half:
                act.wait_ge(weight_loaded, 16 * half + 16)
                act.wait_ge(products_done, half * (CT * S5_CHUNK))
                nc.scalar.activation(w_hi[:], weight[:], ACT.Copy).then_inc(split_hi, 1)
                for ct in range(CT):
                    if ct >= 2:
                        act.wait_ge(turned, half * CT + (ct - 1))
                    else:
                        act.wait_ge(turned, half * CT)
                    for tau in range(S5_CHUNK):
                        act.wait_ge(products_done, half * (CT * S5_CHUNK) + (ct * S5_CHUNK + tau + 1))
                        nc.scalar.activation(rows[:, ct % 2, :, tau, :], psum[0:NT_ROWS, tau % 4, 0:COLS].rearrange("c (g h) -> c g h", h=S5_GROUP),
                                             ACT.Copy).then_inc(evacuated, 1)

        @block.vector
        def _(dve):
            with dve.Fori(0, 2) as half:
                dve.wait_ge(split_hi, half + 1)
                nc.vector.tensor_tensor(w_lo[:], weight[:], w_hi[:].bitcast(F32), ALU.subtract).then_inc(split_lo, 1)
                for ct in range(CT):
                    dve.wait_ge(turned, half * CT + (ct + 1))
                    dve.wait_ge(stored, half * (16 * CT) + 16 * ct)
                    nc.vector.tensor_copy(cols[:].rearrange("p (b g) c -> p b (g c)", b=4), psum[:, 4:8, 0:4 * NT_ROWS]).then_inc(turned_out, 1)


class Count:

    def __init__(self, sem):
        self.sem, self.n = sem, 0

    def __call__(self, instruction):
        instruction.then_inc(self.sem, 1)
        self.n += 1


def s5_scan(nc, name, sems, psum, params, u_in, y_out, ident):
    G, H, C, N = S5_GROUPS, S5_GROUP, S5_CHUNK, S5_CHUNKS
    HG = G // 2
    J = C + 1
    names = ["params_loaded", "act_small", "small_ready", "u_loaded", "tables_built", "e_turned", "e_ready", "kernel_done",
             "kernel_ready", "toeplitz_loaded", "toeplitz_ready", "zeroed", "injected", "inject_used", "state_ready",
             "y_done", "y_ready", "y_turned", "y_flat", "stored", "dve_done", "pads_ready"]
    (params_loaded, act_small, small_ready, u_loaded, tables_built, e_turned, e_ready, kernel_done,
     kernel_ready, toeplitz_loaded, toeplitz_ready, zeroed, injected, inject_used, state_ready,
     y_done, y_ready, y_turned, y_flat, stored, dve_done, pads_ready) = sems(name, names)
    with ExitStack() as ctx:
        sb = lambda n, shape, dt=F32: ctx.enter_context(nc.sbuf_tensor(f"{name}_{n}", shape, dt))
        lam_re, lam_im, log_dt, skip = (sb(n, [P, G]) for n in ("lam_re", "lam_im", "log_dt", "skip"))
        b_re, b_im, c_re, c_im = (sb(n, [P, G, H]) for n in ("b_re", "b_im", "c_re", "c_im"))
        small = sb("small", [P, 16, G])
        dt, rate, theta, turns, angle, quarter, mag, rho, cosine, sine, den, coef_re, coef_im, t0, t1, t2 = (small[:, j, :] for j in range(16))
        pw_re = sb("pw_re", [P, J, G])
        pw_im = sb("pw_im", [P, J, G])
        pw_1 = sb("pw_1", [P, J, G])
        pw_2 = sb("pw_2", [P, J, G])
        pw_ft = sb("pw_ft", [P, 2, C, G])
        pw_t = sb("pw_t", [P, 2, C, G])
        q_1 = sb("q_1", [P, G])
        q_2 = sb("q_2", [P, G])
        b_s = sb("b_s", [P, G, H])
        b_x = sb("b_x", [P, G, H])
        b_t = sb("b_t", [P, G, H])
        phase = sb("phase", [P, 4, G])
        out_1 = sb("out_1", [P, HG, J, H])
        out_2 = sb("out_2", [P, HG, J, H])
        tmp = sb("tmp", [P, HG, J, H])
        in_1 = sb("in_1", [P, HG, C, H])
        in_2 = sb("in_2", [P, HG, C, H])
        in_t = sb("in_t", [P, 2, HG, P])
        kernel_t = sb("kernel_t", [H, HG, P])
        toeplitz = sb("toeplitz", [P, HG, P])
        cos_t = sb("cos_t", [P, HG, N])
        sin_t = sb("sin_t", [P, HG, N])
        u = sb("u", [P, HG, N])
        drive = sb("drive", [P, 2, N])
        drive_b = sb("drive_b", [P, 2, N])
        z = sb("z", [P, 2, N])
        part_c = sb("part_c", [P, 2, 1 + N])
        part_s = sb("part_s", [P, 2, 1 + N])
        y_rows = sb("y_rows", [NT_ROWS, CT, C, HG, H])
        y_cols = sb("y_cols", [P, 2, T])
        turn_tmp = y_cols[:].rearrange("p k t -> p (k t)")[:, 0:HG * P].rearrange("p (g c) -> p g c", g=HG)
        block = ctx.enter_context(nc.Block())
        LO, HI = slice(0, P // 2), slice(P // 2, P)

        @block.sync
        def _(sp):
            for tile, key in ((lam_re, "lam_re"), (lam_im, "lam_im"), (log_dt, "log_dt"), (skip, "skip"),
                              (b_re, "b_re"), (b_im, "b_im"), (c_re, "c_re"), (c_im, "c_im")):
                sp.dma_start(tile[:], params[key]).then_inc(params_loaded, 16)
            for half in range(2):
                sp.wait_ge(y_done, half * HG)
                sp.dma_start(u[:], u_in[:, half * HG:(half + 1) * HG, :]).then_inc(u_loaded, 16)
                sp.wait_ge(kernel_ready, half + 1)
                sp.wait_ge(zeroed, 1)
                for tau in range(C):
                    sp.dma_start(toeplitz[tau * H:(tau + 1) * H, :, tau * H:], kernel_t[:, :, 0:P - tau * H]).then_inc(toeplitz_loaded, 16)
                for kt in range(2):
                    sp.wait_ge(y_flat, 6 * (2 * half + kt + 1))
                    sp.dma_start(y_out[2 * half + kt], y_cols[:, kt, :]).then_inc(stored, 16)
            sp.wait_ge(stored, 64)

        @block.gpsimd
        def _(pool):
            pool.memset(toeplitz[:], 0.0).then_inc(zeroed, 1)

        @block.scalar
        def _(act):
            act.wait_ge(params_loaded, 16 * 8)
            nc.scalar.activation(dt, log_dt[:], ACT.Exp).then_inc(act_small, 1)
            act.wait_ge(small_ready, 1)
            nc.scalar.activation(mag, rate, ACT.Exp).then_inc(act_small, 1)
            nc.scalar.activation(rho, rate, ACT.Exp, scale=float(C)).then_inc(act_small, 1)
            act.wait_ge(small_ready, 2)
            nc.scalar.activation(sine, angle, ACT.Sin).then_inc(act_small, 1)
            nc.scalar.activation(cosine, quarter, ACT.Sin).then_inc(act_small, 1)
            for half in range(2):
                for j in range(2):
                    act.wait_ge(e_turned, 2 * half + j + 1)
                    nc.scalar.activation(in_t[:, j].rearrange("p (b g) c -> p b (g c)", b=4), psum[:, 4 * j:4 * j + 4, :], ACT.Copy).then_inc(e_ready, 1)
                for g in range(HG):
                    if g == 0:
                        act.wait_ge(y_turned, 12 * half)
                    act.wait_ge(y_done, half * HG + g + 1)
                    nc.scalar.activation(y_rows[:, :, :, g, :], psum[0:NT_ROWS, 4 + g % 2, 0:CT * P].rearrange("c (t a h) -> c t a h", t=CT, h=H),
                                         ACT.Gelu_apprx_tanh).then_inc(y_ready, 1)

        @block.vector
        def _(dve):
            own = Count(dve_done)

            def settle():
                dve.wait_ge(dve_done, own.n)

            def tt(out, a, b, op):
                own(nc.vector.tensor_tensor(out, a, b, op))

            def ts(out, a, s1, s2, op0, op1=None):
                own(nc.vector.tensor_scalar(out, a, s1, s2, op0, op1) if op1 is not None else nc.vector.tensor_scalar(out, a, s1, None, op0))

            def complex_product(out_re, out_im, a_re, a_im, b_re, b_im, s, t):
                tt(out_re, a_re, b_re, ALU.mult)
                tt(s, a_im, b_im, ALU.mult)
                tt(out_im, a_re, b_im, ALU.mult)
                tt(t, a_im, b_re, ALU.mult)
                settle()
                tt(out_re, out_re, s, ALU.subtract)
                tt(out_im, out_im, t, ALU.add)
                settle()

            own(nc.vector.memset(part_c[:, :, 0:1], 0.0))
            own(nc.vector.memset(part_s[:, :, 0:1], 0.0))
            dve.wait_ge(params_loaded, 16 * 8)
            ts(lam_re[:], lam_re[:], -1e-4, None, ALU.min)
            dve.wait_ge(act_small, 1)
            settle()
            tt(theta, lam_im[:], dt, ALU.mult)
            nc.vector.tensor_tensor(rate, lam_re[:], dt, ALU.mult).then_inc(small_ready, 1)
            settle()
            ts(turns, theta, 1.0 / (2 * math.pi), None, ALU.mult)
            settle()
            ts(turns, turns, ROUNDER, None, ALU.add)
            settle()
            ts(turns, turns, ROUNDER, None, ALU.subtract)
            own(nc.vector.tensor_copy(angle, theta))
            settle()
            for piece in TWO_PI_PARTS:
                ts(t0, turns, piece, None, ALU.mult)
                settle()
                tt(angle, angle, t0, ALU.subtract)
                settle()
            ts(angle, angle, math.pi, -math.pi, ALU.min, ALU.max)
            settle()
            own(nc.vector.scalar_tensor_tensor(quarter, angle, -1.0, angle, ALU.mult, ALU.min))
            settle()
            nc.vector.tensor_scalar(quarter, quarter, math.pi / 2, None, ALU.add).then_inc(small_ready, 1)
            dve.wait_ge(act_small, 5)
            own(nc.vector.memset(pw_re[:, 0, :], 1.0))
            own(nc.vector.memset(pw_im[:, 0, :], 0.0))
            tt(pw_re[:, 1, :], mag, cosine, ALU.mult)
            tt(pw_im[:, 1, :], mag, sine, ALU.mult)
            settle()
            for n in (1, 2, 4):
                by_re = pw_re[:, n:n + 1, :].broadcast_to([P, n, G])
                by_im = pw_im[:, n:n + 1, :].broadcast_to([P, n, G])
                complex_product(pw_re[:, n + 1:2 * n + 1, :], pw_im[:, n + 1:2 * n + 1, :], pw_re[:, 1:n + 1, :], pw_im[:, 1:n + 1, :], by_re, by_im,
                                pw_t[:, 0, 0:n, :], pw_t[:, 1, 0:n, :])
            tt(t0, lam_re[:], lam_re[:], ALU.mult)
            tt(t1, lam_im[:], lam_im[:], ALU.mult)
            ts(t2, pw_re[:, 1, :], -1.0, None, ALU.add)
            settle()
            tt(den, t0, t1, ALU.add)
            settle()
            own(nc.vector.reciprocal(den, den))
            tt(coef_re, t2, lam_re[:], ALU.mult)
            tt(t0, pw_im[:, 1, :], lam_im[:], ALU.mult)
            tt(coef_im, pw_im[:, 1, :], lam_re[:], ALU.mult)
            tt(t1, t2, lam_im[:], ALU.mult)
            settle()
            tt(coef_re, coef_re, t0, ALU.add)
            tt(coef_im, coef_im, t1, ALU.subtract)
            settle()
            tt(coef_re, coef_re, den, ALU.mult)
            tt(coef_im, coef_im, den, ALU.mult)
            settle()
            own(nc.vector.tensor_copy(pw_1[LO], pw_re[LO]))
            ts(pw_1[HI], pw_im[HI], -1.0, None, ALU.mult)
            own(nc.vector.tensor_copy(pw_2[LO], pw_im[LO]))
            own(nc.vector.tensor_copy(pw_2[HI], pw_re[HI]))
            own(nc.vector.tensor_copy(q_1[LO], coef_re[LO]))
            own(nc.vector.tensor_copy(q_1[HI], coef_im[HI]))
            own(nc.vector.tensor_copy(q_2[LO], coef_im[LO]))
            ts(q_2[HI], coef_re[HI], -1.0, None, ALU.mult)
            for tau in range(C):
                own(nc.vector.tensor_copy(pw_ft[:, 0, tau, :], pw_re[:, C - 1 - tau, :]))
                own(nc.vector.tensor_copy(pw_ft[:, 1, tau, :], pw_im[:, C - 1 - tau, :]))
            settle()
            wide = lambda x: x.unsqueeze(2).broadcast_to([P, G, H])
            tt(b_s[:], b_re[:], wide(q_1[:]), ALU.mult)
            tt(b_t[:], b_im[:], wide(q_2[:]), ALU.mult)
            tt(b_x[:], b_re[:], wide(q_2[:]), ALU.mult)
            settle()
            tt(b_s[:], b_s[:], b_t[:], ALU.subtract)
            settle()
            tt(b_t[:], b_im[:], wide(q_1[:]), ALU.mult)
            settle()
            tt(b_x[:], b_x[:], b_t[:], ALU.add)
            settle()
            ts(b_x[:], b_x[:], -1.0, None, ALU.mult)
            own(nc.vector.tensor_copy(phase[:, 0, :], cosine))
            own(nc.vector.tensor_copy(phase[:, 1, :], sine))
            settle()
            at = 0

            def square_phase(at):
                r, i, r2, i2 = (phase[:, (at + j) % 4, :] for j in range(4))
                complex_product(r2, i2, r, i, r, i, t0, t1)
                return (at + 2) % 4
            for _ in range(3):
                at = square_phase(at)
            own(nc.vector.tensor_copy(t2, phase[:, at, :]))
            own(nc.vector.tensor_copy(den, phase[:, at + 1, :]))
            settle()
            for half in range(2):
                gs = slice(half * HG, (half + 1) * HG)
                over_h = lambda x, j0, j1: x[:, j0:j1, gs].rearrange("p j g -> p g j").unsqueeze(3).broadcast_to([P, HG, j1 - j0, H])
                over_j = lambda x, n: x[:, gs, :].unsqueeze(2).broadcast_to([P, HG, n, H])
                if half:
                    dve.wait_ge(y_done, half * HG)
                tt(out_1[:], over_j(c_re, J), over_h(pw_1, 0, J), ALU.mult)
                tt(tmp[:], over_j(c_im, J), over_h(pw_2, 0, J), ALU.mult)
                settle()
                tt(out_1[:], out_1[:], tmp[:], ALU.subtract)
                tt(out_2[:], over_j(c_re, J), over_h(pw_2, 0, J), ALU.mult)
                settle()
                tt(tmp[:], over_j(c_im, J), over_h(pw_1, 0, J), ALU.mult)
                settle()
                tt(out_2[:], out_2[:], tmp[:], ALU.add)
                settle()
                ts(out_2[:], out_2[:], -1.0, None, ALU.mult)
                tmp_c = tmp[:, :, 0:C, :]
                settle()
                tt(in_1[:], over_j(b_s, C), over_h(pw_ft[:, 0], 0, C), ALU.mult)
                tt(tmp_c, over_j(b_x, C), over_h(pw_ft[:, 1], 0, C), ALU.mult)
                settle()
                tt(in_1[:], in_1[:], tmp_c, ALU.add)
                tt(in_2[:], over_j(b_s, C), over_h(pw_ft[:, 1], 0, C), ALU.mult)
                settle()
                tt(tmp_c, over_j(b_x, C), over_h(pw_ft[:, 0], 0, C), ALU.mult)
                settle()
                nc.vector.tensor_tensor(in_2[:], in_2[:], tmp_c, ALU.subtract).then_inc(tables_built, 1)
                if half:
                    dve.wait_ge(stored, 32)
                own(nc.vector.memset(cos_t[:, :, 0:1], 1.0))
                own(nc.vector.memset(sin_t[:, :, 0:1], 0.0))
                own(nc.vector.tensor_copy(phase[:, 0, :], t2))
                own(nc.vector.tensor_copy(phase[:, 1, :], den))
                settle()
                at, n = 0, 1
                while n < N:
                    m = min(n, N - n)
                    by = lambda j: phase[:, at + j, gs].unsqueeze(2).broadcast_to([P, HG, m])
                    scr = tmp[:].rearrange("p g j h -> p g (j h)")
                    scr2 = turn_tmp
                    complex_product(cos_t[:, :, n:n + m], sin_t[:, :, n:n + m], cos_t[:, :, 0:m], sin_t[:, :, 0:m], by(0), by(1),
                                    scr[:, :, 0:m], scr2[:, :, 0:m])
                    at = square_phase(at) if 2 * n < N else at
                    n += m
                dve.wait_ge(kernel_done, half + 1)
                nc.vector.tensor_copy(kernel_t[:].rearrange("p (b g) c -> p b (g c)", b=4), psum[0:H, 0:4, :]).then_inc(kernel_ready, 1)
                dve.wait_ge(toeplitz_loaded, 16 * C * (half + 1))
                for g in range(HG):
                    last = nc.vector.scalar_tensor_tensor(toeplitz[:, g, :], ident, skip[:, half * HG + g:half * HG + g + 1], toeplitz[:, g, :], ALU.mult, ALU.add)
                    own(last)
                settle()
                dve.sem_inc(toeplitz_ready, 1)
                for g in range(HG):
                    s = half * HG + g
                    v = s % 2
                    cos_g, sin_g = cos_t[:, g, :], sin_t[:, g, :]
                    dve.wait_ge(injected, s + 1)
                    tt(drive[:, v, :], cos_g, psum[:, 2 * v, 0:N], ALU.mult)
                    nc.vector.tensor_tensor(drive_b[:, v, :], sin_g, psum[:, 2 * v + 1, 0:N], ALU.mult).then_inc(inject_used, 1)
                    dve.wait_ge(inject_used, s + 1)
                    settle()
                    tt(drive[:, v, :], drive[:, v, :], drive_b[:, v, :], ALU.add)
                    settle()
                    own(nc.vector.tensor_tensor_scan(z[:, v, :], rho[:, s:s + 1].broadcast_to([P, N]), drive[:, v, :], 0.0, ALU.mult, ALU.add))
                    if s >= 2:
                        dve.wait_ge(y_done, s - 1)
                    settle()
                    nc.vector.tensor_tensor(part_c[:, v, 1:], cos_g, z[:, v, :], ALU.mult).then_inc(state_ready, 1)
                    nc.vector.tensor_tensor(part_s[:, v, 1:], sin_g, z[:, v, :], ALU.mult).then_inc(state_ready, 1)
                for kt in range(2):
                    for ct in range(CT):
                        for th in range(2):
                            e = (kt * CT + ct) * 2 + th
                            dve.wait_ge(y_turned, 12 * half + e + 1)
                            if half:
                                dve.wait_ge(stored, 32)
                            first = ct * NT_ROWS * C + th * 4
                            dst = y_cols[:, kt, ct * NT_ROWS * C:(ct + 1) * NT_ROWS * C].rearrange("p (c a) -> p a c", a=C)[:, 4 * th:4 * th + 4, :]
                            nc.vector.tensor_copy(dst, psum[:, 6 + e % 2, 0:4 * NT_ROWS].rearrange("p (a c) -> p a c", a=4)).then_inc(y_flat, 1)

        @block.tensor
        def _(pe):
            for half in range(2):
                pe.wait_ge(tables_built, half + 1)
                if half:
                    pe.wait_ge(y_ready, half * HG)
                    pe.wait_ge(y_flat, 12 * half)
                for j, table in enumerate((in_1, in_2)):
                    for g in range(HG):
                        mm = nc.tensor.transpose(psum[:, 4 * j + g // 4, (g % 4) * P:(g % 4 + 1) * P], table[:, g].rearrange("p a h -> p (a h)"), ident)
                    mm.then_inc(e_turned, 1)
                pe.wait_ge(e_ready, 2 * half + 1)
                for g in range(HG):
                    mm = nc.tensor.matmul(psum[0:H, g // 4, (g % 4) * P:(g % 4 + 1) * P], b_s[:, half * HG + g, :],
                                          out_1[:, g, 0:C, :].rearrange("p a h -> p (a h)"), start=True, stop=True)
                mm.then_inc(kernel_done, 1)
                pe.wait_ge(e_ready, 2 * half + 2)
                pe.wait_ge(u_loaded, 16 * (half + 1))
                pe.wait_ge(kernel_ready, half + 1)

                def inject(g):
                    s = half * HG + g
                    v = s % 2
                    if s >= 2:
                        pe.wait_ge(inject_used, s - 1)
                    for j in range(2):
                        mm = nc.tensor.matmul(psum[:, 2 * v + j, 0:N], in_t[:, j, g, :], u[:, g, :], start=True, stop=True)
                    mm.then_inc(injected, 1)

                def outputs(g):
                    s = half * HG + g
                    v = s % 2
                    if s >= 2:
                        pe.wait_ge(y_ready, s - 1)
                    pe.wait_ge(state_ready, 2 * s + 2)
                    for ct in range(CT):
                        at = slice(ct * NT_ROWS, (ct + 1) * NT_ROWS)
                        y = psum[0:NT_ROWS, 4 + v, ct * P:(ct + 1) * P]
                        nc.tensor.matmul(y, u[:, g, at], toeplitz[:, g, :], start=True, stop=False)
                        nc.tensor.matmul(y, part_c[:, v, at], out_1[:, g, 1:, :].rearrange("p a h -> p (a h)"), start=False, stop=False)
                        mm = nc.tensor.matmul(y, part_s[:, v, at], out_2[:, g, 1:, :].rearrange("p a h -> p (a h)"), start=False, stop=True)
                    mm.then_inc(y_done, 1)
                inject(0)
                pe.wait_ge(toeplitz_ready, half + 1)
                for g in range(HG):
                    if g + 1 < HG:
                        inject(g + 1)
                    outputs(g)
                pe.wait_ge(y_ready, (half + 1) * HG)
                for kt in range(2):
                    for ct in range(CT):
                        for th in range(2):
                            e = (kt * CT + ct) * 2 + th
                            if 12 * half + e >= 2:
                                pe.wait_ge(y_flat, 12 * half + e - 1)
                            for a in range(4):
                                mm = nc.tensor.transpose(psum[:, 6 + e % 2, a * NT_ROWS:(a + 1) * NT_ROWS],
                                                         y_rows[:, ct, 4 * th + a, 8 * kt:8 * kt + 8, :].rearrange("c g h -> c (g h)"),
                                                         ident[0:NT_ROWS, 0:NT_ROWS])
                            mm.then_inc(y_turned, 1)


def rwkv_prepare(nc, name, sems, psum, proj, lora, cols, prep, bonus_out, gate_out, chunk_decay):
    names = [("tile_loaded", 3), "lora_loaded", "lora_ready", "products_done", "act_done", "dve_done", "sums_done", "mask_ready",
             ("role_stored", 6), "zeroed", "ones_ready"]
    (tile_loaded, lora_loaded, lora_ready, products_done, act_done, dve_done, sums_done, mask_ready,
     role_stored, zeroed, ones_ready) = sems(name, names)
    DECAY = math.exp(-0.5)
    NB = N_BLOCKS
    with ExitStack() as ctx:
        sb = lambda n, shape, dt=F32: ctx.enter_context(nc.sbuf_tensor(f"{name}_{n}", shape, dt))
        ups = sb("ups", [P, 2, RWKV_WIDTH])
        low = sb("low", [P, 2, T])
        rkv = sb("rkv", [P, 3, T])
        sig = sb("sig", [P, T])
        a = sb("a", [P, T])
        cs = sb("cs", [P, T])
        cs_prev = sb("cs_prev", [P, T])
        kk = sb("kk", [P, T])
        work = sb("work", [P, T])
        role = sb("role", [P, 4, T])
        bonus = sb("bonus", [P, T])
        gate = sb("gate", [P, T])
        mask = sb("mask", [P, T])
        heads = sb("heads", [P, P])
        one_less = sb("one_less", [P, PAIRS])
        block = ctx.enter_context(nc.Block())
        col = lambda key, j: cols[:, COL[key] + j:COL[key] + j + 1]
        NB_COLS = [slice(n * N_TOK, (n + 1) * N_TOK) for n in range(NB)]
        A_STEPS, V_STEPS = 9, 15

        @block.sync
        def _(sp):
            sp.dma_start(ups[:], lora).then_inc(lora_loaded, 16)
            sp.dma_start(low[:, 0, :], proj[3 * PAIRS]).then_inc(lora_loaded, 16)
            sp.dma_start(low[:, 1, :], proj[3 * PAIRS + 1]).then_inc(lora_loaded, 16)
            for j in range(PAIRS):
                for n in range(3):
                    if j:
                        sp.wait_ge(dve_done, V_STEPS * j)
                    sp.dma_start(rkv[:, n, :], proj[n * PAIRS + j]).then_inc(tile_loaded[n], 16)
                for n, src in enumerate([role[:, 0, :], role[:, 1, :], role[:, 2, :], role[:, 3, :], bonus[:], gate[:]]):
                    sp.wait_ge(dve_done, V_STEPS * j + V_STEPS)
                    sp.wait_ge(act_done, A_STEPS * j + A_STEPS)
                    dst = prep[n, j] if n < 4 else (bonus_out[j] if n == 4 else gate_out[j])
                    sp.dma_start(dst, src).then_inc(role_stored[n], 16)
            for n in range(6):
                sp.wait_ge(role_stored[n], 16 * PAIRS)

        @block.tensor
        def _(pe):
            pe.wait_ge(lora_ready, 2)
            pe.wait_ge(mask_ready, 3)
            for j in range(PAIRS):
                c = slice(j * P, (j + 1) * P)
                plan = [(ups[0:64, 0, c], low[0:64, 0, :]), (ups[64:128, 0, c], low[64:128, 0, :]), (ups[:, 1, c], low[:, 1, :])]
                for q, (w, x) in enumerate(plan):
                    pe.wait_ge(act_done, A_STEPS * j + q if q else (A_STEPS * j))
                    if q == 0 and j:
                        pe.wait_ge(dve_done, V_STEPS * j)
                    for n in range(NB):
                        mm = nc.tensor.matmul(psum[:, n, 0:N_TOK], w, x[:, NB_COLS[n]], start=True, stop=True)
                    mm.then_inc(products_done, 1)
                pe.wait_ge(act_done, A_STEPS * j + 4)
                for n in range(NB):
                    mm = nc.tensor.matmul(psum[:, n, 0:N_TOK], heads[:], work[:, NB_COLS[n]], start=True, stop=True)
                mm.then_inc(sums_done, 1)
                pe.wait_ge(dve_done, V_STEPS * j + 14)
                for n in range(NB):
                    mm = nc.tensor.matmul(psum[:, n, 0:N_TOK], heads[:], work[:, NB_COLS[n]], start=True, stop=True)
                mm.then_inc(sums_done, 1)

        blocks = psum[:, 0:NB, 0:N_TOK]
        split = lambda t: t.rearrange("p (n c) -> p n c", n=NB)

        @block.scalar
        def _(act):
            act.wait_ge(lora_loaded, 48)
            nc.scalar.activation(low[0:64, 0, :], low[0:64, 0, :], ACT.Tanh).then_inc(lora_ready, 1)
            nc.scalar.activation(low[:, 1, :], low[:, 1, :], ACT.Sigmoid).then_inc(lora_ready, 1)
            for j in range(PAIRS):
                if j:
                    act.wait_ge(dve_done, V_STEPS * j)
                step = lambda ins: ins.then_inc(act_done, 1)
                act.wait_ge(products_done, 3 * j + 1)
                step(nc.scalar.activation(split(sig[:]), blocks, ACT.Sigmoid, bias=col("w0", j)))
                act.wait_ge(products_done, 3 * j + 2)
                step(nc.scalar.activation(split(a[:]), blocks, ACT.Sigmoid, bias=col("a0", j)))
                act.wait_ge(products_done, 3 * j + 3)
                if j:
                    act.wait_ge(role_stored[5], 16 * j)
                step(nc.scalar.activation(split(gate[:]), blocks, ACT.Copy))
                act.wait_ge(dve_done, V_STEPS * j + 1)
                step(nc.scalar.activation(work[:], kk[:], ACT.Square))
                act.wait_ge(dve_done, V_STEPS * j + 3)
                step(nc.scalar.activation(cs_prev[:], cs_prev[:], ACT.Exp, scale=-DECAY))
                step(nc.scalar.activation(sig[:], cs[:], ACT.Exp, scale=-DECAY))
                act.wait_ge(act_done, A_STEPS * j + 6)
                step(nc.scalar.activation(cs[:], cs[:], ACT.Exp, scale=DECAY))
                nc.scalar.activation(chunk_decay[:, j, :], sig[:, N_META - 1:T:CHUNK], ACT.Copy).then_inc(act_done, 1)
                act.wait_ge(sums_done, 2 * j + 1)
                step(nc.scalar.activation(split(work[:]), blocks, ACT.Sqrt))

        @block.vector
        def _(dve):
            nc.vector.memset(heads[:], 0.0).then_inc(zeroed, 1)
            nc.vector.memset(mask[:], 1.0).then_inc(zeroed, 1)
            dve.wait_ge(zeroed, 2)
            nc.vector.memset(heads[0:64, 0:64], 1.0).then_inc(mask_ready, 1)
            nc.vector.memset(heads[64:128, 64:128], 1.0).then_inc(mask_ready, 1)
            nc.vector.memset(mask[:, N_META:T:CHUNK], 0.0).then_inc(mask_ready, 1)
            dve.wait_ge(mask_ready, 3)
            nc.vector.tensor_scalar(one_less[:], cols[:, COL["k_a"]:COL["k_a"] + PAIRS], -1.0, 1.0, ALU.mult, ALU.add).then_inc(ones_ready, 1)
            dve.wait_ge(ones_ready, 1)
            for j in range(PAIRS):
                r, k, v = (rkv[:, n, :] for n in range(3))
                at = V_STEPS * j
                step = lambda ins: ins.then_inc(dve_done, 1)
                A = A_STEPS * j
                dve.wait_ge(tile_loaded[1], 16 * j + 16)
                step(nc.vector.tensor_scalar(kk[:], k, col("k_k", j), None, ALU.mult))
                dve.wait_ge(act_done, A + 1)
                step(nc.vector.tensor_tensor_scan(cs[:], mask[:], sig[:], 0.0, ALU.mult, ALU.add))
                dve.wait_ge(dve_done, at + 2)
                step(nc.vector.tensor_tensor(cs_prev[:], cs[:], sig[:], ALU.subtract))
                dve.wait_ge(act_done, A + 2)
                if j:
                    dve.wait_ge(role_stored[4], 16 * j)
                step(nc.vector.tensor_scalar(bonus[:], a[:], col("k_a", j), one_less[:, j:j + 1], ALU.mult, ALU.add))
                dve.wait_ge(dve_done, at + 4)
                step(nc.vector.tensor_tensor(bonus[:], k, bonus[:], ALU.mult))
                dve.wait_ge(tile_loaded[0], 16 * j + 16)
                dve.wait_ge(act_done, A + 7)
                dve.wait_ge(dve_done, at + 5)
                if j:
                    for n in range(4):
                        dve.wait_ge(role_stored[n], 16 * j)
                step(nc.vector.tensor_tensor(role[:, ROLE_K, :], bonus[:], cs[:], ALU.mult))
                step(nc.vector.tensor_tensor(role[:, ROLE_R, :], r, sig[:], ALU.mult))
                dve.wait_ge(act_done, A + 9)
                step(nc.vector.tensor_scalar(work[:], work[:], 1e-12, None, ALU.max))
                dve.wait_ge(dve_done, at + 8)
                step(nc.vector.reciprocal(work[:], work[:]))
                dve.wait_ge(dve_done, at + 9)
                step(nc.vector.tensor_tensor(kk[:], kk[:], work[:], ALU.mult))
                dve.wait_ge(dve_done, at + 10)
                step(nc.vector.scalar_tensor_tensor(role[:, ROLE_A, :], kk[:], -1.0, cs_prev[:], ALU.mult, ALU.mult))
                step(nc.vector.tensor_tensor(kk[:], kk[:], a[:], ALU.mult))
                dve.wait_ge(dve_done, at + 12)
                step(nc.vector.tensor_tensor(role[:, ROLE_B, :], kk[:], cs[:], ALU.mult))
                step(nc.vector.scalar_tensor_tensor(work[:], r, col("r_k", j), bonus[:], ALU.mult, ALU.mult))
                dve.wait_ge(dve_done, at + 14)
                dve.wait_ge(sums_done, 2 * j + 2)
                dve.wait_ge(tile_loaded[2], 16 * j + 16)
                step(nc.vector.tensor_tensor(split(bonus[:]), blocks, split(v), ALU.mult))


def rwkv_chunks(nc, name, sems, psum, prep, v_dram, chunk_decay, masks_dram, bonus_dram, gate_dram, cols, y_out, ident):
    NC_, S = CHUNKS, CHUNK
    (masks_loaded, roles_loaded, roles_free, cleared, grams_done, masked, toks_done, toks_ready, x1_turned, x1_ready,
     lx_done, q_ready, xq_done, x_ready, xt_turned, xt_ready, w_done, w_ready, u_done, u_ready, m_done, m_ready,
     y_done, y_ready, norm_own, normed, y_turned, y_flat, sq_done, sq_ready, post_loaded, post_own, stored, eps_set, std_done,
     m_half, q_init) = sems(name, [
         "masks_loaded", ("roles_loaded", 2), "roles_free", "cleared", "grams_done", "masked", "toks_done", "toks_ready",
         "x1_turned", "x1_ready", "lx_done", "q_ready", "xq_done", "x_ready", "xt_turned", "xt_ready", "w_done", "w_ready",
         "u_done", "u_ready", "m_done", "m_ready", "y_done", "y_ready", "norm_own", "normed", "y_turned", "y_flat",
         "sq_done", "sq_ready", ("post_loaded", 2), "post_own", "stored", "eps_set", "std_done", "m_half", "q_init"])
    with ExitStack() as ctx:
        sb = lambda n, shape, dt=F32: ctx.enter_context(nc.sbuf_tensor(f"{name}_{n}", shape, dt))
        masks = sb("masks", [P, 8, P])
        roles = sb("roles", [P, 2, 5, PAIRS, 2, S])
        grams = sb("grams", [P, 2, 3, PAIRS, P])
        toks = sb("toks", [P, 2, 3, PAIRS, P])
        l_t = sb("l_t", [P, PAIRS, P])
        x = sb("x", [P, PAIRS, P])
        x_t = sb("x_t", [P, 2, PAIRS, P])
        q = sb("q", [P, PAIRS, P])
        w = sb("w", [P, PAIRS, P])
        u = sb("u", [P, PAIRS, P])
        m = sb("m", [P, 2, PAIRS, P])
        y = sb("y", [P, PAIRS, HEAD_DIM])
        y_sq = sb("y_sq", [P, PAIRS, HEAD_DIM])
        y_bd = sb("y_bd", [P, PAIRS, 2, HEAD_DIM])
        stat = sb("stat", [P, 4, PAIRS])
        eps = sb("eps", [P, 1])
        y_all = sb("y_all", [P, PAIRS, NC_ * S])
        post = sb("post", [P, 2, T])
        block = ctx.enter_context(nc.Block())
        HALVES = (slice(0, 2), slice(2, 4))
        LEVELS = 5
        wide = lambda mk, n: masks[:, mk, :].unsqueeze(1).broadcast_to([P, n, P])
        bank = lambda b: psum[:, b, :].rearrange("p (j c) -> p j c", j=PAIRS)
        half_bank = lambda b: psum[:, b, 0:2 * P].rearrange("p (j c) -> p j c", j=2)
        flat = lambda ap: ap.rearrange("p j h c -> p j (h c)")

        def at(eng, sem, per, c, n):
            eng.wait_ge(sem, per * c + n)

        @block.sync
        def _(sp):
            sp.dma_start(masks[:], masks_dram).then_inc(masks_loaded, 16)
            sp.wait_ge(cleared, 1)

            def load(c, v, t0, n):
                sp.wait_ge(roles_free, c + 1)
                for h in range(2):
                    rows = slice(h * 64, (h + 1) * 64)
                    for r in range(5):
                        src = (prep[r] if r < 4 else v_dram)[:, rows, bass.ds(t0, n)]
                        sp.dma_start(roles[rows, v, r, :, h, S - n:S], src.rearrange("j p t -> p j t")).then_inc(roles_loaded[v], 16)
            load(0, 0, 0, N_META)
            with sp.Fori(0, (NC_ - 1) // 2) as i:
                load(2 * i + 1, 1, i * (2 * S) + N_META, S)
                load(2 * i + 2, 0, i * (2 * S) + (N_META + S), S)
            for j in range(PAIRS):
                sp.wait_ge(post_own, 3 * j)
                sp.dma_start(post[:, 0, :], bonus_dram[j]).then_inc(post_loaded[0], 16)
                sp.dma_start(post[:, 1, :], gate_dram[j]).then_inc(post_loaded[1], 16)
                sp.wait_ge(post_own, 3 * j + 3)
                sp.dma_start(y_out[j], y_all[:, j, NC_ * S - T:]).then_inc(stored, 16)
            sp.wait_ge(stored, 16 * PAIRS)

        @block.tensor
        def _(pe):
            T_ = nc.tensor
            R = lambda v, r, j: roles[:, v, r, j].rearrange("p h c -> p (h c)")

            def grams_of(c, v, loaded):
                pe.wait_ge(roles_loaded[v], loaded)
                plan = [(ROLE_B, ROLE_A), (ROLE_K, ROLE_A), (ROLE_B, ROLE_R), (ROLE_K, ROLE_R)]
                for n, (s, t) in enumerate(plan):
                    for j in range(PAIRS):
                        mm = T_.matmul(bank(n)[:, j, :], R(v, s, j), R(v, t, j), start=True, stop=True)
                    mm.then_inc(grams_done, 1)

            def turn_toks(c, v):
                for n, r in enumerate((ROLE_B, ROLE_K, ROLE_V)):
                    at(pe, masked, 5, c, n + 3)
                    for j in range(PAIRS):
                        mm = T_.transpose(bank(n + 1)[:, j, :], R(v, r, j), ident)
                    mm.then_inc(toks_done, 1)

            def turn_x1(c, v):
                at(pe, masked, 5, c, 2)
                for j in range(PAIRS):
                    mm = T_.transpose(bank(0)[:, j, :], x_t[:, v, j, :], ident)
                mm.then_inc(x1_turned, 1)

            def lx(c, v, l):
                for h in range(2):
                    if l == 0:
                        pe.wait_ge(x1_ready, c + 1)
                        at(pe, toks_ready, 3, c, 1)
                    else:
                        at(pe, x_ready, 10, c, 2 * (l - 1) + h + 1)
                        at(pe, xt_ready, 8, c, 2 * (l - 1) + h + 1)
                    for n, j in enumerate((0, 1)):
                        mm = T_.matmul(half_bank(h)[:, n, :], l_t[:, 2 * h + j, :], x[:, 2 * h + j, :], start=True, stop=True)
                    mm.then_inc(lx_done, 1)

            def xq(c, v, l):
                for h in range(2):
                    at(pe, q_ready, 10, c, 2 * l + h + 1)
                    if l == 0:
                        at(pe, toks_ready, 3, c, 3)
                    else:
                        at(pe, x_ready, 10, c, 2 * (l - 1) + h + 1)
                    for n, j in enumerate((0, 1)):
                        p = 2 * h + j
                        if l < LEVELS - 1:
                            mm = T_.matmul(half_bank(2 + h)[:, n, :], x_t[:, v, p, :], q[:, p, :], start=True, stop=True)
                        else:
                            mm = T_.matmul(half_bank(2 + h)[:, n, :], q[:, p, :], x_t[:, v, p, :], start=True, stop=True)
                    mm.then_inc(xq_done, 1)

            def turn_x(c, v, l):
                for h in range(2):
                    at(pe, x_ready, 10, c, 2 * l + h + 1)
                    for n, j in enumerate((0, 1)):
                        mm = T_.transpose(half_bank(h)[:, n, :], x[:, 2 * h + j, :], ident)
                    mm.then_inc(xt_turned, 1)

            def main_w(c, v):
                at(pe, toks_ready, 3, c, 3)
                at(pe, masked, 5, c, 5)
                pe.wait_ge(m_ready, c + 1)
                pe.wait_ge(y_flat, 2 * c)
                for j in range(PAIRS):
                    T_.matmul(bank(4)[:, j, :], grams[:, v, 0, j, :], toks[:, v, 2, j, :], start=True, stop=False)
                    mm = T_.matmul(bank(4)[:, j, :], R(v, ROLE_A, j), m[:, v, j, :], start=False, stop=True)
                mm.then_inc(w_done, 1)

            def main_u(c, v):
                at(pe, x_ready, 10, c, 10)
                pe.wait_ge(w_ready, c + 1)
                for j in range(PAIRS):
                    mm = T_.matmul(bank(5)[:, j, :], x_t[:, v, j, :], w[:, j, :], start=True, stop=True)
                mm.then_inc(u_done, 1)

            def main_m(c, v):
                pe.wait_ge(u_ready, c + 1)
                for j in range(PAIRS):
                    T_.matmul(bank(6)[:, j, :], toks[:, v, 1, j, :], toks[:, v, 2, j, :], start=True, stop=False)
                    mm = T_.matmul(bank(6)[:, j, :], toks[:, v, 0, j, :], u[:, j, :], start=False, stop=True)
                mm.then_inc(m_done, 1)

            def main_y(c, v):
                pe.wait_ge(y_ready, 2 * c)
                for j in range(PAIRS):
                    T_.matmul(bank(7)[:, j, :], R(v, ROLE_R, j), m[:, v, j, :], start=True, stop=False)
                    T_.matmul(bank(7)[:, j, :], grams[:, v, 2, j, :], toks[:, v, 2, j, :], start=False, stop=False)
                    mm = T_.matmul(bank(7)[:, j, :], grams[:, v, 1, j, :], u[:, j, :], start=False, stop=True)
                mm.then_inc(y_done, 1)

            def turn_y(c):
                pe.wait_ge(normed, 2 * c + 2)
                pe.wait_ge(w_ready, c + 1)
                for j in range(PAIRS):
                    mm = T_.transpose(bank(4)[:, j, :], y_bd[:, j].rearrange("p h c -> p (h c)"), ident)
                mm.then_inc(y_turned, 1)

            def pre_and_main(c, v, loaded, pre=True, main=True):
                n, o = (c + 1, 1 - v) if main else (c, v)
                if main:
                    main_w(c, v)
                if pre:
                    if main:
                        at(pe, x_ready, 10, c, 10)
                    grams_of(n, o, loaded)
                if main:
                    main_u(c, v)
                if pre:
                    turn_x1(n, o)
                if main:
                    main_m(c, v)
                if pre:
                    turn_toks(n, o)
                if main:
                    main_y(c, v)
                for l in range(LEVELS if pre else 0):
                    lx(n, o, l)
                    xq(n, o, l)
                    if l < LEVELS - 1:
                        turn_x(n, o, l)
                    if l == 1 and main:
                        turn_y(c)
                if main and not pre:
                    turn_y(c)

            pe.wait_ge(masks_loaded, 16)
            pre_and_main(0, 0, 160, main=False)
            with pe.Fori(0, (NC_ - 1) // 2) as i:
                pre_and_main(2 * i, 0, 160 * i + 160)
                pre_and_main(2 * i + 1, 1, 160 * i + 320)
            pre_and_main(NC_ - 1, 0, 0, pre=False)

        @block.vector
        def _(dve):
            V = nc.vector
            dve.sem_inc(roles_free, 2)
            V.memset(m[:], 0.0).then_inc(m_ready, 1)
            V.memset(y_bd[:], 0.0).then_inc(eps_set, 1)
            V.memset(eps[:], GN_EPS).then_inc(eps_set, 1)
            V.memset(roles[:].rearrange("p a b c d e -> p (a b c d e)"), 0.0).then_inc(cleared, 1)
            dve.wait_ge(masks_loaded, 16)
            dve.wait_ge(eps_set, 2)

            def mask_grams(c, v):
                at(dve, grams_done, 4, c, 1)
                V.tensor_tensor(l_t[:], bank(0), wide(0, PAIRS), ALU.mult).then_inc(masked, 1)
                at(dve, masked, 5, c, 1)
                V.tensor_tensor(q[:], l_t[:], wide(2, PAIRS), ALU.mult).then_inc(q_init, 1)
                dve.wait_ge(q_init, c + 1)
                V.tensor_tensor(x_t[:, v], q[:], ident.unsqueeze(1).broadcast_to([P, PAIRS, P]), ALU.add).then_inc(masked, 1)
                for n, mk in enumerate((0, 1, 1)):
                    at(dve, grams_done, 4, c, n + 2)
                    V.tensor_tensor(grams[:, v, n], bank(n + 1), wide(mk, PAIRS), ALU.mult).then_inc(masked, 1)

            def level(c, v, l):
                for h, js in enumerate(HALVES):
                    at(dve, lx_done, 10, c, 2 * l + h + 1)
                    V.tensor_tensor(q[:, js, :], half_bank(h), wide(3 + l, 2), ALU.mult).then_inc(q_ready, 1)
                for h, js in enumerate(HALVES):
                    at(dve, xq_done, 10, c, 2 * l + h + 1)
                    if l < LEVELS - 1:
                        V.tensor_tensor(x[:, js, :], x[:, js, :], half_bank(2 + h), ALU.add).then_inc(x_ready, 1)
                    else:
                        V.tensor_tensor(x_t[:, v, js, :], x_t[:, v, js, :], half_bank(2 + h), ALU.add).then_inc(x_ready, 1)

            def state(c, v):
                dve.wait_ge(m_done, c + 1)
                dve.wait_ge(y_done, c)
                V.tensor_tensor(m[:, 1 - v], m[:, v], bank(6), ALU.add).then_inc(m_half, 1)
                dve.wait_ge(m_half, c + 1)
                V.tensor_tensor(m[:, 1 - v], m[:, 1 - v], chunk_decay[:, :, bass.ds(c, 1)].broadcast_to([P, PAIRS, P]), ALU.mult).then_inc(m_ready, 1)

            def norm(c):
                own = 5
                dve.wait_ge(y_ready, 2 * c + 2)
                wide_stat = lambda n: stat[:, n, :].unsqueeze(2).broadcast_to([P, PAIRS, HEAD_DIM])
                V.tensor_reduce(stat[:, 0, :], y[:], mybir.AxisListType.X, ALU.add).then_inc(norm_own, 1)
                at(dve, norm_own, own, c, 1)
                V.tensor_scalar(stat[:, 0, :], stat[:, 0, :], 1.0 / HEAD_DIM, None, ALU.mult).then_inc(norm_own, 1)
                at(dve, norm_own, own, c, 2)
                V.tensor_tensor(y[:], y[:], wide_stat(0), ALU.subtract).then_inc(norm_own, 1)
                at(dve, norm_own, own, c, 3)
                dve.wait_ge(sq_ready, c + 1)
                V.tensor_reduce(stat[:, 1, :], y_sq[:], mybir.AxisListType.X, ALU.add).then_inc(norm_own, 1)
                dve.wait_ge(std_done, c + 1)
                V.reciprocal(stat[:, 3, :], stat[:, 2, :]).then_inc(norm_own, 1)
                at(dve, norm_own, own, c, 5)
                dve.wait_ge(y_turned, c)
                for h in range(2):
                    rows = slice(h * 64, (h + 1) * 64)
                    V.tensor_tensor(y_bd[rows, :, h, :], y[rows], wide_stat(3)[rows], ALU.mult).then_inc(normed, 1)

            def step(c, v, pre=True, main=True):
                n, o = (c + 1, 1 - v) if main else (c, v)
                if pre:
                    mask_grams(n, o)
                if main:
                    state(c, v)
                if pre:
                    level(n, o, 0)
                if main:
                    norm(c)
                    dve.wait_ge(y_done, c + 1)
                    dve.sem_inc(roles_free, 1)
                for l in range(1, LEVELS if pre else 1):
                    level(n, o, l)
            step(0, 0, main=False)
            with dve.Fori(0, (NC_ - 1) // 2) as i:
                step(2 * i, 0)
                step(2 * i + 1, 1)
            step(NC_ - 1, 0, pre=False)
            dve.wait_ge(y_flat, 2 * NC_)
            for j in range(PAIRS):
                out = y_all[:, j, NC_ * S - T:]
                V.tensor_scalar(out, out, cols[:, COL["ln_g"] + j:COL["ln_g"] + j + 1], cols[:, COL["ln_b"] + j:COL["ln_b"] + j + 1], ALU.mult, ALU.add).then_inc(post_own, 1)
                dve.wait_ge(post_own, 3 * j + 1)
                dve.wait_ge(post_loaded[0], 16 * j + 16)
                V.tensor_tensor(out, out, post[:, 0, :], ALU.add).then_inc(post_own, 1)
                dve.wait_ge(post_own, 3 * j + 2)
                dve.wait_ge(post_loaded[1], 16 * j + 16)
                V.tensor_tensor(out, out, post[:, 1, :], ALU.mult).then_inc(post_own, 1)

        @block.scalar
        def _(act):
            A = nc.scalar
            act.wait_ge(eps_set, 2)

            def toks_out(c, v):
                act.wait_ge(x1_turned, c + 1)
                A.activation(x[:], bank(0), ACT.Copy).then_inc(x1_ready, 1)
                for n in range(3):
                    at(act, toks_done, 3, c, n + 1)
                    A.activation(toks[:, v, n], bank(n + 1), ACT.Copy).then_inc(toks_ready, 1)

            def level(c, v, l):
                for h, js in enumerate(HALVES):
                    at(act, xt_turned, 8, c, 2 * l + h + 1)
                    A.activation(x_t[:, v, js, :], half_bank(h), ACT.Copy).then_inc(xt_ready, 1)

            def w_out(c):
                act.wait_ge(w_done, c + 1)
                A.activation(w[:], bank(4), ACT.Copy).then_inc(w_ready, 1)

            def u_out(c):
                act.wait_ge(u_done, c + 1)
                act.wait_ge(y_done, c)
                A.activation(u[:], bank(5), ACT.Copy).then_inc(u_ready, 1)

            def y_out_of(c):
                act.wait_ge(y_done, c + 1)
                act.wait_ge(normed, 2 * c)
                for h in range(2):
                    rows = slice(h * 64, (h + 1) * 64)
                    A.activation(y[rows], bank(7)[rows, :, h * 64:(h + 1) * 64], ACT.Copy).then_inc(y_ready, 1)

            def squares(c):
                at(act, norm_own, 5, c, 3)
                A.activation(y_sq[:], y[:], ACT.Square).then_inc(sq_ready, 1)
                at(act, norm_own, 5, c, 4)
                A.activation(stat[:, 2, :], stat[:, 1, :], ACT.Sqrt, scale=1.0 / HEAD_DIM, bias=eps[:]).then_inc(std_done, 1)

            def y_flat_out(c):
                act.wait_ge(y_turned, c + 1)
                for h in range(2):
                    rows = slice(h * 64, (h + 1) * 64)
                    A.activation(y_all[rows, :, bass.ds(c * S, S)], bank(4)[rows, :, h * 64:(h + 1) * 64], ACT.Copy).then_inc(y_flat, 1)

            def step(c, v, pre=True, main=True):
                n, o = (c + 1, 1 - v) if main else (c, v)
                if main:
                    w_out(c)
                    u_out(c)
                if pre:
                    toks_out(n, o)
                if main:
                    y_out_of(c)
                    squares(c)
                if pre:
                    level(n, o, 0)
                    level(n, o, 1)
                if main:
                    y_flat_out(c)
                if pre:
                    level(n, o, 2)
                    level(n, o, 3)
            step(0, 0, main=False)
            with act.Fori(0, (NC_ - 1) // 2) as i:
                step(2 * i, 0)
                step(2 * i + 1, 1)
            step(NC_ - 1, 0, pre=False)


def branch_mix(nc, name, sems, psum, ya_dram, yb_dram, w_tiles, gates, mix_out):
    act_loaded, act_split_hi, act_split_lo, weight_loaded, split_hi, split_lo, products_done, sig_ready, mul_done, \
        za_used, mixed_ready, gates_loaded, stored = sems(name, [
            ("act_loaded", 2), "act_split_hi", "act_split_lo", "weight_loaded", "split_hi", "split_lo", "products_done",
            "sig_ready", "mul_done", "za_used", "mixed_ready", "gates_loaded", ("stored", 2)])
    with ExitStack() as ctx:
        sb = lambda n, shape, dt: ctx.enter_context(nc.sbuf_tensor(f"{name}_{n}", shape, dt))
        y_hi = sb("y_hi", [P, 2, K4, T], F32R)
        y_lo = sb("y_lo", [P, 2, K4, T], F32R)
        weight = sb("weight", [P, 3, K4, P], F32)
        w_hi = sb("w_hi", [P, SLOTS, 3, K4, P], F32R)
        w_lo = sb("w_lo", [P, SLOTS, 3, K4, P], F32R)
        sig = sb("sig", [P, SLOTS, N_TOK], F32)
        term = sb("term", [P, SLOTS, N_TOK], F32)
        gate = sb("gate", [P, 2, T], F32)
        mixed = sb("mixed", [P, SLOTS, T], F32)
        block = ctx.enter_context(nc.Block())
        LAST = KD // 2 - 1
        HALF = 2 * K4

        def tile_loop(eng, body):
            with eng.Fori(0, LAST) as i:
                for u in range(SLOTS):
                    body(2 * i + u, i, u)
            for u in range(SLOTS):
                body(2 * LAST + u, LAST, u)

        def bank(n, j):
            return (3 * n + j) % 6

        @block.sync
        def _(sp):
            for h in range(HALF):
                if h >= SLOTS:
                    sp.wait_ge(act_split_lo, h - SLOTS + 1)
                src = (ya_dram, yb_dram)[h // K4][h % K4]
                sp.dma_start(mixed[:, h % 2, :], src).then_inc(act_loaded[h % 2], 16)
                if h == 0:
                    sp.dma_start(weight[:], w_tiles[0:1].rearrange("o p a k c -> p (o a k) c")).then_inc(weight_loaded, 16)

            def load_gates(m):
                sp.wait_ge(mixed_ready, (m + 1) * N_BLOCKS)
                sp.dma_start(gate[:, 0, :], gates[bass.ds(m, 1)].rearrange("o p t -> p (o t)")).then_inc(gates_loaded, 16)
                sp.dma_start(gate[:, 1, :], gates[bass.ds(m + KD, 1)].rearrange("o p t -> p (o t)")).then_inc(gates_loaded, 16)

            def load_weights(m):
                sp.wait_ge(split_lo, m)
                sp.dma_start(weight[:], w_tiles[bass.ds(m, 1)].rearrange("o p a k c -> p (o a k) c")).then_inc(weight_loaded, 16)

            def store(m, u):
                sp.wait_ge(mixed_ready, m * N_BLOCKS + 2 * N_BLOCKS)
                sp.dma_start(mix_out[bass.ds(m, 1)].rearrange("o p t -> p (o t)"), mixed[:, u, :]).then_inc(stored[u], 16)
            load_gates(0)
            load_weights(1)
            with sp.Fori(0, KD // 2 - 1) as i:
                for u in range(SLOTS):
                    m = 2 * i + u
                    load_gates(m + 1)
                    load_weights(m + 2)
                    store(m, u)
            load_gates(KD - 1)
            for u in range(SLOTS):
                store(KD - 2 + u, u)
            for u in range(SLOTS):
                sp.wait_ge(stored[u], 16 * KD // 2)

        @block.tensor
        def _(pe):
            pe.sem_inc(products_done, SLOTS * 3 * N_BLOCKS)
            pe.wait_ge(act_split_lo, HALF)

            def tile(m, i, u):
                pe.wait_ge(split_hi, m + 1)
                pe.wait_ge(split_lo, m + 1)
                for n in range(N_BLOCKS):
                    for j in range(3):
                        part = 2 - j
                        b = bank(n, j)
                        if j == 0:
                            pe.wait_ge(sig_ready, m * N_BLOCKS + n + 1)
                        elif j == 1:
                            pe.wait_ge(za_used, m * N_BLOCKS + n + 1)
                        else:
                            pe.wait_ge(mul_done, 2 * (m * N_BLOCKS + n + 1))
                        for k in range(K4):
                            src = 0 if part == 0 else 1
                            cols = slice(n * N_TOK, (n + 1) * N_TOK)
                            for w, y in ((w_hi, y_hi), (w_hi, y_lo), (w_lo, y_hi)):
                                mm = nc.tensor.matmul(psum[:, b, 0:N_TOK], w[:, u, part, k, :], y[:, src, k, cols],
                                                      start=(k == 0 and w is w_hi and y is y_hi), stop=(k == K4 - 1 and w is w_lo))
                        mm.then_inc(products_done, 1)
            tile_loop(pe, tile)

        @block.scalar
        def _(act):
            for h in range(HALF):
                act.wait_ge(act_loaded[h % 2], 16 * (h // 2 + 1))
                nc.scalar.activation(y_hi[:, h // K4, h % K4, :], mixed[:, h % 2, :], ACT.Copy).then_inc(act_split_hi, 1)
            act.sem_inc(sig_ready, SLOTS)

            def split(m, u):
                if isinstance(m, int) and m >= KD:
                    return
                act.wait_ge(weight_loaded, 16 * m + 16)
                act.wait_ge(products_done, (m + 1) * 3 * N_BLOCKS)
                nc.scalar.activation(w_hi[:, u], weight[:], ACT.Copy).then_inc(split_hi, 1)
            split(0, 0)

            def tile(m, i, u):
                split(m + 1, 1 - u)
                for n in range(N_BLOCKS):
                    act.wait_ge(products_done, ((m + SLOTS) * N_BLOCKS + n) * 3 + 1)
                    act.wait_ge(za_used, m * N_BLOCKS + n + 1)
                    nc.scalar.activation(sig[:, n % 2, :], psum[:, bank(n, 0), 0:N_TOK], ACT.Sigmoid).then_inc(sig_ready, 1)
            tile_loop(act, tile)

        @block.vector
        def _(dve):
            for h in range(HALF):
                dve.wait_ge(act_split_hi, h + 1)
                nc.vector.tensor_tensor(y_lo[:, h // K4, h % K4, :], mixed[:, h % 2, :],
                                        y_hi[:, h // K4, h % K4, :].bitcast(F32), ALU.subtract).then_inc(act_split_lo, 1)
            dve.sem_inc(za_used, SLOTS)
            dve.sem_inc(mul_done, 2 * SLOTS)
            dve.sem_inc(mixed_ready, N_BLOCKS)

            def split(m, u):
                if isinstance(m, int) and m >= KD:
                    return
                dve.wait_ge(split_hi, m + 1)
                nc.vector.tensor_tensor(w_lo[:, u], weight[:], w_hi[:, u].bitcast(F32), ALU.subtract).then_inc(split_lo, 1)
            split(0, 0)

            def tile(m, i, u):
                split(m + 1, 1 - u)
                dve.wait_ge(gates_loaded, 32 * m + 32)
                dve.wait_ge(stored[u], 16 * i)
                for n in range(N_BLOCKS):
                    cols = slice(n * N_TOK, (n + 1) * N_TOK)
                    q = m * N_BLOCKS + n
                    dve.wait_ge(products_done, ((m + SLOTS) * N_BLOCKS + n) * 3 + 2)
                    dve.wait_ge(sig_ready, q + 1 + SLOTS)
                    nc.vector.tensor_tensor(term[:, n % 2, :], psum[:, bank(n, 1), 0:N_TOK], sig[:, n % 2, :], ALU.mult).then_inc(za_used, 1)
                    dve.wait_ge(za_used, q + 1 + SLOTS)
                    nc.vector.tensor_tensor(term[:, n % 2, :], term[:, n % 2, :], gate[:, 1, cols], ALU.mult).then_inc(mul_done, 1)
                    dve.wait_ge(products_done, ((m + SLOTS) * N_BLOCKS + n) * 3 + 3)
                    nc.vector.tensor_tensor(mixed[:, u, cols], psum[:, bank(n, 2), 0:N_TOK], gate[:, 0, cols], ALU.mult).then_inc(mul_done, 1)
                    dve.wait_ge(mul_done, 2 * (q + 1 + SLOTS))
                    nc.vector.tensor_tensor(mixed[:, u, cols], mixed[:, u, cols], term[:, n % 2, :], ALU.add).then_inc(mixed_ready, 1)
            tile_loop(dve, tile)


def token_projection(nc, name, sems, psum, acts, first_col, w_dram, k_tiles, passes, gain, residual, out, out_first, meta_tile):
    TILES = SEQ // P
    LAST = TILES // 2 - 1
    HALF = D_MODEL // 2
    assert passes <= 2 and not (meta_tile and passes > 1)
    weight_loaded, w_hi_done, w_lo_done, k_done, acts_loaded, acts_hi, acts_lo, evacuated, rows_loaded, summed, \
        squares_done, std_ready, rstd_ready, scaled, finished, stored, gain_loaded, eps_ready = sems(name, [
            ("weight_loaded", 2), "w_hi_done", "w_lo_done", "k_done", "acts_loaded", "acts_hi", "acts_lo",
            "evacuated", ("rows_loaded", 2), "summed", "squares_done", "std_ready", "rstd_ready", "scaled", "finished",
            ("stored", 2), "gain_loaded", "eps_ready"])
    with ExitStack() as ctx:
        sb = lambda n, shape, dt: ctx.enter_context(nc.sbuf_tensor(f"{name}_{n}", shape, dt))
        w_hi = sb("w_hi", [P, k_tiles, D_MODEL], F32R)
        w_lo = sb("w_lo", [P, k_tiles, D_MODEL], F32R)
        w_raw = sb("w_raw", [P, 2, HALF], F32)
        a_raw = sb("a_raw", [P, k_tiles, P], F32)
        a_hi = sb("a_hi", [P, SLOTS, k_tiles, P], F32R)
        a_lo = sb("a_lo", [P, SLOTS, k_tiles, P], F32R)
        rows = sb("rows", [P, SLOTS, D_MODEL], F32)
        squares = sb("squares", [P, D_MODEL], BF16)
        stat = sb("stat", [P, SLOTS, 3], F32)
        eps = sb("eps", [P, 1], F32)
        gains = sb("gains", [P, D_MODEL], F32)
        sums = sb("sums", [P, TILES if passes > 1 else SLOTS, D_MODEL], F32)
        block = ctx.enter_context(nc.Block())

        def tiles(eng, ahead, body, part):
            def args(i, u):
                r = 2 * i + u
                if isinstance(r, int) and r >= TILES:
                    return (part * TILES + TILES, TILES, 0, TILES // 2, N_META, -N_META) if meta_tile and r == TILES else None
                return (r + part * TILES, r, u, i, P, r * P)

            def step(i, u):
                after = args(i + u, 1 - u)
                if ahead and after:
                    ahead(*after)
                if body:
                    body(*args(i, u))
            if ahead:
                ahead(*args(0, 0))
            with eng.Fori(0, LAST) as i:
                step(i, 0)
                step(i, 1)
            step(LAST, 0)
            step(LAST, 1)
            if meta_tile and body:
                body(*args(LAST + 1, 0))

        def flat(ap):
            return ap.rearrange("p a b -> p (a b)")

        @block.sync
        def _(sp):
            sp.dma_start(gains[:], gain).then_inc(gain_loaded, 16)

            def load_acts(part, r, n, token):
                sp.wait_ge(acts_lo, r + (part * TILES + 1))
                src = acts[part * k_tiles:(part + 1) * k_tiles, :, bass.ds(token + first_col, n)]
                sp.dma_start(a_raw[:, :, 0:n], src.rearrange("k p t -> p k t")).then_inc(acts_loaded, 16)

            def load_rows(r, u, n, token):
                sp.wait_ge(finished, r + 1)
                sp.dma_start(rows[0:n, u, :], residual[bass.ds(token + N_META, n), :]).then_inc(rows_loaded[u], 16)

            def store(r, u, n, token):
                sp.wait_ge(finished, r + (1 + SLOTS))
                total = flat(sums[:, bass.ds(r, 1), :]) if passes > 1 else sums[0:n, u, :]
                sp.dma_start(out[bass.ds(token + out_first, n), :], total).then_inc(stored[u], 16)

            for part in range(passes):
                with sp.Fori(0, k_tiles) as k:
                    for h in range(2):
                        sp.wait_ge(w_lo_done, 2 * k + (h + 1 + part * 2 * k_tiles))
                        sp.dma_start(w_raw[:, h, :], flat(w_dram[bass.ds(k + part * k_tiles, 1), :, h * HALF:(h + 1) * HALF].rearrange("o p n -> p o n"))).then_inc(weight_loaded[h], 16)
                if part < passes - 1:
                    with sp.Fori(0, TILES) as r:
                        load_acts(part, r, P, r * P)
            for u in range(SLOTS):
                load_acts(part, u, P, u * P)
                load_rows(u, u, P, u * P)
            with sp.Fori(1, TILES // 2) as i:
                for u in range(SLOTS):
                    r = 2 * i + u
                    load_acts(part, r, P, r * P)
                    load_rows(r, u, P, r * P)
                    store(r - 2, u, P, (r - 2) * P)
            if meta_tile:
                load_acts(part, TILES, N_META, -N_META)
                load_rows(TILES, 0, N_META, -N_META)
            for u in range(SLOTS):
                store(TILES - 2 + u, u, P, (TILES - 2 + u) * P)
            if meta_tile:
                store(TILES, 0, N_META, -N_META)
            for u in range(SLOTS):
                sp.wait_ge(stored[u], 16 * (TILES // 2 + (meta_tile and u == 0)))

        @block.tensor
        def _(pe):
            for part in range(passes):
                def products(s, r, u, i, n, token):
                    pe.wait_ge(acts_hi, s + 1)
                    pe.wait_ge(acts_lo, s + 2)
                    pe.wait_ge(evacuated, s + 1)
                    for k in range(k_tiles):
                        pe.wait_ge(w_lo_done, 2 * (part * k_tiles + k + 1) + 2)
                        for h in range(2):
                            for a, w in ((a_hi, w_hi), (a_hi, w_lo), (a_lo, w_hi)):
                                mm = nc.tensor.matmul(psum[0:n, 2 * u + h, :], a[:, u, k, 0:n], w[:, k, h * HALF:(h + 1) * HALF],
                                                      start=(k == 0 and a is a_hi and w is w_hi), stop=(k == k_tiles - 1 and a is a_lo))
                        mm.then_inc(k_done, 1)
                tiles(pe, None, products, part)

        @block.scalar
        def _(act):
            act.wait_ge(eps_ready, 1)
            for part in range(passes):
                def split(s, r, u, i, n, token):
                    act.wait_ge(acts_loaded, 16 * s + 16)
                    if part or not (isinstance(i, int) and i == 0):
                        act.wait_ge(k_done, (s - 1) * k_tiles if not isinstance(s, int) or s > 1 else 0)
                    nc.scalar.activation(a_hi[:, u, :, 0:n], a_raw[:, :, 0:n], ACT.Copy).then_inc(acts_hi, 1)

                def finish(s, r, u, i, n, token):
                    banks = flat(psum[0:n, 2 * u:2 * u + 2, :])
                    if part < passes - 1:
                        act.wait_ge(k_done, (s + 1) * k_tiles)
                        nc.scalar.activation(flat(sums[:, bass.ds(r, 1), :]), banks, ACT.Copy).then_inc(evacuated, 1)
                        return
                    if passes > 1:
                        act.wait_ge(summed, r + 1)
                        total = flat(sums[:, bass.ds(r, 1), :])
                    else:
                        act.wait_ge(k_done, (s + 1) * k_tiles)
                        total = banks
                    act.wait_ge(scaled, r + 1)
                    act.wait_ge(squares_done, r)
                    nc.scalar.activation(squares[0:n, :], total, ACT.Square, accum_out=stat[0:n, u, 0:1]).then_inc(squares_done, 1)
                    act.wait_ge(squares_done, r + 1)
                    nc.scalar.activation(stat[0:n, u, 1:2], stat[0:n, u, 0:1], ACT.Sqrt, scale=1.0 / D_MODEL, bias=eps[0:n]).then_inc(std_ready, 1)

                with act.Fori(0, k_tiles) as k:
                    for h in range(2):
                        act.wait_ge(weight_loaded[h], 16 * k + (16 + 16 * part * k_tiles))
                        if part:
                            act.wait_ge(k_done, k + ((TILES - 1) * k_tiles + 1))
                        nc.scalar.activation(flat(w_hi[:, bass.ds(k, 1), h * HALF:(h + 1) * HALF]), w_raw[:, h, :], ACT.Copy).then_inc(w_hi_done, 1)
                tiles(act, split, finish, part)

        @block.vector
        def _(dve):
            nc.vector.memset(eps[:], RMS_EPS).then_inc(eps_ready, 1)
            dve.sem_inc(w_lo_done, 2)
            dve.sem_inc(acts_lo, 1)
            dve.sem_inc(evacuated, SLOTS)
            dve.sem_inc(scaled, SLOTS)
            dve.sem_inc(finished, SLOTS)
            dve.wait_ge(gain_loaded, 16)
            for part in range(passes):
                def split(s, r, u, i, n, token):
                    dve.wait_ge(acts_hi, s + 1)
                    nc.vector.tensor_tensor(a_lo[:, u, :, 0:n], a_raw[:, :, 0:n], a_hi[:, u, :, 0:n].bitcast(F32), ALU.subtract).then_inc(acts_lo, 1)

                def finish(s, r, u, i, n, token):
                    banks = flat(psum[0:n, 2 * u:2 * u + 2, :])
                    if passes > 1:
                        total = source = flat(sums[:, bass.ds(r, 1), :])
                        dve.wait_ge(k_done, (s + 1) * k_tiles)
                        nc.vector.tensor_tensor(total, total, banks, ALU.add).then_inc(summed, 1)
                        dve.wait_ge(summed, r + 1)
                        dve.sem_inc(evacuated, 1)
                    else:
                        total, source = sums[0:n, u, :], banks
                        dve.wait_ge(stored[u], 16 * i)
                    dve.wait_ge(std_ready, r + 1)
                    nc.vector.reciprocal(stat[0:n, u, 2:3], stat[0:n, u, 1:2]).then_inc(rstd_ready, 1)
                    dve.wait_ge(rstd_ready, r + 1)
                    nc.vector.scalar_tensor_tensor(total, source, stat[0:n, u, 2:3], gains[0:n, :], ALU.mult, ALU.mult).then_inc(scaled, 1)
                    dve.wait_ge(scaled, r + (1 + SLOTS))
                    if passes == 1:
                        dve.sem_inc(evacuated, 1)
                    dve.wait_ge(rows_loaded[u], 16 * i + 16)
                    nc.vector.tensor_tensor(total, total, rows[0:n, u, :], ALU.add).then_inc(finished, 1)

                with dve.Fori(0, k_tiles) as k:
                    for h in range(2):
                        dve.wait_ge(w_hi_done, 2 * k + (h + 1 + part * 2 * k_tiles))
                        nc.vector.tensor_tensor(flat(w_lo[:, bass.ds(k, 1), h * HALF:(h + 1) * HALF]), w_raw[:, h, :],
                                                flat(w_hi[:, bass.ds(k, 1), h * HALF:(h + 1) * HALF].bitcast(F32)), ALU.subtract).then_inc(w_lo_done, 1)
                tiles(dve, split, finish if part == passes - 1 else None, part)


def ffn_up(nc, name, sems, psum, x_hi, x_lo, w_tiles, conv_w, conv_b, hidden_out):
    weight_loaded, split_hi, split_lo, products_done, a_evacuated, conv_done, gelu_done, b_used, tap_done, stored = sems(name, [
        "weight_loaded", "split_hi", "split_lo", "products_done", "a_evacuated", "conv_done", "gelu_done", "b_used", "tap_done", ("stored", 2)])
    with ExitStack() as ctx:
        sb = lambda n, shape, dt: ctx.enter_context(nc.sbuf_tensor(f"{name}_{n}", shape, dt))
        weight = sb("weight", [P, 2, KD, P], F32)
        w_hi = sb("w_hi", [P, SLOTS, 2, KD, P], F32R)
        w_lo = sb("w_lo", [P, SLOTS, 2, KD, P], F32R)
        a_pre = sb("a_pre", [P, T], F32)
        hidden = sb("hidden", [P, SLOTS, SEQ], F32)
        block = ctx.enter_context(nc.Block())
        GROUPS = 2 * N_BLOCKS
        LAST = M_FF // 2 - 1

        def tile_loop(eng, body):
            with eng.Fori(0, LAST) as i:
                for u in range(SLOTS):
                    body(2 * i + u, i, u)
            for u in range(SLOTS):
                body(2 * LAST + u, LAST, u)

        def bank(u, part, n):
            return (u * GROUPS + part * N_BLOCKS + n) % 8

        @block.sync
        def _(sp):
            def load(m):
                sp.wait_ge(split_lo, m + 1)
                sp.dma_start(weight[:], w_tiles[bass.ds(m, 1)].rearrange("o p a k c -> p (o a k) c")).then_inc(weight_loaded, 16)

            def store(m, u):
                sp.wait_ge(b_used, m * N_BLOCKS + 2 * N_BLOCKS)
                sp.dma_start(hidden_out[bass.ds(m, 1)].rearrange("o p t -> p (o t)"), hidden[:, u, :]).then_inc(stored[u], 16)
            for u in range(SLOTS):
                load(u)
            with sp.Fori(1, M_FF // 2) as i:
                for u in range(SLOTS):
                    load(2 * i + u)
                    store(2 * i - 2 + u, u)
            for u in range(SLOTS):
                store(2 * LAST + u, u)
            for u in range(SLOTS):
                sp.wait_ge(stored[u], 16 * M_FF // 2)

        @block.tensor
        def _(pe):
            pe.sem_inc(products_done, SLOTS * GROUPS)

            def tile(m, i, u):
                pe.wait_ge(split_hi, m + 1)
                pe.wait_ge(split_lo, m + 2)
                for part in range(2):
                    for n in range(N_BLOCKS):
                        before = part * N_BLOCKS + n - 8
                        if before >= N_BLOCKS:
                            pe.wait_ge(b_used, m * N_BLOCKS + before - N_BLOCKS + 1 + N_BLOCKS)
                        elif before >= 0:
                            pe.wait_ge(a_evacuated, m * N_BLOCKS + before + 1 + N_BLOCKS)
                        elif before + GROUPS >= N_BLOCKS:
                            pe.wait_ge(b_used, m * N_BLOCKS + before + N_BLOCKS + 1)
                        else:
                            pe.wait_ge(a_evacuated, m * N_BLOCKS + before + GROUPS + 1)
                        for k in range(KD):
                            for w, x in ((w_hi, x_hi), (w_hi, x_lo), (w_lo, x_hi)):
                                mm = nc.tensor.matmul(psum[:, bank(u, part, n), 0:N_TOK], w[:, u, part, k, :],
                                                      x[:, k, n * N_TOK:(n + 1) * N_TOK],
                                                      start=(k == 0 and w is w_hi and x is x_hi), stop=(k == KD - 1 and w is w_lo))
                        mm.then_inc(products_done, 1)
            tile_loop(pe, tile)

        @block.scalar
        def _(act):
            act.sem_inc(a_evacuated, N_BLOCKS)

            def split(m, i, u):
                if isinstance(i, int) and i > LAST:
                    return
                act.wait_ge(weight_loaded, 16 * m + 16)
                act.wait_ge(products_done, (m + 1) * GROUPS)
                nc.scalar.activation(w_hi[:, u], weight[:], ACT.Copy).then_inc(split_hi, 1)
            split(0, 0, 0)

            def tile(m, i, u):
                split(m + 1, i + u, 1 - u)
                act.wait_ge(conv_done, m + 1)
                for n in range(N_BLOCKS):
                    act.wait_ge(products_done, (m + SLOTS) * GROUPS + n + 1)
                    nc.scalar.activation(a_pre[:, n * N_TOK:(n + 1) * N_TOK], psum[:, bank(u, 0, n), 0:N_TOK], ACT.Copy).then_inc(a_evacuated, 1)
                act.wait_ge(conv_done, m + 2)
                nc.scalar.activation(hidden[:, u, :], hidden[:, u, :], ACT.Gelu_apprx_tanh).then_inc(gelu_done, 1)
            tile_loop(act, tile)

        @block.vector
        def _(dve):
            dve.sem_inc(split_lo, 1)
            dve.sem_inc(conv_done, 1)
            dve.sem_inc(b_used, N_BLOCKS)

            def split(m, i, u):
                if isinstance(i, int) and i > LAST:
                    return
                dve.wait_ge(split_hi, m + 1)
                nc.vector.tensor_tensor(w_lo[:, u], weight[:], w_hi[:, u].bitcast(F32), ALU.subtract).then_inc(split_lo, 1)
            split(0, 0, 0)

            def tile(m, i, u):
                split(m + 1, i + u, 1 - u)
                dve.wait_ge(a_evacuated, (m + 2) * N_BLOCKS)
                dve.wait_ge(stored[u], 16 * i)
                out = hidden[:, u, :]
                tap = lambda j: a_pre[:, N_META - 2 + j:N_META - 2 + j + SEQ]
                weight_of = lambda j: conv_w[:, bass.ds(m + j * M_FF, 1)]
                nc.vector.tensor_scalar(out, tap(2), weight_of(2), conv_b[:, bass.ds(m, 1)], ALU.mult, ALU.add).then_inc(tap_done, 1)
                dve.wait_ge(tap_done, 2 * m + 1)
                nc.vector.scalar_tensor_tensor(out, tap(1), weight_of(1), out, ALU.mult, ALU.add).then_inc(tap_done, 1)
                dve.wait_ge(tap_done, 2 * m + 2)
                nc.vector.scalar_tensor_tensor(out, tap(0), weight_of(0), out, ALU.mult, ALU.add).then_inc(conv_done, 1)
                dve.wait_ge(gelu_done, m + 1)
                for n in range(N_BLOCKS):
                    skip = N_META if n == 0 else 0
                    cols = hidden[:, u, n * N_TOK - N_META + skip:(n + 1) * N_TOK - N_META]
                    dve.wait_ge(products_done, (m + SLOTS) * GROUPS + N_BLOCKS + n + 1)
                    nc.vector.tensor_tensor(cols, cols, psum[:, bank(u, 1, n), skip:N_TOK], ALU.mult).then_inc(b_used, 1)
            tile_loop(dve, tile)


def hybrid_block(nc, ins, out):
    dram = lambda name, shape: nc.dram_tensor("scratch_" + name, shape, F32).ap()
    rwkv_proj = dram("rwkv_proj", [M_RWKV, P, T])
    gates = dram("gates", [M_GATE, P, T])
    s5_u = dram("s5_u", [P, S5_GROUPS, S5_CHUNKS])
    roles = dram("roles", [4, PAIRS, P, T])
    bonus = dram("bonus", [PAIRS, P, T])
    rwkv_gate = dram("rwkv_gate", [PAIRS, P, T])
    rwkv_y = dram("rwkv_y", [K4, P, T])
    s5_y = dram("s5_y", [K4, P, T])
    mixed = dram("mixed", [KD, P, T])
    h1 = dram("h1", [T, D_MODEL])
    hidden = dram("hidden", [M_FF, P, SEQ])

    with ExitStack() as ctx:
        in_use = []

        def sems(prefix, names):
            def new(n):
                in_use.append(nc.alloc_semaphore(f"{prefix}_{n}"))
                return in_use[-1]
            return [new(n) if isinstance(n, str) else [new(f"{n[0]}{j}") for j in range(n[1])] for n in names]

        def stage_ends():
            nc.clear_and_free_semaphores(in_use)
            in_use.clear()
            nc.all_engine_barrier()

        psum = ctx.enter_context(nc.psum_tensor("psum", [P, 8, 512], F32))
        cols_t = ctx.enter_context(nc.sbuf_tensor("cols_sb", [P, N_COLS], F32))
        ident_t = ctx.enter_context(nc.sbuf_tensor("ident_sb", [P, P], F32))
        decay_t = ctx.enter_context(nc.sbuf_tensor("chunk_decay", [P, PAIRS, CHUNKS], F32))
        cols, ident, decay = cols_t[:], ident_t[:], decay_t[:]
        consts_loaded, = sems("main", ["consts_loaded"])
        with nc.Block() as block:
            @block.sync
            def _(sp):
                sp.dma_start(cols, ins["columns"]).then_inc(consts_loaded, 16)
                sp.dma_start(ident, ins["identity"]).then_inc(consts_loaded, 16)
                sp.wait_ge(consts_loaded, 32)

        def normed_parts(name, stack):
            return [stack.enter_context(nc.sbuf_tensor(f"{name}_{part}", [P, KD, T], F32R)) for part in ("hi", "lo")]

        with ExitStack() as inner:
            x_hi, x_lo = normed_parts("x", inner)
            norm_transpose(nc, "pre", sems, psum, ins["h0"], x_hi, x_lo, cols[:, COL["mix_pre"]:COL["mix_pre"] + KD], ident)
            in_projection(nc, "proj", sems, psum, x_hi, x_lo, ins["w_in_tiles"], cols[:, COL["mu"]:COL["mu"] + M_RWKV], rwkv_proj, gates)
            s5_inputs(nc, "s5in", sems, psum, x_hi, x_lo, ins["w_in_s5"], s5_u, ident)
        stage_ends()
        rwkv_prepare(nc, "prep", sems, psum, rwkv_proj, ins["lora"], cols, roles, bonus, rwkv_gate, decay)
        rwkv_chunks(nc, "chunk", sems, psum, roles, rwkv_proj[2 * PAIRS:3 * PAIRS], decay, ins["chunk_masks"], bonus, rwkv_gate, cols, rwkv_y, ident)
        stage_ends()
        s5_scan(nc, "s5", sems, psum, ins, s5_u, s5_y, ident)
        branch_mix(nc, "mix", sems, psum, rwkv_y, s5_y, ins["w_mix_tiles"], gates, mixed)
        token_projection(nc, "mixout", sems, psum, mixed, N_META, ins["w_out"], KD, 1, ins["mix_post"], ins["h0"], h1, N_META, True)
        stage_ends()
        with ExitStack() as inner:
            h_hi, h_lo = normed_parts("h", inner)
            norm_transpose(nc, "ffnpre", sems, psum, h1, h_hi, h_lo, cols[:, COL["ffn_pre"]:COL["ffn_pre"] + KD], ident)
            ffn_up(nc, "up", sems, psum, h_hi, h_lo, ins["w_up_tiles"], cols[:, COL["conv_w"]:COL["conv_w"] + CONV_W * M_FF],
                   cols[:, COL["conv_b"]:COL["conv_b"] + M_FF], hidden)
        token_projection(nc, "down", sems, psum, hidden, 0, ins["w_down"], M_FF // 2, 2, ins["ffn_post"], h1, out, 0, False)
        stage_ends()


def lay_out(np, i):
    i = {name: np.asarray(a) for name, a in i.items()}
    one = {name: a[0] for name, a in i.items() if name != "meta_tokens"}
    channels = lambda a: a.reshape(-1, P).T

    def k_tiles(w, width):
        k, m = w.shape
        return w.reshape(k // P, P, m // width, width).transpose(2, 1, 0, 3)

    columns = {"mu": "rwkv_shift_mu", "w0": "rwkv_w0", "a0": "rwkv_a0", "k_k": "rwkv_k_k", "k_a": "rwkv_k_a", "r_k": "rwkv_r_k",
               "ln_g": "rwkv_ln_gain", "ln_b": "rwkv_ln_bias", "mix_pre": "norm_mix_pre", "ffn_pre": "norm_ffn_pre",
               "conv_w": "ffn_conv_w", "conv_b": "ffn_conv_b"}
    w_in = one["w_in"]
    s5_at = RWKV_PROJ
    gates_at = s5_at + D_MODEL // 2
    glu, up = one["s5_w_glu"], one["ffn_w_up"]
    twice = lambda a: np.concatenate([a, a], axis=0)
    rows = lambda a: np.broadcast_to(a[None], (P, *a.shape))
    index = np.arange(P)
    head, token = index // CHUNK, index % CHUNK
    same = head[:, None] == head[None, :]
    r, c = token[:, None], token[None, :]
    masks = [same & (r < c), same & (r <= c), same & (c == r + 1) & (r % 2 == 0)]
    masks += [same & (r // b % 2 == 1) & (c // b == r // b - 1) for b in (2, 4, 8, 16, 32)]
    arrays = {
        "h0": np.concatenate([i["meta_tokens"], one["x"]], axis=0),
        "columns": np.concatenate([channels(one[columns[name]]) for name, _ in COLUMNS], axis=1),
        "identity": np.eye(P, dtype=np.float32),
        "chunk_masks": np.stack(masks, axis=1).astype(np.float32),
        "w_in_tiles": np.concatenate([k_tiles(w_in[:, :s5_at], P), k_tiles(w_in[:, gates_at:], P)], axis=0),
        "w_in_s5": k_tiles(w_in[:, s5_at:gates_at], S5_GROUPS * S5_GROUP // 2),
        "lora": np.stack([np.concatenate([one["rwkv_w_up"], one["rwkv_a_up"]], axis=0), one["rwkv_g_up"]], axis=1),
        "w_mix_tiles": np.stack([k_tiles(w, P) for w in (one["rwkv_w_branch"], glu[:, :D_MODEL], glu[:, D_MODEL:])], axis=2),
        "w_out": one["w_out"].reshape(KD, P, D_MODEL),
        "mix_post": rows(one["norm_mix_post"]),
        "w_up_tiles": np.stack([k_tiles(up[:, :D_FF], P), k_tiles(up[:, D_FF:], P)], axis=2),
        "w_down": one["ffn_w_down"].reshape(M_FF, P, D_MODEL),
        "ffn_post": rows(one["norm_ffn_post"]),
        "lam_re": twice(one["s5_lambda_re"].T),
        "lam_im": twice(one["s5_lambda_im"].T),
        "log_dt": rows(one["s5_log_dt"]),
        "skip": np.tile(one["s5_d"].reshape(S5_GROUPS, S5_GROUP).T, (S5_CHUNK, 1)),
        "b_re": twice(one["s5_b_re"].transpose(1, 0, 2)),
        "b_im": twice(one["s5_b_im"].transpose(1, 0, 2)),
        "c_re": twice(one["s5_c_re"].transpose(2, 0, 1)),
        "c_im": twice(one["s5_c_im"].transpose(2, 0, 1)),
    }
    return {name: np.ascontiguousarray(a) for name, a in arrays.items()}


def kernel(**inputs):
    import numpy as np
    import concourse.bacc as bacc
    from concourse.bass_utils import run_bass_kernel_spmd

    arrays = lay_out(np, inputs)
    nc = bacc.Bacc("TRN2", target_bir_lowering=False, num_devices=1)
    ins = {name: nc.dram_tensor(f"in_{name}", a.shape, F32, kind="ExternalInput").ap() for name, a in arrays.items()}
    out = nc.dram_tensor("out_h", [SEQ, D_MODEL], F32, kind="ExternalOutput").ap()
    hybrid_block(nc, ins, out)
    r = run_bass_kernel_spmd(nc, [{f"in_{name}": a for name, a in arrays.items()}], core_ids=[0])
    return r.results[0]["out_h"].reshape(1, SEQ, D_MODEL)
```

```python
import math
from contextlib import ExitStack

import concourse.bass as bass
from concourse import mybir

F32 = mybir.dt.float32
F32R = mybir.dt.float32r
BF16 = mybir.dt.bfloat16
ALU = mybir.AluOpType
ACT = mybir.ActivationFunctionType

P = 128
D_MODEL, SEQ, N_META = 1024, 2048, 16
T = N_META + SEQ
KD = D_MODEL // P
SLOTS = 2
RMS_EPS, GN_EPS = 1e-6, 64e-5

RWKV_WIDTH, HEAD_DIM = D_MODEL // 2, 64
PAIRS = RWKV_WIDTH // P
RWKV_PROJ = 3 * RWKV_WIDTH + 256
CHUNK = 64
CHUNKS = -(-T // CHUNK)
ROLE_A, ROLE_B, ROLE_K, ROLE_R, ROLE_V = range(5)

S5_GROUPS, S5_GROUP, S5_STATE = 32, 16, 64
S5_CHUNK = P // S5_GROUP
S5_CHUNKS = T // S5_CHUNK
CT = 3
NT_ROWS = S5_CHUNKS // CT

M_RWKV, M_GATE = RWKV_PROJ // P, 2 * D_MODEL // P
D_FF, CONV_W = 2816, 3
M_FF = D_FF // P
K4 = RWKV_WIDTH // P
N_BLOCKS = 6
N_TOK = T // N_BLOCKS

COLUMNS = (("mu", M_RWKV), ("w0", PAIRS), ("a0", PAIRS), ("k_k", PAIRS), ("k_a", PAIRS), ("r_k", PAIRS), ("ln_g", PAIRS),
           ("ln_b", PAIRS), ("mix_pre", KD), ("ffn_pre", KD), ("conv_w", CONV_W * M_FF), ("conv_b", M_FF))
COL = {name: sum(n for _, n in COLUMNS[:j]) for j, (name, _) in enumerate(COLUMNS)}
N_COLS = sum(n for _, n in COLUMNS)

ROUNDER = 1.5 * 2.0 ** 23


def two_pi_parts():
    parts, rest = [], 2 * math.pi
    for bits in (8, 10):
        unit = 2.0 ** (math.floor(math.log2(rest)) - bits + 1)
        parts.append(math.floor(rest / unit) * unit)
        rest -= parts[-1]
    return parts + [rest]


TWO_PI_PARTS = two_pi_parts()


def norm_transpose(nc, name, sems, psum, src, x_hi, x_lo, gain, ident):
    rows_loaded, squares_done, std_ready, rstd_ready, rows_normed, turned, gained_ready, hi_ready, lo_ready, \
        eps_ready = sems(name, [("rows_loaded", 2), "squares_done", "std_ready", "rstd_ready", "rows_normed",
                                "turned", "gained_ready", "hi_ready", "lo_ready", "eps_ready"])
    with ExitStack() as ctx:
        sb = lambda n, shape, dt: ctx.enter_context(nc.sbuf_tensor(f"{name}_{n}", shape, dt))
        rows = sb("rows", [NT_ROWS, SLOTS, D_MODEL], F32)
        normed = sb("normed", [NT_ROWS, SLOTS, D_MODEL], F32)
        squares = sb("squares", [NT_ROWS, SLOTS, D_MODEL], BF16)
        stat = sb("stat", [NT_ROWS, SLOTS, 3], F32)
        eps = sb("eps", [NT_ROWS, 1], F32)
        gained = sb("gained", [P, SLOTS, KD, NT_ROWS], F32)
        block = ctx.enter_context(nc.Block())
        PAIRS_OF_TILES = T // NT_ROWS // SLOTS

        def turned_ps(u):
            return psum[:, 2 * u:2 * u + 2, 0:4 * NT_ROWS].rearrange("p b (k t) -> p b k t", k=4)

        LAST = PAIRS_OF_TILES - 1

        def tiles(eng, ahead, body):
            def step(i, u):
                if not (isinstance(i, int) and i == LAST and u == 1):
                    ahead(2 * i + u + 1, 1 - u, i + u)
                body(2 * i + u, u, i)
            ahead(0, 0, 0)
            with eng.Fori(0, LAST) as i:
                step(i, 0)
                step(i, 1)
            step(LAST, 0)
            step(LAST, 1)

        @block.sync
        def _(sp):
            with sp.Fori(0, PAIRS_OF_TILES) as i:
                for u in range(SLOTS):
                    sp.wait_ge(rows_normed, 2 * i + u + 1)
                    sp.dma_start(rows[:, u, :], src[bass.ds((2 * i + u) * NT_ROWS, NT_ROWS), :]).then_inc(rows_loaded[u], 16)

        @block.scalar
        def _(act):
            nc.scalar.preload_act_table(ACT.Sqrt)
            act.wait_ge(eps_ready, 1)

            def statistics(s, u, i):
                act.wait_ge(rows_loaded[u], 16 * i + 16)
                act.wait_ge(rows_normed, s + 1)
                nc.scalar.activation(squares[:, u, :], rows[:, u, :], ACT.Square, accum_out=stat[:, u, 0:1]).then_inc(squares_done, 1)
                act.wait_ge(squares_done, s + 1)
                nc.scalar.activation(stat[:, u, 1:2], stat[:, u, 0:1], ACT.Sqrt, scale=1.0 / D_MODEL, bias=eps[:]).then_inc(std_ready, 1)

            def split(s, u, i):
                act.wait_ge(gained_ready, s + 1 + SLOTS)
                nc.scalar.activation(x_hi[:, :, bass.ds(s * NT_ROWS, NT_ROWS)], gained[:, u], ACT.Copy).then_inc(hi_ready, 1)
            tiles(act, statistics, split)

        @block.vector
        def _(dve):
            dve.sem_inc(rows_normed, SLOTS)
            dve.sem_inc(gained_ready, SLOTS)
            dve.sem_inc(lo_ready, SLOTS)
            nc.vector.memset(eps[:], RMS_EPS).then_inc(eps_ready, 1)

            def norm(s, u, i):
                dve.wait_ge(std_ready, s + 1)
                nc.vector.reciprocal(stat[:, u, 2:3], stat[:, u, 1:2]).then_inc(rstd_ready, 1)
                dve.wait_ge(rstd_ready, s + 1)
                dve.wait_ge(turned, s + 1)
                nc.vector.tensor_scalar(normed[:, u, :], rows[:, u, :], stat[:, u, 2:3], None, ALU.mult).then_inc(rows_normed, 1)

            def split(s, u, i):
                dve.wait_ge(turned, s + 1 + SLOTS)
                dve.wait_ge(lo_ready, s + 1)
                nc.vector.tensor_tensor(gained[:, u].rearrange("p (b k) t -> p b k t", b=2), turned_ps(u),
                                        gain.rearrange("p (b k) -> p b k", b=2).unsqueeze(3).broadcast_to([P, 2, 4, NT_ROWS]), ALU.mult).then_inc(gained_ready, 1)
                dve.wait_ge(hi_ready, s + 1)
                nc.vector.tensor_tensor(x_lo[:, :, bass.ds(s * NT_ROWS, NT_ROWS)], gained[:, u],
                                        x_hi[:, :, bass.ds(s * NT_ROWS, NT_ROWS)].bitcast(F32), ALU.subtract).then_inc(lo_ready, 1)
            tiles(dve, norm, split)

        @block.tensor
        def _(pe):
            pe.sem_inc(turned, SLOTS)
            with pe.Fori(0, PAIRS_OF_TILES) as i:
                for u in range(SLOTS):
                    pe.wait_ge(rows_normed, 2 * i + u + 1 + SLOTS)
                    pe.wait_ge(gained_ready, 2 * i + u + 1)
                    for k in range(KD):
                        mm = nc.tensor.transpose(turned_ps(u)[:, k // 4, k % 4, :], normed[:, u, k * P:(k + 1) * P],
                                                 ident[0:NT_ROWS, 0:NT_ROWS])
                    mm.then_inc(turned, 1)


def in_projection(nc, name, sems, psum, x_hi, x_lo, w_tiles, mu, rwkv_out, gate_out):
    weight_loaded, split_hi, split_lo, products_done, evacuated, difference_ready, mixed_ready, stored, pad_ready = sems(name, [
        ("weight_loaded", 2), "split_hi", "split_lo", "products_done", "evacuated", "difference_ready", "mixed_ready",
        ("stored", 2), "pad_ready"])
    with ExitStack() as ctx:
        sb = lambda n, shape, dt: ctx.enter_context(nc.sbuf_tensor(f"{name}_{n}", shape, dt))
        weight = sb("weight", [P, SLOTS, KD, P], F32)
        w_hi = sb("w_hi", [P, SLOTS, KD, P], F32R)
        w_lo = sb("w_lo", [P, SLOTS, KD, P], F32R)
        pre = sb("pre", [P, SLOTS, 2 + T], F32)
        mixed = sb("mixed", [P, SLOTS, T], F32)
        block = ctx.enter_context(nc.Block())

        LAST = (M_RWKV + M_GATE) // 2 - 1

        def tile_loop(eng, body):
            with eng.Fori(0, M_RWKV // 2) as i:
                for u in range(SLOTS):
                    body(2 * i + u, i, u, True)
            with eng.Fori(M_RWKV // 2, LAST) as i:
                for u in range(SLOTS):
                    body(2 * i + u, i, u, False)
            for u in range(SLOTS):
                body(2 * LAST + u, LAST, u, False)

        @block.sync
        def _(sp):
            def load(m, u):
                sp.wait_ge(split_lo, m + 1)
                sp.dma_start(weight[:, u], w_tiles[bass.ds(m, 1)].rearrange("o p k c -> p (o k) c")).then_inc(weight_loaded[u], 16)

            def store_rwkv(m, u):
                sp.wait_ge(mixed_ready, m + 1 + SLOTS)
                sp.dma_start(rwkv_out[bass.ds(m, 1)].rearrange("o p t -> p (o t)"), mixed[:, u, :]).then_inc(stored[u], 16)

            def store_gate(m, u):
                sp.wait_ge(evacuated, m * N_BLOCKS + 2 * N_BLOCKS)
                sp.dma_start(gate_out[bass.ds(m - M_RWKV, 1)].rearrange("o p t -> p (o t)"), mixed[:, u, :]).then_inc(stored[u], 16)
            for u in range(SLOTS):
                sp.sem_inc(stored[u], 16)
            for u in range(SLOTS):
                load(u, u)
            for first, last, store in ((1, M_RWKV // 2 + 1, store_rwkv), (M_RWKV // 2 + 1, LAST + 1, store_gate)):
                with sp.Fori(first, last) as i:
                    for u in range(SLOTS):
                        load(2 * i + u, u)
                        store(2 * i - 2 + u, u)
            for u in range(SLOTS):
                store_gate(2 * LAST + u, u)
            for u in range(SLOTS):
                sp.wait_ge(stored[u], 16 * (M_RWKV + M_GATE) // 2 + 16)

        @block.tensor
        def _(pe):
            pe.sem_inc(products_done, SLOTS * N_BLOCKS)

            def tile(m, i, u, rwkv):
                pe.wait_ge(split_hi, m + 1)
                pe.wait_ge(split_lo, m + 1 + SLOTS)
                for n in range(N_BLOCKS):
                    pe.wait_ge(evacuated, m * N_BLOCKS + n + 1)
                    cols = slice(n * N_TOK, (n + 1) * N_TOK)
                    for k in range(KD):
                        for w, x in ((w_hi, x_hi), (w_hi, x_lo), (w_lo, x_hi)):
                            mm = nc.tensor.matmul(psum[:, n, 0:N_TOK], w[:, u, k, :], x[:, k, cols],
                                                  start=(k == 0 and w is w_hi and x is x_hi), stop=(k == KD - 1 and w is w_lo))
                    mm.then_inc(products_done, 1)
            tile_loop(pe, tile)

        @block.scalar
        def _(act):
            act.sem_inc(evacuated, N_BLOCKS)
            act.wait_ge(pad_ready, 1)

            def split(m, i, u):
                if u == 0 and isinstance(i, int) and i > LAST:
                    return
                act.wait_ge(weight_loaded[u], 16 * i + 16)
                act.wait_ge(products_done, (m + 1) * N_BLOCKS)
                nc.scalar.activation(w_hi[:, u], weight[:, u], ACT.Copy).then_inc(split_hi, 1)

            split(0, 0, 0)

            def tile(m, i, u, rwkv):
                split(m + 1, i + u, 1 - u)
                if rwkv:
                    act.wait_ge(mixed_ready, m + 1)
                else:
                    act.wait_ge(stored[u], 16 * i + 16)
                for n in range(N_BLOCKS):
                    act.wait_ge(products_done, (m + SLOTS) * N_BLOCKS + n + 1)
                    if rwkv:
                        nc.scalar.activation(pre[:, u, 2 + n * N_TOK:2 + (n + 1) * N_TOK], psum[:, n, 0:N_TOK], ACT.Copy).then_inc(evacuated, 1)
                    else:
                        nc.scalar.activation(mixed[:, u, n * N_TOK:(n + 1) * N_TOK], psum[:, n, 0:N_TOK], ACT.Sigmoid).then_inc(evacuated, 1)
            tile_loop(act, tile)

        @block.vector
        def _(dve):
            nc.vector.memset(pre[:, :, 0:2], 0.0).then_inc(pad_ready, 1)
            dve.sem_inc(split_lo, SLOTS)
            dve.sem_inc(mixed_ready, SLOTS)

            def split(m, i, u):
                if u == 0 and isinstance(i, int) and i > LAST:
                    return
                dve.wait_ge(weight_loaded[u], 16 * i + 16)
                dve.wait_ge(split_hi, m + 1)
                nc.vector.tensor_tensor(w_lo[:, u], weight[:, u], w_hi[:, u].bitcast(F32), ALU.subtract).then_inc(split_lo, 1)

            split(0, 0, 0)

            def tile(m, i, u, rwkv):
                split(m + 1, i + u, 1 - u)
                if not rwkv:
                    return
                dve.wait_ge(evacuated, (m + 2) * N_BLOCKS)
                dve.wait_ge(stored[u], 16 * i + 16)
                nc.vector.tensor_tensor(mixed[:, u, :], pre[:, u, 1:1 + T], pre[:, u, 2:2 + T], ALU.subtract).then_inc(difference_ready, 1)
                dve.wait_ge(difference_ready, m + 1)
                nc.vector.scalar_tensor_tensor(mixed[:, u, :], mixed[:, u, :], mu[:, bass.ds(m, 1)], pre[:, u, 2:2 + T],
                                               ALU.mult, ALU.add).then_inc(mixed_ready, 1)
            tile_loop(dve, tile)


def s5_inputs(nc, name, sems, psum, x_hi, x_lo, w_dram, u_out, ident):
    HG = S5_GROUPS // 2
    COLS = HG * S5_GROUP
    weight_loaded, split_hi, split_lo, products_done, evacuated, turned, turned_out, stored = sems(name, [
        "weight_loaded", "split_hi", "split_lo", "products_done", "evacuated", "turned", "turned_out", "stored"])
    with ExitStack() as ctx:
        sb = lambda n, shape, dt: ctx.enter_context(nc.sbuf_tensor(f"{name}_{n}", shape, dt))
        weight = sb("weight", [P, KD, COLS], F32)
        w_hi = sb("w_hi", [P, 2, KD, COLS], F32R)
        w_lo = sb("w_lo", [P, 2, KD, COLS], F32R)
        rows = sb("rows", [NT_ROWS, SLOTS, HG, S5_CHUNK, S5_GROUP], F32)
        cols = sb("cols", [P, HG, NT_ROWS], F32)
        block = ctx.enter_context(nc.Block())

        @block.sync
        def _(sp):
            sp.sem_inc(stored, 16)
            for half in range(2):
                sp.wait_ge(split_lo, half + 1)
                sp.dma_start(weight[:], w_dram[half]).then_inc(weight_loaded, 16)
            for half in range(2):
                for ct in range(CT):
                    sp.wait_ge(turned_out, half * CT + (ct + 2))
                    sp.dma_start(u_out[:, half * HG:(half + 1) * HG, ct * NT_ROWS:(ct + 1) * NT_ROWS], cols[:]).then_inc(stored, 16)
            sp.wait_ge(stored, 16 * 2 * CT + 16)

        @block.tensor
        def _(pe):
            pe.sem_inc(products_done, 1)
            pe.sem_inc(turned, 1)
            for half in range(2):
                def products(ct):
                    for tau in range(S5_CHUNK):
                        pe.wait_ge(evacuated, half * (CT * S5_CHUNK) + (ct * S5_CHUNK + tau + 1))
                        first = ct * NT_ROWS * S5_CHUNK + tau
                        for k in range(KD):
                            for x, w in ((x_hi, w_hi), (x_hi, w_lo), (x_lo, w_hi)):
                                mm = nc.tensor.matmul(psum[0:NT_ROWS, tau % 4, 0:COLS], x[:, k, first:first + (NT_ROWS - 1) * S5_CHUNK + 1:S5_CHUNK], w[:, half, k, :],
                                                      start=(k == 0 and x is x_hi and w is w_hi), stop=(k == KD - 1 and x is x_lo))
                        mm.then_inc(products_done, 1)

                def turn(ct):
                    pe.wait_ge(evacuated, half * (CT * S5_CHUNK) + ((ct + 1) * S5_CHUNK + 4))
                    pe.wait_ge(turned_out, half * CT + (ct + 1))
                    for g in range(HG):
                        mm = nc.tensor.transpose(psum[:, 4 + g // 4, (g % 4) * NT_ROWS:(g % 4 + 1) * NT_ROWS],
                                                 rows[:, ct % 2, g].rearrange("c t h -> c (t h)"), ident[0:NT_ROWS, 0:NT_ROWS])
                    mm.then_inc(turned, 1)
                pe.wait_ge(split_hi, half + 1)
                pe.wait_ge(split_lo, half + 2)
                products(0)
                for ct in range(1, CT):
                    products(ct)
                    turn(ct - 1)
                turn(CT - 1)

        @block.scalar
        def _(act):
            act.sem_inc(evacuated, 4)

            def split(half):
                act.wait_ge(weight_loaded, 16 * half + 16)
                nc.scalar.activation(w_hi[:, half], weight[:], ACT.Copy).then_inc(split_hi, 1)
            split(0)
            for half in range(2):
                for ct in range(CT):
                    if half == 0 and ct == 1:
                        split(1)
                    if ct >= 2:
                        act.wait_ge(turned, half * CT + ct)
                    else:
                        act.wait_ge(turned, half * CT + 1)
                    for tau in range(S5_CHUNK):
                        act.wait_ge(products_done, half * (CT * S5_CHUNK) + (ct * S5_CHUNK + tau + 2))
                        nc.scalar.activation(rows[:, ct % 2, :, tau, :], psum[0:NT_ROWS, tau % 4, 0:COLS].rearrange("c (g h) -> c g h", h=S5_GROUP),
                                             ACT.Copy).then_inc(evacuated, 1)

        @block.vector
        def _(dve):
            dve.sem_inc(split_lo, 1)
            dve.sem_inc(turned_out, 1)

            def split(half):
                dve.wait_ge(split_hi, half + 1)
                nc.vector.tensor_tensor(w_lo[:, half], weight[:], w_hi[:, half].bitcast(F32), ALU.subtract).then_inc(split_lo, 1)
            split(0)
            for half in range(2):
                for ct in range(CT):
                    if half == 0 and ct == 1:
                        split(1)
                    dve.wait_ge(turned, half * CT + (ct + 2))
                    dve.wait_ge(stored, half * (16 * CT) + (16 * ct + 16))
                    nc.vector.tensor_copy(cols[:].rearrange("p (b g) c -> p b (g c)", b=4), psum[:, 4:8, 0:4 * NT_ROWS]).then_inc(turned_out, 1)


class Count:

    def __init__(self, sem):
        self.sem, self.n = sem, 0

    def __call__(self, instruction):
        instruction.then_inc(self.sem, 1)
        self.n += 1


def s5_scan(nc, name, sems, psum, params, u_in, y_out, ident):
    G, H, C, N = S5_GROUPS, S5_GROUP, S5_CHUNK, S5_CHUNKS
    HG = G // 2
    J = C + 1
    names = ["params_loaded", "act_small", "small_ready", "u_loaded", "tables_built", "e_turned", "e_ready", "kernel_done",
             "kernel_ready", "toeplitz_loaded", "toeplitz_ready", "zeroed", "injected", "inject_used", "state_ready",
             "y_done", "y_ready", "y_turned", "y_flat", "stored", "dve_done", "factors_ready", "pool_done", "out_built"]
    (params_loaded, act_small, small_ready, u_loaded, tables_built, e_turned, e_ready, kernel_done,
     kernel_ready, toeplitz_loaded, toeplitz_ready, zeroed, injected, inject_used, state_ready,
     y_done, y_ready, y_turned, y_flat, stored, dve_done, factors_ready, pool_done, out_built) = sems(name, names)
    with ExitStack() as ctx:
        sb = lambda n, shape, dt=F32: ctx.enter_context(nc.sbuf_tensor(f"{name}_{n}", shape, dt))
        lam_re, lam_im, log_dt, skip = (sb(n, [P, G]) for n in ("lam_re", "lam_im", "log_dt", "skip"))
        b_re, b_im, c_re, c_im = (sb(n, [P, G, H]) for n in ("b_re", "b_im", "c_re", "c_im"))
        small = sb("small", [P, 16, G])
        dt, rate, theta, turns, angle, quarter, mag, rho, cosine, sine, den, coef_re, coef_im, t0, t1, t2 = (small[:, j, :] for j in range(16))
        pw_re = sb("pw_re", [P, J, G])
        pw_im = sb("pw_im", [P, J, G])
        pw_1 = sb("pw_1", [P, J, G])
        pw_2 = sb("pw_2", [P, J, G])
        pw_ft = sb("pw_ft", [P, 2, C, G])
        pw_t = sb("pw_t", [P, 2, C // 2, G])
        q_1 = sb("q_1", [P, G])
        q_2 = sb("q_2", [P, G])
        b_s = sb("b_s", [P, G, H])
        b_x = sb("b_x", [P, G, H])
        phase = sb("phase", [P, 4, G])
        out_1 = sb("out_1", [P, HG, J, H])
        out_2 = sb("out_2", [P, HG, J, H])
        tmp = sb("tmp", [P, HG, J, H])
        in_1 = sb("in_1", [P, HG, C, H])
        in_2 = sb("in_2", [P, HG, C, H])
        in_tmp = sb("in_tmp", [P, HG, C, H])
        b_t = in_tmp[:].rearrange("p g c h -> p (g c h)")[:, 0:G * H].rearrange("p (g h) -> p g h", g=G)
        in_t = sb("in_t", [P, 2, HG, P])
        kernel_t = sb("kernel_t", [H, HG, P])
        toeplitz = sb("toeplitz", [P, HG, P])
        cos_t = sb("cos_t", [P, HG, N])
        sin_t = sb("sin_t", [P, HG, N])
        u = sb("u", [P, HG, N])
        drive = sb("drive", [P, 2, N])
        drive_b = sb("drive_b", [P, 2, N])
        z = sb("z", [P, 2, N])
        part_c = sb("part_c", [P, 2, 1 + N])
        part_s = sb("part_s", [P, 2, 1 + N])
        y_rows = sb("y_rows", [NT_ROWS, CT, C, HG, H])
        y_cols = sb("y_cols", [P, 2, T])
        turn_tmp = y_cols[:].rearrange("p k t -> p (k t)")[:, 0:HG * P].rearrange("p (g c) -> p g c", g=HG)
        block = ctx.enter_context(nc.Block())
        LO, HI = slice(0, P // 2), slice(P // 2, P)

        def wide_tables(gs):
            over_h = lambda x, j0, j1: x[:, j0:j1, gs].rearrange("p j g -> p g j").unsqueeze(3).broadcast_to([P, HG, j1 - j0, H])
            over_j = lambda x, n: x[:, gs, :].unsqueeze(2).broadcast_to([P, HG, n, H])
            return over_h, over_j

        @block.sync
        def _(sp):
            for tile, key in ((lam_re, "lam_re"), (lam_im, "lam_im"), (log_dt, "log_dt"), (skip, "skip"),
                              (b_re, "b_re"), (b_im, "b_im"), (c_re, "c_re"), (c_im, "c_im")):
                sp.dma_start(tile[:], params[key]).then_inc(params_loaded, 16)
            for half in range(2):
                sp.wait_ge(y_done, half * HG)
                sp.dma_start(u[:], u_in[:, half * HG:(half + 1) * HG, :]).then_inc(u_loaded, 16)
                sp.wait_ge(kernel_ready, half + 1)
                sp.wait_ge(zeroed, 1)
                for tau in range(C):
                    sp.dma_start(toeplitz[tau * H:(tau + 1) * H, :, tau * H:], kernel_t[:, :, 0:P - tau * H]).then_inc(toeplitz_loaded, 16)
                for kt in range(2):
                    sp.wait_ge(y_flat, 6 * (2 * half + kt + 1))
                    sp.dma_start(y_out[2 * half + kt], y_cols[:, kt, :]).then_inc(stored, 16)
            sp.wait_ge(stored, 64)

        @block.gpsimd
        def _(pool):
            pool.memset(toeplitz[:], 0.0).then_inc(zeroed, 1)
            own = Count(pool_done)
            pool.wait_ge(factors_ready, 1)
            for half in range(2):
                over_h, over_j = wide_tables(slice(half * HG, (half + 1) * HG))
                if half:
                    pool.wait_ge(e_turned, 2)
                own(nc.gpsimd.tensor_tensor(in_1[:], over_j(b_s, C), over_h(pw_ft[:, 0], 0, C), ALU.mult))
                own(nc.gpsimd.tensor_tensor(in_tmp[:], over_j(b_x, C), over_h(pw_ft[:, 1], 0, C), ALU.mult))
                pool.wait_ge(pool_done, own.n)
                own(nc.gpsimd.tensor_tensor(in_1[:], in_1[:], in_tmp[:], ALU.add))
                own(nc.gpsimd.tensor_tensor(in_2[:], over_j(b_s, C), over_h(pw_ft[:, 1], 0, C), ALU.mult))
                pool.wait_ge(pool_done, own.n)
                own(nc.gpsimd.tensor_tensor(in_tmp[:], over_j(b_x, C), over_h(pw_ft[:, 0], 0, C), ALU.mult))
                pool.wait_ge(pool_done, own.n)
                nc.gpsimd.tensor_tensor(in_2[:], in_2[:], in_tmp[:], ALU.subtract).then_inc(tables_built, 1)
                pool.wait_ge(tables_built, half + 1)

        @block.scalar
        def _(act):
            act.wait_ge(params_loaded, 16 * 8)
            nc.scalar.activation(dt, log_dt[:], ACT.Exp).then_inc(act_small, 1)
            act.wait_ge(small_ready, 1)
            nc.scalar.activation(mag, rate, ACT.Exp).then_inc(act_small, 1)
            nc.scalar.activation(rho, rate, ACT.Exp, scale=float(C)).then_inc(act_small, 1)
            act.wait_ge(small_ready, 2)
            nc.scalar.activation(sine, angle, ACT.Sin).then_inc(act_small, 1)
            nc.scalar.activation(cosine, quarter, ACT.Sin).then_inc(act_small, 1)
            for half in range(2):
                for j in range(2):
                    act.wait_ge(e_turned, 2 * half + j + 1)
                    nc.scalar.activation(in_t[:, j].rearrange("p (b g) c -> p b (g c)", b=4), psum[:, 4 * j:4 * j + 4, :], ACT.Copy).then_inc(e_ready, 1)
                for g in range(HG):
                    if g == 0:
                        act.wait_ge(y_turned, 12 * half)
                    act.wait_ge(y_done, half * HG + g + 1)
                    nc.scalar.activation(y_rows[:, :, :, g, :], psum[0:NT_ROWS, 4 + g % 2, 0:CT * P].rearrange("c (t a h) -> c t a h", t=CT, h=H),
                                         ACT.Gelu_apprx_tanh).then_inc(y_ready, 1)
                for kt in range(2):
                    for ct in range(CT):
                        for th in range(2):
                            e = (kt * CT + ct) * 2 + th
                            act.wait_ge(y_turned, 12 * half + e + 1)
                            if half:
                                act.wait_ge(stored, 32)
                            first = ct * NT_ROWS * C + th * 4
                            dst = y_cols[:, kt, ct * NT_ROWS * C:(ct + 1) * NT_ROWS * C].rearrange("p (c a) -> p a c", a=C)[:, 4 * th:4 * th + 4, :]
                            nc.scalar.activation(dst, psum[:, 6 + e % 2, 0:4 * NT_ROWS].rearrange("p (a c) -> p a c", a=4), ACT.Copy).then_inc(y_flat, 1)

        @block.vector
        def _(dve):
            own = Count(dve_done)

            def settle():
                dve.wait_ge(dve_done, own.n)

            def tt(out, a, b, op):
                own(nc.vector.tensor_tensor(out, a, b, op))

            def ts(out, a, s1, s2, op0, op1=None):
                own(nc.vector.tensor_scalar(out, a, s1, s2, op0, op1) if op1 is not None else nc.vector.tensor_scalar(out, a, s1, None, op0))

            def complex_product(out_re, out_im, a_re, a_im, b_re, b_im, s, t):
                tt(out_re, a_re, b_re, ALU.mult)
                tt(s, a_im, b_im, ALU.mult)
                tt(out_im, a_re, b_im, ALU.mult)
                tt(t, a_im, b_re, ALU.mult)
                settle()
                tt(out_re, out_re, s, ALU.subtract)
                tt(out_im, out_im, t, ALU.add)
                settle()

            own(nc.vector.memset(part_c[:, :, 0:1], 0.0))
            own(nc.vector.memset(part_s[:, :, 0:1], 0.0))
            dve.wait_ge(params_loaded, 16 * 8)
            ts(lam_re[:], lam_re[:], -1e-4, None, ALU.min)
            dve.wait_ge(act_small, 1)
            settle()
            tt(theta, lam_im[:], dt, ALU.mult)
            nc.vector.tensor_tensor(rate, lam_re[:], dt, ALU.mult).then_inc(small_ready, 1)
            settle()
            ts(turns, theta, 1.0 / (2 * math.pi), None, ALU.mult)
            settle()
            ts(turns, turns, ROUNDER, None, ALU.add)
            settle()
            ts(turns, turns, ROUNDER, None, ALU.subtract)
            own(nc.vector.tensor_copy(angle, theta))
            settle()
            for piece in TWO_PI_PARTS:
                ts(t0, turns, piece, None, ALU.mult)
                settle()
                tt(angle, angle, t0, ALU.subtract)
                settle()
            ts(angle, angle, math.pi, -math.pi, ALU.min, ALU.max)
            settle()
            own(nc.vector.scalar_tensor_tensor(quarter, angle, -1.0, angle, ALU.mult, ALU.min))
            settle()
            nc.vector.tensor_scalar(quarter, quarter, math.pi / 2, None, ALU.add).then_inc(small_ready, 1)
            dve.wait_ge(act_small, 5)
            own(nc.vector.memset(pw_re[:, 0, :], 1.0))
            own(nc.vector.memset(pw_im[:, 0, :], 0.0))
            tt(pw_re[:, 1, :], mag, cosine, ALU.mult)
            tt(pw_im[:, 1, :], mag, sine, ALU.mult)
            settle()
            for n in (1, 2, 4):
                by_re = pw_re[:, n:n + 1, :].broadcast_to([P, n, G])
                by_im = pw_im[:, n:n + 1, :].broadcast_to([P, n, G])
                complex_product(pw_re[:, n + 1:2 * n + 1, :], pw_im[:, n + 1:2 * n + 1, :], pw_re[:, 1:n + 1, :], pw_im[:, 1:n + 1, :], by_re, by_im,
                                pw_t[:, 0, 0:n, :], pw_t[:, 1, 0:n, :])
            tt(t0, lam_re[:], lam_re[:], ALU.mult)
            tt(t1, lam_im[:], lam_im[:], ALU.mult)
            ts(t2, pw_re[:, 1, :], -1.0, None, ALU.add)
            settle()
            tt(den, t0, t1, ALU.add)
            settle()
            own(nc.vector.reciprocal(den, den))
            tt(coef_re, t2, lam_re[:], ALU.mult)
            tt(t0, pw_im[:, 1, :], lam_im[:], ALU.mult)
            tt(coef_im, pw_im[:, 1, :], lam_re[:], ALU.mult)
            tt(t1, t2, lam_im[:], ALU.mult)
            settle()
            tt(coef_re, coef_re, t0, ALU.add)
            tt(coef_im, coef_im, t1, ALU.subtract)
            settle()
            tt(coef_re, coef_re, den, ALU.mult)
            tt(coef_im, coef_im, den, ALU.mult)
            settle()
            own(nc.vector.tensor_copy(pw_1[LO], pw_re[LO]))
            ts(pw_1[HI], pw_im[HI], -1.0, None, ALU.mult)
            own(nc.vector.tensor_copy(pw_2[LO], pw_im[LO]))
            own(nc.vector.tensor_copy(pw_2[HI], pw_re[HI]))
            own(nc.vector.tensor_copy(q_1[LO], coef_re[LO]))
            own(nc.vector.tensor_copy(q_1[HI], coef_im[HI]))
            own(nc.vector.tensor_copy(q_2[LO], coef_im[LO]))
            ts(q_2[HI], coef_re[HI], -1.0, None, ALU.mult)
            for tau in range(C):
                own(nc.vector.tensor_copy(pw_ft[:, 0, tau, :], pw_re[:, C - 1 - tau, :]))
                own(nc.vector.tensor_copy(pw_ft[:, 1, tau, :], pw_im[:, C - 1 - tau, :]))
            settle()
            wide = lambda x: x.unsqueeze(2).broadcast_to([P, G, H])
            tt(b_s[:], b_re[:], wide(q_1[:]), ALU.mult)
            tt(b_t, b_im[:], wide(q_2[:]), ALU.mult)
            tt(b_x[:], b_re[:], wide(q_2[:]), ALU.mult)
            settle()
            tt(b_s[:], b_s[:], b_t, ALU.subtract)
            settle()
            tt(b_t, b_im[:], wide(q_1[:]), ALU.mult)
            settle()
            tt(b_x[:], b_x[:], b_t, ALU.add)
            settle()
            ts(b_x[:], b_x[:], -1.0, None, ALU.mult)
            settle()
            dve.sem_inc(factors_ready, 1)
            own(nc.vector.tensor_copy(phase[:, 0, :], cosine))
            own(nc.vector.tensor_copy(phase[:, 1, :], sine))
            settle()
            at = 0

            def square_phase(at):
                r, i, r2, i2 = (phase[:, (at + j) % 4, :] for j in range(4))
                complex_product(r2, i2, r, i, r, i, t0, t1)
                return (at + 2) % 4
            for _ in range(3):
                at = square_phase(at)
            own(nc.vector.tensor_copy(t2, phase[:, at, :]))
            own(nc.vector.tensor_copy(den, phase[:, at + 1, :]))
            settle()
            for half in range(2):
                gs = slice(half * HG, (half + 1) * HG)
                over_h, over_j = wide_tables(gs)
                if half:
                    dve.wait_ge(y_done, half * HG)
                tt(out_1[:], over_j(c_re, J), over_h(pw_1, 0, J), ALU.mult)
                tt(tmp[:], over_j(c_im, J), over_h(pw_2, 0, J), ALU.mult)
                settle()
                nc.vector.tensor_tensor(out_1[:], out_1[:], tmp[:], ALU.subtract).then_inc(out_built, 1)
                tt(out_2[:], over_j(c_re, J), over_h(pw_2, 0, J), ALU.mult)
                settle()
                dve.wait_ge(out_built, half + 1)
                tt(tmp[:], over_j(c_im, J), over_h(pw_1, 0, J), ALU.mult)
                settle()
                tt(out_2[:], out_2[:], tmp[:], ALU.add)
                settle()
                ts(out_2[:], out_2[:], -1.0, None, ALU.mult)
                dve.wait_ge(kernel_done, half + 1)
                nc.vector.tensor_copy(kernel_t[:].rearrange("p (b g) c -> p b (g c)", b=4), psum[0:H, 0:4, :]).then_inc(kernel_ready, 1)
                if half:
                    dve.wait_ge(tables_built, 2)
                own(nc.vector.memset(cos_t[:, :, 0:1], 1.0))
                own(nc.vector.memset(sin_t[:, :, 0:1], 0.0))
                own(nc.vector.tensor_copy(phase[:, 0, :], t2))
                own(nc.vector.tensor_copy(phase[:, 1, :], den))
                settle()
                at, n = 0, 1
                while n < N:
                    m = min(n, N - n)
                    by = lambda j: phase[:, at + j, gs].unsqueeze(2).broadcast_to([P, HG, m])
                    scr = tmp[:].rearrange("p g j h -> p g (j h)")
                    scr2 = in_tmp[:].rearrange("p g c h -> p g (c h)") if half else turn_tmp
                    complex_product(cos_t[:, :, n:n + m], sin_t[:, :, n:n + m], cos_t[:, :, 0:m], sin_t[:, :, 0:m], by(0), by(1),
                                    scr[:, :, 0:m], scr2[:, :, 0:m])
                    at = square_phase(at) if 2 * n < N else at
                    n += m
                dve.wait_ge(toeplitz_loaded, 16 * C * (half + 1))
                for g in range(HG):
                    last = nc.vector.scalar_tensor_tensor(toeplitz[:, g, :], ident, skip[:, half * HG + g:half * HG + g + 1], toeplitz[:, g, :], ALU.mult, ALU.add)
                    own(last)
                settle()
                dve.sem_inc(toeplitz_ready, 1)
                for g in range(HG):
                    s = half * HG + g
                    v = s % 2
                    cos_g, sin_g = cos_t[:, g, :], sin_t[:, g, :]
                    dve.wait_ge(injected, s + 1)
                    tt(drive[:, v, :], cos_g, psum[:, 2 * v, 0:N], ALU.mult)
                    nc.vector.tensor_tensor(drive_b[:, v, :], sin_g, psum[:, 2 * v + 1, 0:N], ALU.mult).then_inc(inject_used, 1)
                    dve.wait_ge(inject_used, s + 1)
                    settle()
                    tt(drive[:, v, :], drive[:, v, :], drive_b[:, v, :], ALU.add)
                    settle()
                    own(nc.vector.tensor_tensor_scan(z[:, v, :], rho[:, s:s + 1].broadcast_to([P, N]), drive[:, v, :], 0.0, ALU.mult, ALU.add))
                    if s >= 2:
                        dve.wait_ge(y_done, s - 1)
                    settle()
                    nc.vector.tensor_tensor(part_c[:, v, 1:], cos_g, z[:, v, :], ALU.mult).then_inc(state_ready, 1)
                    nc.vector.tensor_tensor(part_s[:, v, 1:], sin_g, z[:, v, :], ALU.mult).then_inc(state_ready, 1)

        @block.tensor
        def _(pe):
            for half in range(2):
                if half:
                    pe.wait_ge(y_ready, half * HG)
                    pe.wait_ge(y_flat, 12 * half)
                pe.wait_ge(out_built, half + 1)
                for g in range(HG):
                    mm = nc.tensor.matmul(psum[0:H, g // 4, (g % 4) * P:(g % 4 + 1) * P], b_s[:, half * HG + g, :],
                                          out_1[:, g, 0:C, :].rearrange("p a h -> p (a h)"), start=True, stop=True)
                mm.then_inc(kernel_done, 1)
                pe.wait_ge(tables_built, half + 1)
                pe.wait_ge(kernel_ready, half + 1)
                for j, table in enumerate((in_1, in_2)):
                    for g in range(HG):
                        mm = nc.tensor.transpose(psum[:, 4 * j + g // 4, (g % 4) * P:(g % 4 + 1) * P], table[:, g].rearrange("p a h -> p (a h)"), ident)
                    mm.then_inc(e_turned, 1)
                pe.wait_ge(e_ready, 2 * half + 2)
                pe.wait_ge(u_loaded, 16 * (half + 1))

                def inject(g):
                    s = half * HG + g
                    v = s % 2
                    if s >= 2:
                        pe.wait_ge(inject_used, s - 1)
                    for j in range(2):
                        mm = nc.tensor.matmul(psum[:, 2 * v + j, 0:N], in_t[:, j, g, :], u[:, g, :], start=True, stop=True)
                    mm.then_inc(injected, 1)

                def outputs(g):
                    s = half * HG + g
                    v = s % 2
                    if s >= 2:
                        pe.wait_ge(y_ready, s - 1)
                    pe.wait_ge(state_ready, 2 * s + 2)
                    for ct in range(CT):
                        at = slice(ct * NT_ROWS, (ct + 1) * NT_ROWS)
                        y = psum[0:NT_ROWS, 4 + v, ct * P:(ct + 1) * P]
                        nc.tensor.matmul(y, u[:, g, at], toeplitz[:, g, :], start=True, stop=False)
                        nc.tensor.matmul(y, part_c[:, v, at], out_1[:, g, 1:, :].rearrange("p a h -> p (a h)"), start=False, stop=False)
                        mm = nc.tensor.matmul(y, part_s[:, v, at], out_2[:, g, 1:, :].rearrange("p a h -> p (a h)"), start=False, stop=True)
                    mm.then_inc(y_done, 1)
                inject(0)
                pe.wait_ge(toeplitz_ready, half + 1)
                for g in range(HG):
                    if g + 1 < HG:
                        inject(g + 1)
                    outputs(g)
                pe.wait_ge(y_ready, (half + 1) * HG)
                for kt in range(2):
                    for ct in range(CT):
                        for th in range(2):
                            e = (kt * CT + ct) * 2 + th
                            if 12 * half + e >= 2:
                                pe.wait_ge(y_flat, 12 * half + e - 1)
                            for a in range(4):
                                mm = nc.tensor.transpose(psum[:, 6 + e % 2, a * NT_ROWS:(a + 1) * NT_ROWS],
                                                         y_rows[:, ct, 4 * th + a, 8 * kt:8 * kt + 8, :].rearrange("c g h -> c (g h)"),
                                                         ident[0:NT_ROWS, 0:NT_ROWS])
                            mm.then_inc(y_turned, 1)


def rwkv_prepare(nc, name, sems, psum, proj, lora, cols, prep, bonus_out, gate_out, chunk_decay):
    (loaded, lora_loaded, lora_ready, constants_ready, zeroed, ones_ready,
     w_summed, a_summed, g_summed, norm_summed, bonus_summed,
     sig_ready, a_ready, gate_ready, kk_squared, prev_exp, decay_exp, grow_exp, chunk_copied, norm_log,
     kk_scaled, scanned, prev_ready, factor_ready, key_ready, role_k, role_r, norm_capped, norm_inverted, kk_normed,
     role_a, kk_a, role_b, rk_ready, bonus_ready, roles_stored, bonus_stored, gate_stored) = sems(name, [
         ("loaded", 3), "lora_loaded", "lora_ready", "constants_ready", "zeroed", "ones_ready",
         "w_summed", "a_summed", "g_summed", "norm_summed", "bonus_summed",
         "sig_ready", "a_ready", "gate_ready", "kk_squared", "prev_exp", "decay_exp", "grow_exp", "chunk_copied", "norm_log",
         "kk_scaled", "scanned", "prev_ready", "factor_ready", "key_ready", "role_k", "role_r", "norm_capped", "norm_inverted",
         "kk_normed", "role_a", "kk_a", "role_b", "rk_ready", "bonus_ready", ("roles_stored", 2), ("bonus_stored", 2),
         ("gate_stored", 2)])
    DECAY = math.exp(-0.5)
    UNITS = 2 * PAIRS
    BLOCKS = 4
    RKV_SLOTS = 3
    FIRST = (CHUNKS + 1) // 2
    SPAN = (N_META + (FIRST - 1) * CHUNK, T - N_META - (FIRST - 1) * CHUNK)
    START = (0, SPAN[0])
    WIDE = SPAN[0]
    with ExitStack() as ctx:
        sb = lambda n, shape, dt=F32: ctx.enter_context(nc.sbuf_tensor(f"{name}_{n}", shape, dt))
        ups = sb("ups", [P, 2, RWKV_WIDTH])
        low = sb("low", [P, 2, T])
        rkv = sb("rkv", [P, RKV_SLOTS, 3, WIDE])
        sig, a, cs, cs_prev, kk, work, bonus, gate = (sb(n, [P, 2, WIDE]) for n in
                                                      ("sig", "a", "cs", "cs_prev", "kk", "work", "bonus", "gate"))
        rk = sb("rk", [P, 2, WIDE])
        role = sb("role", [P, 2, 4, WIDE])
        mask = sb("mask", [P, T])
        heads = sb("heads", [P, P])
        one_less = sb("one_less", [P, PAIRS])
        block = ctx.enter_context(nc.Block())
        col = lambda key, j: cols[:, COL[key] + j:COL[key] + j + 1]

        def units(first=0, last=UNITS):
            for s in range(first, last):
                yield s, s // 2, s % 2, SPAN[s % 2]

        def banks(g, n):
            return psum[:, 4 * g:4 * g + 4, 0:n // BLOCKS]

        blocks = lambda t: t.rearrange("p (n c) -> p n c", n=BLOCKS)
        ORDER = ("w", "a", "g", "bonus", "norm")
        banks_of = lambda which, s, n: banks((ORDER.index(which) + s) % 2, n)

        @block.sync
        def _(sp):
            tokens = lambda h: slice(START[h], START[h] + SPAN[h])

            def load(s, j, h, n):
                if s >= RKV_SLOTS:
                    sp.wait_ge(bonus_ready, s - RKV_SLOTS + 1)
                sp.dma_start(rkv[:, s % RKV_SLOTS, :, 0:n], proj[j:3 * PAIRS:PAIRS, :, tokens(h)].rearrange("a p t -> p a t")).then_inc(loaded[s % RKV_SLOTS], 16)

            sp.dma_start(ups[:], lora).then_inc(lora_loaded, 16)
            sp.dma_start(low[:], proj[3 * PAIRS:3 * PAIRS + 2].rearrange("a p t -> p a t")).then_inc(lora_loaded, 16)
            for unit in units(0, RKV_SLOTS):
                load(*unit)
            for s, j, h, n in units():
                sp.wait_ge(gate_ready, s + 1)
                sp.dma_start(gate_out[j][:, tokens(h)], gate[:, h, 0:n]).then_inc(gate_stored[h], 16)
                for ready in (role_k, role_r, role_a, role_b):
                    sp.wait_ge(ready, s + 1)
                sp.dma_start(prep[:, j, :, tokens(h)].rearrange("r p t -> p r t"), role[:, h, :, 0:n]).then_inc(roles_stored[h], 16)
                sp.wait_ge(bonus_ready, s + 1)
                sp.dma_start(bonus_out[j][:, tokens(h)], bonus[:, h, 0:n]).then_inc(bonus_stored[h], 16)
                for unit in units(s + RKV_SLOTS, min(s + RKV_SLOTS + 1, UNITS)):
                    load(*unit)
            for h in range(2):
                for stored in (gate_stored, roles_stored, bonus_stored):
                    sp.wait_ge(stored[h], 16 * PAIRS)

        @block.tensor
        def _(pe):
            pe.wait_ge(lora_ready, 2)
            pe.wait_ge(constants_ready, 3)

            def product(which, s, weights, x, n, done):
                for b in range(BLOCKS):
                    w = n // BLOCKS
                    mm = nc.tensor.matmul(banks_of(which, s, n)[:, b, :], weights, x[:, b * w:(b + 1) * w], start=True, stop=True)
                mm.then_inc(done, 1)

            def low_rank(s, j, h, n):
                c, t = slice(j * P, (j + 1) * P), slice(START[h], START[h] + n)
                if s >= 3:
                    pe.wait_ge(bonus_ready, s - 2)
                product("w", s, ups[0:64, 0, c], low[0:64, 0, t], n, w_summed)
                if s:
                    pe.wait_ge(norm_capped, s)
                product("a", s, ups[64:128, 0, c], low[64:128, 0, t], n, a_summed)
                pe.wait_ge(sig_ready, s + 1)
                product("g", s, ups[:, 1, c], low[:, 1, t], n, g_summed)
                pe.wait_ge(a_ready, s + 1)
                pe.wait_ge(gate_ready, s + 1)

            def norm(s, j, h, n):
                pe.wait_ge(kk_squared, s + 1)
                product("norm", s, heads[:], work[:, h], n, norm_summed)

            for unit in units(0, 2):
                low_rank(*unit)
                norm(*unit)
            for s, j, h, n in units():
                ahead = list(units(s + 2, min(s + 3, UNITS)))
                for unit in ahead:
                    low_rank(*unit)
                if not ahead:
                    pe.wait_ge(norm_capped, UNITS)
                    pe.wait_ge(bonus_ready, max(s - 1, 1))
                pe.wait_ge(rk_ready, s + 1)
                product("bonus", s, heads[:], rk[:, h], n, bonus_summed)
                for unit in ahead:
                    norm(*unit)

        @block.scalar
        def _(act):
            act.wait_ge(lora_loaded, 32)
            nc.scalar.activation(low[0:64, 0, :], low[0:64, 0, :], ACT.Tanh).then_inc(lora_ready, 1)
            nc.scalar.activation(low[:, 1, :], low[:, 1, :], ACT.Sigmoid).then_inc(lora_ready, 1)

            def first_steps(s, j, h, n):
                act.wait_ge(w_summed, s + 1)
                if s >= 2:
                    act.wait_ge(role_r, s - 1)
                    act.wait_ge(chunk_copied, s - 1)
                nc.scalar.activation(blocks(sig[:, h, 0:n]), banks_of("w", s, n), ACT.Sigmoid, bias=col("w0", j)).then_inc(sig_ready, 1)
                act.wait_ge(a_summed, s + 1)
                if s >= 2:
                    act.wait_ge(kk_a, s - 1)
                nc.scalar.activation(blocks(a[:, h, 0:n]), banks_of("a", s, n), ACT.Sigmoid, bias=col("a0", j)).then_inc(a_ready, 1)
                act.wait_ge(g_summed, s + 1)
                if s >= 2:
                    act.wait_ge(gate_stored[h], 16 * (s // 2))
                nc.scalar.activation(blocks(gate[:, h, 0:n]), banks_of("g", s, n), ACT.Copy).then_inc(gate_ready, 1)
                act.wait_ge(kk_scaled, s + 1)
                if s >= 2:
                    act.wait_ge(kk_normed, s - 1)
                nc.scalar.activation(work[:, h, 0:n], kk[:, h, 0:n], ACT.Square).then_inc(kk_squared, 1)

            for unit in units(0, 2):
                first_steps(*unit)
            for s, j, h, n in units():
                act.wait_ge(norm_capped, s + 1)
                nc.scalar.activation(work[:, h, 0:n], work[:, h, 0:n], ACT.Ln).then_inc(norm_log, 1)
                act.wait_ge(scanned, s + 1)
                act.wait_ge(prev_ready, s + 1)
                nc.scalar.activation(sig[:, h, 0:n], cs[:, h, 0:n], ACT.Exp, scale=-DECAY).then_inc(decay_exp, 1)
                nc.scalar.activation(cs_prev[:, h, 0:n], cs_prev[:, h, 0:n], ACT.Exp, scale=-DECAY).then_inc(prev_exp, 1)
                act.wait_ge(decay_exp, s + 1)
                nc.scalar.activation(cs[:, h, 0:n], cs[:, h, 0:n], ACT.Exp, scale=DECAY).then_inc(grow_exp, 1)
                c0, ends = (0, slice(N_META - 1, n, CHUNK)) if h == 0 else (FIRST, slice(CHUNK - 1, n, CHUNK))
                nc.scalar.activation(chunk_decay[:, j, c0:c0 + (CHUNKS - FIRST if h else FIRST)], sig[:, h, ends], ACT.Copy).then_inc(chunk_copied, 1)
                act.wait_ge(norm_log, s + 1)
                nc.scalar.activation(work[:, h, 0:n], work[:, h, 0:n], ACT.Exp, scale=-0.5).then_inc(norm_inverted, 1)
                for unit in units(s + 2, min(s + 3, UNITS)):
                    first_steps(*unit)

        @block.vector
        def _(dve):
            V = nc.vector
            V.memset(heads[:], 0.0).then_inc(zeroed, 1)
            V.memset(mask[:], 1.0).then_inc(zeroed, 1)
            dve.wait_ge(zeroed, 2)
            V.memset(heads[0:64, 0:64], 1.0).then_inc(constants_ready, 1)
            V.memset(heads[64:128, 64:128], 1.0).then_inc(constants_ready, 1)
            V.memset(mask[:, N_META:T:CHUNK], 0.0).then_inc(constants_ready, 1)
            V.tensor_scalar(one_less[:], cols[:, COL["k_a"]:COL["k_a"] + PAIRS], -1.0, 1.0, ALU.mult, ALU.add).then_inc(ones_ready, 1)
            dve.wait_ge(constants_ready, 3)
            dve.wait_ge(ones_ready, 1)

            def scale_kk(s, j, h, n):
                dve.wait_ge(loaded[s % RKV_SLOTS], 16 * (s // RKV_SLOTS) + 16)
                V.tensor_scalar(kk[:, h, 0:n], rkv[:, s % RKV_SLOTS, 1, 0:n], col("k_k", j), None, ALU.mult).then_inc(kk_scaled, 1)

            def first_steps(s, j, h, n):
                dve.wait_ge(sig_ready, s + 1)
                V.tensor_tensor_scan(cs[:, h, 0:n], mask[:, START[h]:START[h] + n], sig[:, h, 0:n], 0.0, ALU.mult, ALU.add).then_inc(scanned, 1)
                dve.wait_ge(scanned, s + 1)
                V.tensor_tensor(cs_prev[:, h, 0:n], cs[:, h, 0:n], sig[:, h, 0:n], ALU.subtract).then_inc(prev_ready, 1)
                dve.wait_ge(a_ready, s + 1)
                if s >= 2:
                    dve.wait_ge(bonus_stored[h], 16 * (s // 2))
                V.tensor_scalar(bonus[:, h, 0:n], a[:, h, 0:n], col("k_a", j), one_less[:, j:j + 1], ALU.mult, ALU.add).then_inc(factor_ready, 1)
                dve.wait_ge(factor_ready, s + 1)
                V.tensor_tensor(bonus[:, h, 0:n], rkv[:, s % RKV_SLOTS, 1, 0:n], bonus[:, h, 0:n], ALU.mult).then_inc(key_ready, 1)
                dve.wait_ge(norm_summed, s + 1)
                V.tensor_scalar(blocks(work[:, h, 0:n]), banks_of("norm", s, n), 1e-24, None, ALU.max).then_inc(norm_capped, 1)

            for unit in units(0, 1):
                scale_kk(*unit)
                first_steps(*unit)
            for unit in units(1, 2):
                scale_kk(*unit)
            for s, j, h, n in units():
                r, v = rkv[:, s % RKV_SLOTS, 0, 0:n], rkv[:, s % RKV_SLOTS, 2, 0:n]
                kk_, work_, a_, bonus_ = kk[:, h, 0:n], work[:, h, 0:n], a[:, h, 0:n], bonus[:, h, 0:n]
                for unit in units(s + 1, min(s + 2, UNITS)):
                    first_steps(*unit)
                if s >= 2:
                    dve.wait_ge(roles_stored[h], 16 * (s // 2))
                    dve.wait_ge(bonus_summed, s - 1)
                dve.wait_ge(key_ready, s + 1)
                V.scalar_tensor_tensor(rk[:, h, 0:n], r, col("r_k", j), bonus_, ALU.mult, ALU.mult).then_inc(rk_ready, 1)
                dve.wait_ge(decay_exp, s + 1)
                V.tensor_tensor(role[:, h, ROLE_R, 0:n], r, sig[:, h, 0:n], ALU.mult).then_inc(role_r, 1)
                dve.wait_ge(grow_exp, s + 1)
                V.tensor_tensor(role[:, h, ROLE_K, 0:n], bonus_, cs[:, h, 0:n], ALU.mult).then_inc(role_k, 1)
                dve.wait_ge(norm_inverted, s + 1)
                V.tensor_tensor(kk_, kk_, work_, ALU.mult).then_inc(kk_normed, 1)
                dve.wait_ge(kk_normed, s + 1)
                dve.wait_ge(prev_exp, s + 1)
                V.scalar_tensor_tensor(role[:, h, ROLE_A, 0:n], kk_, -1.0, cs_prev[:, h, 0:n], ALU.mult, ALU.mult).then_inc(role_a, 1)
                V.tensor_tensor(kk_, kk_, a_, ALU.mult).then_inc(kk_a, 1)
                dve.wait_ge(kk_a, s + 1)
                V.tensor_tensor(role[:, h, ROLE_B, 0:n], kk_, cs[:, h, 0:n], ALU.mult).then_inc(role_b, 1)
                for unit in units(s + 2, min(s + 3, UNITS)):
                    dve.wait_ge(role_b, s + 1)
                    scale_kk(*unit)
                dve.wait_ge(bonus_summed, s + 1)
                dve.wait_ge(role_k, s + 1)
                V.tensor_tensor(blocks(bonus_), banks_of("bonus", s, n), blocks(v), ALU.mult).then_inc(bonus_ready, 1)


def rwkv_chunks(nc, name, sems, psum, prep, v_dram, chunk_decay, masks_dram, bonus_dram, gate_dram, cols, y_out, ident):
    NC_, S = CHUNKS, CHUNK
    (masks_loaded, roles_loaded, r_loaded, ar_loaded, cleared, grams_cleared, grams_done, masked, toks_done, toks_ready, x1_turned, x1_ready,
     lx_done, q_ready, xq_done, x_ready, xt_turned, xt_ready, w_done, w_ready, u_done, u_ready, m_done, m_ready,
     y_done, y_ready, norm_own, normed, y_turned, y_flat, sq_done, sq_ready, post_loaded, post_own, post_gained, stored, eps_set, std_done,
     m_half, q_init) = sems(name, [
         "masks_loaded", ("roles_loaded", 2), ("r_loaded", 2), ("ar_loaded", 2), "cleared", "grams_cleared", "grams_done", "masked", "toks_done", "toks_ready",
         "x1_turned", "x1_ready", "lx_done", "q_ready", "xq_done", "x_ready", "xt_turned", "xt_ready", "w_done", "w_ready",
         "u_done", "u_ready", "m_done", "m_ready", "y_done", "y_ready", "norm_own", "normed", "y_turned", "y_flat",
         "sq_done", "sq_ready", ("post_loaded", 4), "post_own", "post_gained", "stored", "eps_set", "std_done", "m_half", "q_init"])
    with ExitStack() as ctx:
        sb = lambda n, shape, dt=F32: ctx.enter_context(nc.sbuf_tensor(f"{name}_{n}", shape, dt))
        masks = sb("masks", [P, 8, P])
        roles = sb("roles", [P, 2, 5, PAIRS, 2, S])
        grams = sb("grams", [P, 2, 3, PAIRS, P])
        toks = sb("toks", [P, 2, 3, PAIRS, P])
        pairs_ar = sb("pairs_ar", [P, 2, PAIRS, 2, S])
        l_t = sb("l_t", [P, PAIRS, P])
        x = sb("x", [P, PAIRS, P])
        x_t = sb("x_t", [P, 2, PAIRS, P])
        q = sb("q", [P, PAIRS, P])
        w = sb("w", [P, PAIRS, P])
        u = sb("u", [P, PAIRS, P])
        m = sb("m", [P, 2, PAIRS, P])
        y = sb("y", [P, PAIRS, HEAD_DIM])
        y_sq = sb("y_sq", [P, PAIRS, HEAD_DIM])
        y_bd = sb("y_bd", [P, PAIRS, 2, HEAD_DIM])
        stat = sb("stat", [P, 4, PAIRS])
        eps = sb("eps", [P, 1])
        y_all = sb("y_all", [P, PAIRS, NC_ * S])
        post = sb("post", [P, SLOTS, 2, T])
        block = ctx.enter_context(nc.Block())
        HALVES = (slice(0, 2), slice(2, 4))
        LEVELS = 5
        TOKS = ((ROLE_K, 2, 1), (ROLE_V, 3, 2), (ROLE_B, 2, 0))
        MASKED = 9
        wide = lambda mk, n: masks[:, mk, :].unsqueeze(1).broadcast_to([P, n, P])
        bank = lambda b: psum[:, b, :].rearrange("p (j c) -> p j c", j=PAIRS)
        half_bank = lambda b: psum[:, b, 0:2 * P].rearrange("p (j c) -> p j c", j=2)
        flat = lambda ap: ap.rearrange("p j h c -> p j (h c)")

        def at(eng, sem, per, c, n):
            eng.wait_ge(sem, per * c + n)

        def done(eng, sem, per, c):
            if not isinstance(c, int) or c > 0:
                eng.wait_ge(sem, per * c)

        def steps(eng, step):
            step(-1, 1, 0, True, False)
            step(0, 0, 0, True, True)
            with eng.Fori(0, (NC_ - 3) // 2) as i:
                step(2 * i + 1, 1, i + 1, True, True)
                step(2 * i + 2, 0, i + 1, True, True)
            step(NC_ - 2, 1, (NC_ - 1) // 2, True, True)
            step(NC_ - 1, 0, (NC_ - 1) // 2, False, True)

        @block.sync
        def _(sp):
            sp.dma_start(masks[:], masks_dram).then_inc(masks_loaded, 16)

            def load(r, v, t0, n, sem):
                for h in range(2):
                    rows = slice(h * 64, (h + 1) * 64)
                    src = (prep[r] if r < 4 else v_dram)[:, rows, bass.ds(t0, n)]
                    sp.dma_start(roles[rows, v, r, :, h, S - n:S], src.rearrange("j p t -> p j t")).then_inc(sem[v], 16)

            def load_chunk(c, v):
                t0, n = (0, N_META) if isinstance(c, int) and c == 0 else (c * S + (N_META - S), S)
                if not isinstance(c, int) or c >= 2:
                    sp.wait_ge(w_done, c - 1)
                for q, r in enumerate((ROLE_A, ROLE_R)):
                    sp.dma_start(pairs_ar[:, v, :, q, S - n:S], prep[r][:, :, bass.ds(t0, n)].rearrange("j p t -> p j t")).then_inc(ar_loaded[v], 16)
                for r in (ROLE_B, ROLE_K, ROLE_A, ROLE_V):
                    load(r, v, t0, n, roles_loaded)
                if not isinstance(c, int) or c >= 2:
                    sp.wait_ge(y_done, c - 1)
                load(ROLE_R, v, t0, n, r_loaded)

            def load_post(j):
                sp.dma_start(post[:, j % 2, 0, :], bonus_dram[j]).then_inc(post_loaded[2 * (j % 2)], 16)
                sp.dma_start(post[:, j % 2, 1, :], gate_dram[j]).then_inc(post_loaded[2 * (j % 2) + 1], 16)
            sp.wait_ge(cleared, 2)
            load_chunk(0, 0)
            sp.wait_ge(cleared, 4)
            load_chunk(1, 1)
            load_post(0)
            load_post(1)
            with sp.Fori(0, (NC_ - 3) // 2) as i:
                load_chunk(2 * i + 2, 0)
                load_chunk(2 * i + 3, 1)
            load_chunk(NC_ - 1, 0)
            for j in range(PAIRS):
                sp.wait_ge(post_own, 2 * j + 2)
                sp.dma_start(y_out[j], y_all[:, j, NC_ * S - T:]).then_inc(stored, 16)
                if j + 2 < PAIRS:
                    load_post(j + 2)
            sp.wait_ge(stored, 16 * PAIRS)

        @block.tensor
        def _(pe):
            T_ = nc.tensor
            R = lambda v, r, j: roles[:, v, r, j].rearrange("p h c -> p (h c)")

            def grams_of(c, v, k):
                pe.wait_ge(roles_loaded[v], 128 * k + 128)
                pe.wait_ge(ar_loaded[v], 32 * k + 32)
                done(pe, q_ready, 2 * LEVELS, c)
                for n, s in enumerate((ROLE_B, ROLE_K)):
                    for j in range(PAIRS):
                        mm = T_.matmul(bank(n)[:, j, :], R(v, s, j), pairs_ar[:, v, j].rearrange("p q c -> p (q c)"), start=True, stop=True)
                    mm.then_inc(grams_done, 1)

            def turn_toks(c, v):
                done(pe, x_ready, 2 * LEVELS, c)
                for n, (r, b, _) in enumerate(TOKS):
                    if n == 2:
                        at(pe, toks_ready, 3, c, 1)
                    for j in range(PAIRS):
                        mm = T_.transpose(bank(b)[:, j, :], R(v, r, j), ident)
                    mm.then_inc(toks_done, 1)

            def turn_x1(c, v):
                at(pe, masked, MASKED, c, 3)
                at(pe, masked, MASKED, c, MASKED - 4)
                for j in range(PAIRS):
                    mm = T_.transpose(bank(0)[:, j, :], x_t[:, v, j, :], ident)
                mm.then_inc(x1_turned, 1)

            def lx(c, v, l):
                for h in range(2):
                    if l == 0:
                        at(pe, x1_ready, 1, c, 1)
                        at(pe, masked, MASKED, c, MASKED)
                    else:
                        at(pe, x_ready, 10, c, 2 * (l - 1) + h + 1)
                        at(pe, xt_ready, 8, c, 2 * (l - 1) + h + 1)
                    for n, j in enumerate((0, 1)):
                        mm = T_.matmul(half_bank(h)[:, n, :], l_t[:, 2 * h + j, :], x[:, 2 * h + j, :], start=True, stop=True)
                    mm.then_inc(lx_done, 1)

            def xq(c, v, l):
                for h in range(2):
                    at(pe, q_ready, 10, c, 2 * l + h + 1)
                    if l == 0:
                        at(pe, toks_ready, 3, c, 3)
                    else:
                        at(pe, x_ready, 10, c, 2 * (l - 1) + h + 1)
                    for n, j in enumerate((0, 1)):
                        p = 2 * h + j
                        if l < LEVELS - 1:
                            mm = T_.matmul(half_bank(2 + h)[:, n, :], x_t[:, v, p, :], q[:, p, :], start=True, stop=True)
                        else:
                            mm = T_.matmul(half_bank(2 + h)[:, n, :], q[:, p, :], x_t[:, v, p, :], start=True, stop=True)
                    mm.then_inc(xq_done, 1)

            def turn_x(c, v, l):
                for h in range(2):
                    at(pe, x_ready, 10, c, 2 * l + h + 1)
                    for n, j in enumerate((0, 1)):
                        mm = T_.transpose(half_bank(h)[:, n, :], x[:, 2 * h + j, :], ident)
                    mm.then_inc(xt_turned, 1)

            def main_w(c, v, pairs):
                if pairs[0] == 0:
                    at(pe, toks_ready, 3, c, 3)
                    at(pe, masked, MASKED, c, MASKED)
                    at(pe, m_ready, 1, c, 1)
                    done(pe, w_ready, 1, c)
                for j in pairs:
                    T_.matmul(bank(4)[:, j, :], grams[:, v, 0, j, :], toks[:, v, 2, j, :], start=True, stop=False)
                    mm = T_.matmul(bank(4)[:, j, :], R(v, ROLE_A, j), m[:, v, j, :], start=False, stop=True)
                if pairs[-1] == PAIRS - 1:
                    mm.then_inc(w_done, 1)

            def main_u(c, v):
                at(pe, x_ready, 10, c, 10)
                at(pe, w_ready, 1, c, 1)
                done(pe, y_flat, 2, c)
                for j in range(PAIRS):
                    mm = T_.matmul(bank(5)[:, j, :], x_t[:, v, j, :], w[:, j, :], start=True, stop=True)
                mm.then_inc(u_done, 1)

            def main_m(c, v, pairs):
                if pairs[0] == 0:
                    at(pe, u_ready, 1, c, 1)
                    done(pe, m_half, 1, c)
                for j in pairs:
                    T_.matmul(bank(6)[:, j, :], toks[:, v, 1, j, :], toks[:, v, 2, j, :], start=True, stop=False)
                    mm = T_.matmul(bank(6)[:, j, :], toks[:, v, 0, j, :], u[:, j, :], start=False, stop=True)
                if pairs[-1] == PAIRS - 1:
                    mm.then_inc(m_done, 1)

            def main_y(c, v, k, pairs):
                if pairs[0] == 0:
                    at(pe, u_ready, 1, c, 1)
                    pe.wait_ge(r_loaded[v], 32 * k + 32)
                    done(pe, y_ready, 2, c)
                for j in pairs:
                    T_.matmul(bank(7)[:, j, :], R(v, ROLE_R, j), m[:, v, j, :], start=True, stop=False)
                    T_.matmul(bank(7)[:, j, :], grams[:, v, 2, j, :], toks[:, v, 2, j, :], start=False, stop=False)
                    mm = T_.matmul(bank(7)[:, j, :], grams[:, v, 1, j, :], u[:, j, :], start=False, stop=True)
                if pairs[-1] == PAIRS - 1:
                    mm.then_inc(y_done, 1)

            def turn_y(c):
                at(pe, normed, 2, c, 2)
                at(pe, u_ready, 1, c, 2 if not isinstance(c, int) or c < NC_ - 1 else 1)
                if isinstance(c, int) and c == NC_ - 1:
                    at(pe, y_flat, 2, c, 2)
                for j in range(PAIRS):
                    mm = T_.transpose(bank(5)[:, j, :], y_bd[:, j].rearrange("p h c -> p (h c)"), ident)
                mm.then_inc(y_turned, 1)

            def step(c, v, k, pre, main):
                n, o = c + 1, 1 - v
                if pre:
                    grams_of(n, o, k)
                    turn_toks(n, o)
                if main:
                    main_u(c, v)
                if pre:
                    turn_x1(n, o)
                    if main:
                        main_m(c, v, (0, 1, 2, 3))
                    ys, ws = (lambda *pairs: main and main_y(c, v, k - v, pairs)), (lambda *pairs: main_w(n, o, pairs))
                    between = {(0, 0): (ys, (0,)), (1, 0): (ys, (1,)), (1, 2): (ys, (2,)), (2, 0): (ys, (3,)),
                               (2, 1): (ws, (0,)), (2, 2): (ws, (1,)), (3, 0): (ws, (2,)), (3, 1): (ws, (3,))}
                    for l in range(LEVELS):
                        for n_step, chain in enumerate((lx, xq, turn_x)):
                            if l < LEVELS - 1 or chain is not turn_x:
                                chain(n, o, l)
                            if (l, n_step) in between:
                                product, pairs = between[l, n_step]
                                product(*pairs)
                            if (l, n_step) == (LEVELS - 1, 0) and main and not (isinstance(c, int) and c == 0):
                                turn_y(c - 1)
                else:
                    main_y(c, v, k, (0, 1, 2, 3))
                    turn_y(c - 1)
                    turn_y(c)

            pe.wait_ge(masks_loaded, 16)
            steps(pe, step)

        @block.vector
        def _(dve):
            V = nc.vector
            V.memset(m[:], 0.0).then_inc(m_ready, 1)
            V.memset(y_bd[:], 0.0).then_inc(eps_set, 1)
            V.memset(eps[:], GN_EPS).then_inc(eps_set, 1)
            for v in range(2):
                V.memset(roles[:, v].rearrange("p b c d e -> p (b c d e)"), 0.0).then_inc(cleared, 1)
                V.memset(pairs_ar[:, v].rearrange("p b c d -> p (b c d)"), 0.0).then_inc(cleared, 1)
            V.memset(l_t[:], 0.0).then_inc(grams_cleared, 1)
            V.memset(grams[:].rearrange("p a b c d -> p (a b c d)"), 0.0).then_inc(grams_cleared, 1)
            dve.wait_ge(grams_cleared, 2)
            dve.wait_ge(masks_loaded, 16)
            dve.wait_ge(eps_set, 2)

            def mask_grams(c, v):
                at(dve, grams_done, 2, c, 1)
                if not (isinstance(c, int) and c < 2):
                    dve.wait_ge(y_done, c - 1)
                product = lambda n, q: bank(n)[:, :, q * S:(q + 1) * S]
                mask_of = lambda mk, h: masks[:, mk, h * S:(h + 1) * S]

                def mask_product(dst, n, q, mk):
                    for h in range(2):
                        rows = slice(h * 64, (h + 1) * 64)
                        V.tensor_tensor(dst[rows, :, h * S:(h + 1) * S], product(n, q)[rows],
                                        mask_of(mk, h)[rows].unsqueeze(1).broadcast_to([64, PAIRS, S]), ALU.mult).then_inc(masked, 1)
                mask_product(l_t[:], 0, 0, 0)
                at(dve, masked, MASKED, c, 2)
                V.tensor_tensor(q[:], l_t[:], wide(2, PAIRS), ALU.mult).then_inc(q_init, 1)
                at(dve, q_init, 1, c, 1)
                V.tensor_tensor(x_t[:, v], q[:], ident.unsqueeze(1).broadcast_to([P, PAIRS, P]), ALU.add).then_inc(masked, 1)
                mask_product(grams[:, v, 1], 0, 1, 1)
                at(dve, grams_done, 2, c, 2)
                mask_product(grams[:, v, 0], 1, 0, 0)
                mask_product(grams[:, v, 2], 1, 1, 1)

            def level(c, v, l):
                for h, js in enumerate(HALVES):
                    at(dve, lx_done, 10, c, 2 * l + h + 1)
                    V.tensor_tensor(q[:, js, :], half_bank(h), wide(3 + l, 2), ALU.mult).then_inc(q_ready, 1)
                for h, js in enumerate(HALVES):
                    at(dve, xq_done, 10, c, 2 * l + h + 1)
                    if l < LEVELS - 1:
                        V.tensor_tensor(x[:, js, :], x[:, js, :], half_bank(2 + h), ALU.add).then_inc(x_ready, 1)
                    else:
                        V.tensor_tensor(x_t[:, v, js, :], x_t[:, v, js, :], half_bank(2 + h), ALU.add).then_inc(x_ready, 1)

            def state(c, v):
                at(dve, m_done, 1, c, 1)
                done(dve, y_done, 1, c)
                V.tensor_tensor(m[:, 1 - v], m[:, v], bank(6), ALU.add).then_inc(m_half, 1)
                at(dve, m_half, 1, c, 1)
                V.tensor_tensor(m[:, 1 - v], m[:, 1 - v], chunk_decay[:, :, bass.ds(c, 1)].broadcast_to([P, PAIRS, P]), ALU.mult).then_inc(m_ready, 1)

            OWN = 5
            wide_stat = lambda n: stat[:, n, :].unsqueeze(2).broadcast_to([P, PAIRS, HEAD_DIM])

            def norm_mean(c):
                at(dve, y_ready, 2, c, 2)
                V.tensor_reduce(stat[:, 0, :], y[:], mybir.AxisListType.X, ALU.add).then_inc(norm_own, 1)
                at(dve, norm_own, OWN, c, 1)
                V.tensor_scalar(stat[:, 0, :], stat[:, 0, :], 1.0 / HEAD_DIM, None, ALU.mult).then_inc(norm_own, 1)
                at(dve, norm_own, OWN, c, 2)
                V.tensor_tensor(y[:], y[:], wide_stat(0), ALU.subtract).then_inc(norm_own, 1)

            def norm_squares(c):
                at(dve, sq_ready, 1, c, 1)
                V.tensor_reduce(stat[:, 1, :], y_sq[:], mybir.AxisListType.X, ALU.add).then_inc(norm_own, 1)

            def norm_divide(c):
                at(dve, std_done, 1, c, 1)
                V.reciprocal(stat[:, 3, :], stat[:, 2, :]).then_inc(norm_own, 1)
                at(dve, norm_own, OWN, c, 5)
                at(dve, y_turned, 1, c, 1)
                for h in range(2):
                    rows = slice(h * 64, (h + 1) * 64)
                    V.tensor_tensor(y_bd[rows, :, h, :], y[rows], wide_stat(3)[rows], ALU.mult).then_inc(normed, 1)

            def step(c, v, k, pre, main):
                n, o = c + 1, 1 - v
                norms = []
                if main and not (isinstance(c, int) and c == 0):
                    norms = [norm_mean, norm_squares, norm_divide]
                if pre:
                    mask_grams(n, o)
                    for l in range(LEVELS):
                        if l == 0 and main:
                            state(c, v)
                        level(n, o, l)
                        if 1 <= l <= 3 and norms:
                            norms[l - 1](c - 1)
                else:
                    for at_chunk in (c - 1, c):
                        for norm in norms:
                            norm(at_chunk)
            steps(dve, step)
            for j in range(PAIRS):
                out = y_all[:, j, NC_ * S - T:]
                dve.wait_ge(post_gained, j + 1)
                dve.wait_ge(post_loaded[2 * (j % 2)], 16 * (j // 2) + 16)
                V.tensor_tensor(out, out, post[:, j % 2, 0, :], ALU.add).then_inc(post_own, 1)
                dve.wait_ge(post_own, 2 * j + 1)
                dve.wait_ge(post_loaded[2 * (j % 2) + 1], 16 * (j // 2) + 16)
                V.tensor_tensor(out, out, post[:, j % 2, 1, :], ALU.mult).then_inc(post_own, 1)

        @block.scalar
        def _(act):
            A = nc.scalar
            A.preload_act_table(ACT.Sqrt)
            act.wait_ge(eps_set, 2)

            def toks_out(c, v):
                for n, (_, b, place) in enumerate(TOKS):
                    at(act, toks_done, 3, c, n + 1)
                    A.activation(toks[:, v, place], bank(b), ACT.Copy).then_inc(toks_ready, 1)

            def x1_out(c):
                at(act, x1_turned, 1, c, 1)
                A.activation(x[:], bank(0), ACT.Copy).then_inc(x1_ready, 1)

            def level(c, v, l):
                for h, js in enumerate(HALVES):
                    at(act, xt_turned, 8, c, 2 * l + h + 1)
                    A.activation(x_t[:, v, js, :], half_bank(h), ACT.Copy).then_inc(xt_ready, 1)

            def w_out(c):
                at(act, w_done, 1, c, 1)
                A.activation(w[:], bank(4), ACT.Copy).then_inc(w_ready, 1)

            def u_out(c):
                at(act, u_done, 1, c, 1)
                done(act, y_done, 1, c)
                A.activation(u[:], bank(5), ACT.Copy).then_inc(u_ready, 1)

            def y_out_of(c):
                at(act, y_done, 1, c, 1)
                done(act, normed, 2, c)
                for h in range(2):
                    rows = slice(h * 64, (h + 1) * 64)
                    A.activation(y[rows], bank(7)[rows, :, h * 64:(h + 1) * 64], ACT.Copy).then_inc(y_ready, 1)

            def squares(c):
                at(act, norm_own, 5, c, 3)
                A.activation(y_sq[:], y[:], ACT.Square).then_inc(sq_ready, 1)

            def deviation(c):
                at(act, norm_own, 5, c, 4)
                A.activation(stat[:, 2, :], stat[:, 1, :], ACT.Sqrt, scale=1.0 / HEAD_DIM, bias=eps[:]).then_inc(std_done, 1)

            def y_flat_out(c):
                at(act, y_turned, 1, c, 2)
                for h in range(2):
                    rows = slice(h * 64, (h + 1) * 64)
                    A.activation(y_all[rows, :, bass.ds(c * S, S)], bank(5)[rows, :, h * 64:(h + 1) * 64], ACT.Copy).then_inc(y_flat, 1)
            act.sem_inc(y_flat, 2)
            act.sem_inc(y_turned, 1)

            def step(c, v, k, pre, main):
                n, o = c + 1, 1 - v
                norm = main and not (isinstance(c, int) and c == 0)
                if pre:
                    done(act, y_done, 1, c)
                    toks_out(n, o)
                if main:
                    u_out(c)
                if pre:
                    x1_out(n)
                    level(n, o, 0)
                    level(n, o, 1)
                    if norm:
                        squares(c - 1)
                    level(n, o, 2)
                    if norm:
                        deviation(c - 1)
                    level(n, o, 3)
                    if main:
                        y_out_of(c)
                    w_out(n)
                    if norm:
                        y_flat_out(c - 1)
                else:
                    squares(c - 1)
                    deviation(c - 1)
                    y_out_of(c)
                    y_flat_out(c - 1)
                    squares(c)
                    deviation(c)
                    y_flat_out(c)
            steps(act, step)
            act.wait_ge(y_flat, 2 * NC_ + 2)
            for j in range(PAIRS):
                out = y_all[:, j, NC_ * S - T:]
                A.activation(out, out, ACT.Identity, scale=cols[:, COL["ln_g"] + j:COL["ln_g"] + j + 1], bias=cols[:, COL["ln_b"] + j:COL["ln_b"] + j + 1]).then_inc(post_gained, 1)


def branch_mix(nc, name, sems, psum, ya_dram, yb_dram, w_tiles, gates, mix_out):
    act_loaded, act_split_hi, act_split_lo, weight_loaded, split_hi, split_lo, products_done, sig_ready, mul_done, \
        za_used, mixed_ready, gates_loaded, stored = sems(name, [
            ("act_loaded", 2), "act_split_hi", "act_split_lo", "weight_loaded", "split_hi", "split_lo", "products_done",
            "sig_ready", "mul_done", "za_used", "mixed_ready", ("gates_loaded", 2), ("stored", 2)])
    with ExitStack() as ctx:
        sb = lambda n, shape, dt: ctx.enter_context(nc.sbuf_tensor(f"{name}_{n}", shape, dt))
        y_hi = sb("y_hi", [P, 2, K4, T], F32R)
        y_lo = sb("y_lo", [P, 2, K4, T], F32R)
        weight = sb("weight", [P, 3, K4, P], F32)
        w_hi = sb("w_hi", [P, SLOTS, 3, K4, P], F32R)
        w_lo = sb("w_lo", [P, SLOTS, 3, K4, P], F32R)
        sig = sb("sig", [P, SLOTS, N_TOK], F32)
        term = sb("term", [P, SLOTS, N_TOK], F32)
        gate = sb("gate", [P, 2, T], F32)
        mixed = sb("mixed", [P, SLOTS, T], F32)
        raw_a = sb("raw_a", [P, K4, N_TOK], F32)
        raw = (mixed[:, 1, 0:K4 * N_TOK].rearrange("p (k t) -> p k t", k=K4), raw_a[:])
        block = ctx.enter_context(nc.Block())
        LAST = KD // 2 - 1

        def tile_loop(eng, body, first=0):
            with eng.Fori(first, LAST) as i:
                for u in range(SLOTS):
                    body(2 * i + u, i, u)
            for u in range(SLOTS):
                body(2 * LAST + u, LAST, u)

        def bank(n, j):
            return (3 * n + j) % 6

        @block.sync
        def _(sp):
            for u in range(SLOTS):
                sp.sem_inc(stored[u], 16)
            def load_activations(n):
                for b, src in enumerate((yb_dram, ya_dram)):
                    if n:
                        sp.wait_ge(act_split_lo, 2 * n - 1 + b)
                    sp.dma_start(raw[b], src[:, :, n * N_TOK:(n + 1) * N_TOK].rearrange("k p t -> p k t")).then_inc(act_loaded[b], 16)

            def load_gates(m, h):
                cols = slice(h * (T // 2), (h + 1) * (T // 2))
                sp.wait_ge(mixed_ready, m * N_BLOCKS + (h + 1) * (N_BLOCKS // 2))
                for q in range(2):
                    sp.dma_start(gate[:, q, cols], gates[bass.ds(m + q * KD, 1), :, cols].rearrange("o p t -> p (o t)")).then_inc(gates_loaded[h], 16)

            def load_weights(m):
                sp.wait_ge(split_lo, m)
                sp.dma_start(weight[:], w_tiles[bass.ds(m, 1)].rearrange("o p a k c -> p (o a k) c")).then_inc(weight_loaded, 16)

            def store(m, u):
                sp.wait_ge(mixed_ready, m * N_BLOCKS + 2 * N_BLOCKS)
                sp.dma_start(mix_out[bass.ds(m, 1)].rearrange("o p t -> p (o t)"), mixed[:, u, :]).then_inc(stored[u], 16)
            sp.dma_start(weight[:], w_tiles[0:1].rearrange("o p a k c -> p (o a k) c")).then_inc(weight_loaded, 16)
            load_activations(0)
            load_gates(0, 0)
            for n in range(1, N_BLOCKS):
                load_activations(n)
                if n == 1:
                    load_gates(0, 1)
                    load_weights(1)
            with sp.Fori(0, KD // 2 - 1) as i:
                for u in range(SLOTS):
                    m = 2 * i + u
                    load_gates(m + 1, 0)
                    load_weights(m + 2)
                    load_gates(m + 1, 1)
                    store(m, u)
            load_gates(KD - 1, 0)
            load_gates(KD - 1, 1)
            for u in range(SLOTS):
                store(KD - 2 + u, u)
            for u in range(SLOTS):
                sp.wait_ge(stored[u], 16 * KD // 2 + 16)

        @block.tensor
        def _(pe):
            pe.sem_inc(products_done, SLOTS * 3 * N_BLOCKS)

            def tile(m, i, u):
                pe.wait_ge(split_hi, m + 1)
                pe.wait_ge(split_lo, m + 1)
                for n in range(N_BLOCKS):
                    for j in range(3):
                        part = 2 - j
                        b = bank(n, j)
                        if j == 0:
                            pe.wait_ge(sig_ready, m * N_BLOCKS + n + 1)
                        elif j == 1:
                            pe.wait_ge(za_used, m * N_BLOCKS + n + 1)
                        else:
                            pe.wait_ge(mul_done, 2 * (m * N_BLOCKS + n + 1))
                        pe.wait_ge(act_split_lo, 2 * n + (2 if part == 0 else 1))
                        for k in range(K4):
                            src = 0 if part == 0 else 1
                            cols = slice(n * N_TOK, (n + 1) * N_TOK)
                            for w, y in ((w_hi, y_hi), (w_hi, y_lo), (w_lo, y_hi)):
                                mm = nc.tensor.matmul(psum[:, b, 0:N_TOK], w[:, u, part, k, :], y[:, src, k, cols],
                                                      start=(k == 0 and w is w_hi and y is y_hi), stop=(k == K4 - 1 and w is w_lo))
                        mm.then_inc(products_done, 1)
            tile_loop(pe, tile)

        @block.scalar
        def _(act):
            act.sem_inc(sig_ready, SLOTS)

            def split(m, u):
                if isinstance(m, int) and m >= KD:
                    return
                act.wait_ge(weight_loaded, 16 * m + 16)
                act.wait_ge(products_done, (m + 1) * 3 * N_BLOCKS)
                nc.scalar.activation(w_hi[:, u], weight[:], ACT.Copy).then_inc(split_hi, 1)
            split(0, 0)

            def split_activations(n):
                for b in range(2):
                    act.wait_ge(act_loaded[b], 16 * n + 16)
                    nc.scalar.activation(y_hi[:, 1 - b, :, n * N_TOK:(n + 1) * N_TOK], raw[b], ACT.Copy).then_inc(act_split_hi, 1)
            split_activations(0)

            def tile(m, i, u):
                split(m + 1, 1 - u)
                for n in range(N_BLOCKS):
                    if isinstance(m, int) and m == 0 and n + 1 < N_BLOCKS:
                        split_activations(n + 1)
                    act.wait_ge(products_done, ((m + SLOTS) * N_BLOCKS + n) * 3 + 1)
                    act.wait_ge(za_used, m * N_BLOCKS + n + 1)
                    nc.scalar.activation(sig[:, n % 2, :], psum[:, bank(n, 0), 0:N_TOK], ACT.Sigmoid).then_inc(sig_ready, 1)
            for u in range(SLOTS):
                tile(u, 0, u)
            tile_loop(act, tile, 1)

        @block.vector
        def _(dve):
            dve.sem_inc(za_used, SLOTS)
            dve.sem_inc(mul_done, 2 * SLOTS)
            dve.sem_inc(mixed_ready, N_BLOCKS)

            def split(m, u):
                if isinstance(m, int) and m >= KD:
                    return
                dve.wait_ge(split_hi, m + 1)
                nc.vector.tensor_tensor(w_lo[:, u], weight[:], w_hi[:, u].bitcast(F32), ALU.subtract).then_inc(split_lo, 1)
            split(0, 0)

            def split_activations(n):
                for b in range(2):
                    cols = slice(n * N_TOK, (n + 1) * N_TOK)
                    dve.wait_ge(act_split_hi, 2 * n + b + 1)
                    nc.vector.tensor_tensor(y_lo[:, 1 - b, :, cols], raw[b], y_hi[:, 1 - b, :, cols].bitcast(F32), ALU.subtract).then_inc(act_split_lo, 1)
            split_activations(0)

            def tile(m, i, u):
                split(m + 1, 1 - u)
                dve.wait_ge(stored[u], 16 * i + 16)
                for n in range(N_BLOCKS):
                    cols = slice(n * N_TOK, (n + 1) * N_TOK)
                    q = m * N_BLOCKS + n
                    if isinstance(m, int) and m == 0 and n + 1 < N_BLOCKS:
                        split_activations(n + 1)
                    dve.wait_ge(gates_loaded[n // (N_BLOCKS // 2)], 32 * m + 32)
                    dve.wait_ge(products_done, ((m + SLOTS) * N_BLOCKS + n) * 3 + 2)
                    dve.wait_ge(sig_ready, q + 1 + SLOTS)
                    nc.vector.tensor_tensor(term[:, n % 2, :], psum[:, bank(n, 1), 0:N_TOK], sig[:, n % 2, :], ALU.mult).then_inc(za_used, 1)
                    dve.wait_ge(za_used, q + 1 + SLOTS)
                    nc.vector.tensor_tensor(term[:, n % 2, :], term[:, n % 2, :], gate[:, 1, cols], ALU.mult).then_inc(mul_done, 1)
                    dve.wait_ge(products_done, ((m + SLOTS) * N_BLOCKS + n) * 3 + 3)
                    nc.vector.tensor_tensor(mixed[:, u, cols], psum[:, bank(n, 2), 0:N_TOK], gate[:, 0, cols], ALU.mult).then_inc(mul_done, 1)
                    dve.wait_ge(mul_done, 2 * (q + 1 + SLOTS))
                    nc.vector.tensor_tensor(mixed[:, u, cols], mixed[:, u, cols], term[:, n % 2, :], ALU.add).then_inc(mixed_ready, 1)
            for u in range(SLOTS):
                tile(u, 0, u)
            tile_loop(dve, tile, 1)


def token_projection(nc, name, sems, psum, acts, first_col, w_dram, k_tiles, passes, gain, residual, out, out_first, meta_tile, next_norm=None):
    TILES = SEQ // P
    LAST = TILES // 2 - 1
    HALF = D_MODEL // 2
    RAW = 3
    assert passes <= 2 and not ((meta_tile or next_norm) and passes > 1)
    weight_loaded, w_hi_done, w_lo_done, k_done, acts_loaded, acts_hi, acts_lo, evacuated, rows_loaded, summed, \
        squares_done, std_ready, rstd_ready, scaled, finished, stored, gain_loaded, eps_ready = sems(name, [
            ("weight_loaded", RAW), "w_hi_done", "w_lo_done", "k_done", "acts_loaded", "acts_hi", "acts_lo",
            "evacuated", ("rows_loaded", 2), "summed", "squares_done", "std_ready", "rstd_ready", "scaled", "finished",
            ("stored", 2), "gain_loaded", "eps_ready"])
    row_squares_done, row_std_ready, row_rstd_ready, row_normed, turned, turned_out = sems(name + "_next", [
        "row_squares_done", "row_std_ready", "row_rstd_ready", "row_normed", "turned", "turned_out"])
    with ExitStack() as ctx:
        sb = lambda n, shape, dt: ctx.enter_context(nc.sbuf_tensor(f"{name}_{n}", shape, dt))
        w_hi = sb("w_hi", [P, k_tiles, D_MODEL], F32R)
        w_lo = sb("w_lo", [P, k_tiles, D_MODEL], F32R)
        w_raw = sb("w_raw", [P, RAW, D_MODEL], F32)
        a_raw = sb("a_raw", [P, k_tiles, P], F32)
        a_hi = sb("a_hi", [P, SLOTS, k_tiles, P], F32R)
        a_lo = sb("a_lo", [P, SLOTS, k_tiles, P], F32R)
        rows = sb("rows", [P, SLOTS, D_MODEL], F32)
        squares = sb("squares", [P, D_MODEL], BF16)
        stat = sb("stat", [P, SLOTS, 3], F32)
        eps = sb("eps", [P, 1], F32)
        gains = sb("gains", [P, D_MODEL], F32)
        sums = sb("sums", [P, TILES if passes > 1 else SLOTS, D_MODEL], F32)
        if next_norm:
            next_x, next_gain, ident = next_norm
            row_normed_buf = sb("row_normed_buf", [P, SLOTS, D_MODEL], F32)
            row_squares = sb("row_squares", [P, D_MODEL], BF16)
            row_stat = sb("row_stat", [P, SLOTS, 3], F32)
        block = ctx.enter_context(nc.Block())

        def tiles(eng, ahead, body, part, first=0):
            def args(i, u):
                r = 2 * i + u
                if isinstance(r, int) and r >= TILES:
                    return (part * TILES + TILES, TILES, 0, TILES // 2, N_META, -N_META) if meta_tile and r == TILES else None
                return (r + part * TILES, r, u, i, P, r * P)

            def step(i, u):
                after = args(i + u, 1 - u)
                if ahead and after:
                    ahead(*after)
                if body:
                    body(*args(i, u))
            for i in range(first):
                step(i, 0)
                step(i, 1)
            with eng.Fori(first, LAST) as i:
                step(i, 0)
                step(i, 1)
            step(LAST, 0)
            step(LAST, 1)
            if meta_tile and body:
                body(*args(LAST + 1, 0))

        def flat(ap):
            return ap.rearrange("p a b -> p (a b)")

        @block.sync
        def _(sp):
            for u in range(SLOTS):
                sp.sem_inc(stored[u], 16)

            def load_acts(part, r, n, token):
                sp.wait_ge(acts_lo, r + (part * TILES + 1))
                src = acts[part * k_tiles:(part + 1) * k_tiles, :, bass.ds(token + first_col, n)]
                sp.dma_start(a_raw[:, :, 0:n], src.rearrange("k p t -> p k t")).then_inc(acts_loaded, 16)

            def load_rows(r, u, n, token):
                sp.wait_ge(finished, r + 1)
                sp.dma_start(rows[0:n, u, :], residual[bass.ds(token + N_META, n), :]).then_inc(rows_loaded[u], 16)

            def store(r, u, n, token):
                sp.wait_ge(finished, r + (1 + SLOTS))
                total = flat(sums[:, bass.ds(r, 1), :]) if passes > 1 else sums[0:n, u, :]
                sp.dma_start(out[bass.ds(token + out_first, n), :], total).then_inc(stored[u], 16)

            def load_weights(first, last):
                for q in range(first, last):
                    if q >= RAW:
                        sp.wait_ge(w_lo_done, q - RAW + 1)
                    sp.dma_start(w_raw[:, q % RAW, :], w_dram[q]).then_inc(weight_loaded[q % RAW], 16)

            load_acts(0, 0, P, 0)
            load_weights(0, k_tiles)
            sp.dma_start(gains[:], gain).then_inc(gain_loaded, 16)
            if passes > 1:
                load_weights(k_tiles, k_tiles + RAW)
                with sp.Fori(1, TILES) as r:
                    load_acts(0, r, P, r * P)
                load_acts(1, 0, P, 0)
                load_weights(k_tiles + RAW, 2 * k_tiles)
            part = passes - 1
            load_rows(0, 0, P, 0)
            load_acts(part, 1, P, P)
            load_rows(1, 1, P, P)
            with sp.Fori(1, TILES // 2) as i:
                for u in range(SLOTS):
                    r = 2 * i + u
                    load_acts(part, r, P, r * P)
                    load_rows(r, u, P, r * P)
                    store(r - 2, u, P, (r - 2) * P)
            if meta_tile:
                load_acts(part, TILES, N_META, -N_META)
                load_rows(TILES, 0, N_META, -N_META)
            for u in range(SLOTS):
                store(TILES - 2 + u, u, P, (TILES - 2 + u) * P)
            if meta_tile:
                store(TILES, 0, N_META, -N_META)
            for u in range(SLOTS):
                sp.wait_ge(stored[u], 16 * (TILES // 2 + 1 + (meta_tile and u == 0)))

        @block.tensor
        def _(pe):
            pe.sem_inc(k_done, k_tiles)
            for part in range(passes):
                def products(s, r, u, i, n, token):
                    pe.wait_ge(acts_hi, s + 1)
                    pe.wait_ge(acts_lo, s + 2)
                    pe.wait_ge(evacuated, s + 1)
                    for k in range(k_tiles):
                        pe.wait_ge(w_lo_done, part * k_tiles + k + 1)
                        for h in range(2):
                            for a, w in ((a_hi, w_hi), (a_hi, w_lo), (a_lo, w_hi)):
                                mm = nc.tensor.matmul(psum[0:n, 2 * u + h, :], a[:, u, k, 0:n], w[:, k, h * HALF:(h + 1) * HALF],
                                                      start=(k == 0 and a is a_hi and w is w_hi), stop=(k == k_tiles - 1 and a is a_lo))
                        mm.then_inc(k_done, 1)
                def turn(s, r, u, i, n, token):
                    pe.wait_ge(row_normed, r + 1 + SLOTS)
                    pe.wait_ge(turned_out, r + 1)
                    for k in range(KD):
                        mm = nc.tensor.transpose(psum[:, 4 + 2 * u + k // 4, k % 4 * P:k % 4 * P + n], row_normed_buf[0:n, u, k * P:(k + 1) * P], ident[0:n, 0:n])
                    mm.then_inc(turned, 1)

                if next_norm:
                    pe.sem_inc(turned, SLOTS)
                    products(0, 0, 0, 0, P, 0)
                    tiles(pe, products, turn, part)
                else:
                    tiles(pe, None, products, part)

        @block.scalar
        def _(act):
            nc.scalar.preload_act_table(ACT.Sqrt)
            act.sem_inc(squares_done, 1)
            act.sem_inc(row_squares_done, 1)
            act.wait_ge(eps_ready, 1)
            for part in range(passes):
                def split(s, r, u, i, n, token):
                    act.wait_ge(acts_loaded, 16 * s + 16)
                    act.wait_ge(k_done, s * k_tiles if not isinstance(s, int) or s > 1 else k_tiles)
                    nc.scalar.activation(a_hi[:, u, :, 0:n], a_raw[:, :, 0:n], ACT.Copy).then_inc(acts_hi, 1)

                def finish(s, r, u, i, n, token):
                    banks = flat(psum[0:n, 2 * u:2 * u + 2, :])
                    if part < passes - 1:
                        act.wait_ge(k_done, (s + 2) * k_tiles)
                        nc.scalar.activation(flat(sums[:, bass.ds(r, 1), :]), banks, ACT.Copy).then_inc(evacuated, 1)
                        return
                    if passes > 1:
                        act.wait_ge(summed, r + 1)
                        total = flat(sums[:, bass.ds(r, 1), :])
                    else:
                        act.wait_ge(k_done, (s + 2) * k_tiles)
                        total = banks
                    act.wait_ge(scaled, r + 1)
                    act.wait_ge(squares_done, r + 1)
                    nc.scalar.activation(squares[0:n, :], total, ACT.Square, accum_out=stat[0:n, u, 0:1]).then_inc(squares_done, 1)
                    act.wait_ge(squares_done, r + 2)
                    nc.scalar.activation(stat[0:n, u, 1:2], stat[0:n, u, 0:1], ACT.Sqrt, scale=1.0 / D_MODEL, bias=eps[0:n]).then_inc(std_ready, 1)
                    if next_norm:
                        act.wait_ge(finished, r + (1 + SLOTS))
                        act.wait_ge(row_normed, r + 1)
                        act.wait_ge(row_squares_done, r + 1)
                        nc.scalar.activation(row_squares[0:n, :], sums[0:n, u, :], ACT.Square, accum_out=row_stat[0:n, u, 0:1]).then_inc(row_squares_done, 1)
                        act.wait_ge(row_squares_done, r + 2)
                        nc.scalar.activation(row_stat[0:n, u, 1:2], row_stat[0:n, u, 0:1], ACT.Sqrt, scale=1.0 / D_MODEL, bias=eps[0:n]).then_inc(row_std_ready, 1)

                split(part * TILES, 0, 0, 0, P, 0)
                for k in range(k_tiles):
                    q = part * k_tiles + k
                    act.wait_ge(weight_loaded[q % RAW], 16 * (q // RAW) + 16)
                    if part:
                        act.wait_ge(k_done, TILES * k_tiles + k + 1)
                    nc.scalar.activation(w_hi[:, k, :], w_raw[:, q % RAW, :], ACT.Copy).then_inc(w_hi_done, 1)
                tiles(act, split, finish, part)

        @block.vector
        def _(dve):
            nc.vector.memset(eps[:], RMS_EPS).then_inc(eps_ready, 1)
            dve.sem_inc(acts_lo, 1)
            dve.sem_inc(evacuated, SLOTS)
            dve.sem_inc(scaled, SLOTS)
            dve.sem_inc(finished, SLOTS)
            dve.sem_inc(row_normed, SLOTS)
            dve.sem_inc(turned_out, SLOTS)
            for part in range(passes):
                def split(s, r, u, i, n, token):
                    dve.wait_ge(acts_hi, s + 1)
                    nc.vector.tensor_tensor(a_lo[:, u, :, 0:n], a_raw[:, :, 0:n], a_hi[:, u, :, 0:n].bitcast(F32), ALU.subtract).then_inc(acts_lo, 1)

                def finish(s, r, u, i, n, token):
                    banks = flat(psum[0:n, 2 * u:2 * u + 2, :])
                    if passes > 1:
                        total = source = flat(sums[:, bass.ds(r, 1), :])
                        dve.wait_ge(k_done, (s + 2) * k_tiles)
                        nc.vector.tensor_tensor(total, total, banks, ALU.add).then_inc(summed, 1)
                        dve.wait_ge(summed, r + 1)
                        dve.sem_inc(evacuated, 1)
                    else:
                        total, source = sums[0:n, u, :], banks
                        dve.wait_ge(stored[u], 16 * i + 16)
                    dve.wait_ge(std_ready, r + 1)
                    nc.vector.reciprocal(stat[0:n, u, 2:3], stat[0:n, u, 1:2]).then_inc(rstd_ready, 1)
                    dve.wait_ge(rstd_ready, r + 1)
                    nc.vector.scalar_tensor_tensor(total, source, stat[0:n, u, 2:3], gains[0:n, :], ALU.mult, ALU.mult).then_inc(scaled, 1)
                    dve.wait_ge(scaled, r + (1 + SLOTS))
                    if passes == 1:
                        dve.sem_inc(evacuated, 1)
                    dve.wait_ge(rows_loaded[u], 16 * i + 16)
                    nc.vector.tensor_tensor(total, total, rows[0:n, u, :], ALU.add).then_inc(finished, 1)
                    if next_norm:
                        dve.wait_ge(row_std_ready, r + 1)
                        nc.vector.reciprocal(row_stat[0:n, u, 2:3], row_stat[0:n, u, 1:2]).then_inc(row_rstd_ready, 1)
                        dve.wait_ge(row_rstd_ready, r + 1)
                        dve.wait_ge(finished, r + (1 + SLOTS))
                        dve.wait_ge(turned, r + 1)
                        nc.vector.tensor_scalar(row_normed_buf[0:n, u, :], total, row_stat[0:n, u, 2:3], None, ALU.mult).then_inc(row_normed, 1)
                        if not isinstance(r, int) or r > 0:
                            channels_out(r - 1, 1 - u, P, (token - P) if n == P else SEQ - P)

                def channels_out(r, u, n, token):
                    dve.wait_ge(turned, r + 1 + SLOTS)
                    banks = psum[:, 4 + 2 * u:6 + 2 * u, :].rearrange("p b (k t) -> p b k t", t=P)[:, :, :, 0:n]
                    nc.vector.tensor_tensor(next_x[:, :, bass.ds(token + N_META, n)].rearrange("p (b k) t -> p b k t", b=2), banks,
                                            next_gain.rearrange("p (b k) -> p b k", b=2).unsqueeze(3).broadcast_to([P, 2, 4, n]), ALU.mult).then_inc(turned_out, 1)

                split(part * TILES, 0, 0, 0, P, 0)
                for k in range(k_tiles):
                    q = part * k_tiles + k
                    dve.wait_ge(w_hi_done, q + 1)
                    nc.vector.tensor_tensor(w_lo[:, k, :], w_raw[:, q % RAW, :], w_hi[:, k, :].bitcast(F32), ALU.subtract).then_inc(w_lo_done, 1)
                if part == passes - 1:
                    dve.wait_ge(gain_loaded, 16)
                tiles(dve, split, finish if part == passes - 1 else None, part, 1 if next_norm else 0)
                if next_norm:
                    channels_out(TILES, 0, N_META, -N_META)


def ffn_up(nc, name, sems, psum, x, x_hi, x_lo, w_tiles, conv_w, conv_b, hidden_out):
    weight_loaded, split_hi, split_lo, products_done, a_evacuated, conv_done, gelu_done, b_used, tap_done, stored = sems(name, [
        "weight_loaded", "split_hi", "split_lo", "products_done", "a_evacuated", "conv_done", "gelu_done", "b_used", "tap_done", ("stored", 2)])
    x_split_hi, x_split_lo = sems(name + "_x", ["x_split_hi", "x_split_lo"])
    with ExitStack() as ctx:
        sb = lambda n, shape, dt: ctx.enter_context(nc.sbuf_tensor(f"{name}_{n}", shape, dt))
        weight = sb("weight", [P, 2, KD, P], F32)
        w_hi = sb("w_hi", [P, SLOTS, 2, KD, P], F32R)
        w_lo = sb("w_lo", [P, SLOTS, 2, KD, P], F32R)
        a_pre = sb("a_pre", [P, T], F32)
        hidden = sb("hidden", [P, SLOTS, SEQ], F32)
        block = ctx.enter_context(nc.Block())
        GROUPS = 2 * N_BLOCKS
        LAST = M_FF // 2 - 1

        def tile_loop(eng, body):
            with eng.Fori(0, LAST) as i:
                for u in range(SLOTS):
                    body(2 * i + u, i, u)
            for u in range(SLOTS):
                body(2 * LAST + u, LAST, u)

        block_cols = lambda n: slice(n * N_TOK, (n + 1) * N_TOK)

        def bank(u, part, n):
            return (u * GROUPS + part * N_BLOCKS + n) % 8

        @block.sync
        def _(sp):
            def load(m):
                sp.wait_ge(split_lo, m + 1)
                sp.dma_start(weight[:], w_tiles[bass.ds(m, 1)].rearrange("o p a k c -> p (o a k) c")).then_inc(weight_loaded, 16)

            def store(m, u):
                sp.wait_ge(b_used, m * N_BLOCKS + 2 * N_BLOCKS)
                sp.dma_start(hidden_out[bass.ds(m, 1)].rearrange("o p t -> p (o t)"), hidden[:, u, :]).then_inc(stored[u], 16)
            for u in range(SLOTS):
                sp.sem_inc(stored[u], 16)
            for u in range(SLOTS):
                load(u)
            with sp.Fori(1, M_FF // 2) as i:
                for u in range(SLOTS):
                    load(2 * i + u)
                    store(2 * i - 2 + u, u)
            for u in range(SLOTS):
                store(2 * LAST + u, u)
            for u in range(SLOTS):
                sp.wait_ge(stored[u], 16 * M_FF // 2 + 16)

        @block.tensor
        def _(pe):
            pe.sem_inc(products_done, SLOTS * GROUPS)

            def tile(m, i, u):
                pe.wait_ge(split_hi, m + 1)
                pe.wait_ge(split_lo, m + 2)
                for part in range(2):
                    for n in range(N_BLOCKS):
                        before = part * N_BLOCKS + n - 8
                        if before >= N_BLOCKS:
                            pe.wait_ge(b_used, m * N_BLOCKS + before - N_BLOCKS + 1 + N_BLOCKS)
                        elif before >= 0:
                            pe.wait_ge(a_evacuated, m * N_BLOCKS + before + 1 + N_BLOCKS)
                        elif before + GROUPS >= N_BLOCKS:
                            pe.wait_ge(b_used, m * N_BLOCKS + before + N_BLOCKS + 1)
                        else:
                            pe.wait_ge(a_evacuated, m * N_BLOCKS + before + GROUPS + 1)
                        pe.wait_ge(x_split_lo, n + 1)
                        for k in range(KD):
                            for w, y in ((w_hi, x_hi), (w_hi, x_lo), (w_lo, x_hi)):
                                mm = nc.tensor.matmul(psum[:, bank(u, part, n), 0:N_TOK], w[:, u, part, k, :],
                                                      y[:, k, block_cols(n)],
                                                      start=(k == 0 and w is w_hi and y is x_hi), stop=(k == KD - 1 and w is w_lo))
                        mm.then_inc(products_done, 1)
            tile_loop(pe, tile)

        @block.scalar
        def _(act):
            act.sem_inc(a_evacuated, N_BLOCKS)

            def split(m, i, u):
                if isinstance(i, int) and i > LAST:
                    return
                act.wait_ge(weight_loaded, 16 * m + 16)
                act.wait_ge(products_done, (m + 1) * GROUPS)
                nc.scalar.activation(w_hi[:, u], weight[:], ACT.Copy).then_inc(split_hi, 1)

            def split_x(n):
                nc.scalar.activation(x_hi[:, :, block_cols(n)], x[:, :, block_cols(n)], ACT.Copy).then_inc(x_split_hi, 1)
            for n in range(N_BLOCKS):
                if n == N_BLOCKS // 2:
                    split(0, 0, 0)
                split_x(n)

            def tile(m, i, u):
                split(m + 1, i + u, 1 - u)
                act.wait_ge(conv_done, m + 1)
                for n in range(N_BLOCKS):
                    act.wait_ge(products_done, (m + SLOTS) * GROUPS + n + 1)
                    nc.scalar.activation(a_pre[:, n * N_TOK:(n + 1) * N_TOK], psum[:, bank(u, 0, n), 0:N_TOK], ACT.Copy).then_inc(a_evacuated, 1)
                act.wait_ge(conv_done, m + 2)
                nc.scalar.activation(hidden[:, u, :], hidden[:, u, :], ACT.Gelu_apprx_tanh).then_inc(gelu_done, 1)
            tile_loop(act, tile)

        @block.vector
        def _(dve):
            dve.sem_inc(split_lo, 1)
            dve.sem_inc(conv_done, 1)
            dve.sem_inc(b_used, N_BLOCKS)

            def split(m, i, u):
                if isinstance(i, int) and i > LAST:
                    return
                dve.wait_ge(split_hi, m + 1)
                nc.vector.tensor_tensor(w_lo[:, u], weight[:], w_hi[:, u].bitcast(F32), ALU.subtract).then_inc(split_lo, 1)

            def split_x(n):
                dve.wait_ge(x_split_hi, n + 1)
                nc.vector.tensor_tensor(x_lo[:, :, block_cols(n)], x[:, :, block_cols(n)], x_hi[:, :, block_cols(n)].bitcast(F32), ALU.subtract).then_inc(x_split_lo, 1)
            for n in range(N_BLOCKS):
                if n == N_BLOCKS // 2:
                    split(0, 0, 0)
                split_x(n)

            def tile(m, i, u):
                split(m + 1, i + u, 1 - u)
                dve.wait_ge(a_evacuated, (m + 2) * N_BLOCKS)
                dve.wait_ge(stored[u], 16 * i + 16)
                out = hidden[:, u, :]
                tap = lambda j: a_pre[:, N_META - 2 + j:N_META - 2 + j + SEQ]
                weight_of = lambda j: conv_w[:, bass.ds(m + j * M_FF, 1)]
                nc.vector.tensor_scalar(out, tap(2), weight_of(2), conv_b[:, bass.ds(m, 1)], ALU.mult, ALU.add).then_inc(tap_done, 1)
                dve.wait_ge(tap_done, 2 * m + 1)
                nc.vector.scalar_tensor_tensor(out, tap(1), weight_of(1), out, ALU.mult, ALU.add).then_inc(tap_done, 1)
                dve.wait_ge(tap_done, 2 * m + 2)
                nc.vector.scalar_tensor_tensor(out, tap(0), weight_of(0), out, ALU.mult, ALU.add).then_inc(conv_done, 1)
                dve.wait_ge(gelu_done, m + 1)
                for n in range(N_BLOCKS):
                    skip = N_META if n == 0 else 0
                    cols = hidden[:, u, n * N_TOK - N_META + skip:(n + 1) * N_TOK - N_META]
                    dve.wait_ge(products_done, (m + SLOTS) * GROUPS + N_BLOCKS + n + 1)
                    nc.vector.tensor_tensor(cols, cols, psum[:, bank(u, 1, n), skip:N_TOK], ALU.mult).then_inc(b_used, 1)
            tile_loop(dve, tile)


def hybrid_block(nc, ins, out):
    dram = lambda name, shape: nc.dram_tensor("scratch_" + name, shape, F32).ap()
    rwkv_proj = dram("rwkv_proj", [M_RWKV, P, T])
    gates = dram("gates", [M_GATE, P, T])
    s5_u = dram("s5_u", [P, S5_GROUPS, S5_CHUNKS])
    roles = dram("roles", [4, PAIRS, P, T])
    bonus = dram("bonus", [PAIRS, P, T])
    rwkv_gate = dram("rwkv_gate", [PAIRS, P, T])
    rwkv_y = dram("rwkv_y", [K4, P, T])
    s5_y = dram("s5_y", [K4, P, T])
    mixed = dram("mixed", [KD, P, T])
    h1 = dram("h1", [T, D_MODEL])
    hidden = dram("hidden", [M_FF, P, SEQ])

    with ExitStack() as ctx:
        in_use = []

        def sems(prefix, names):
            def new(n):
                in_use.append(nc.alloc_semaphore(f"{prefix}_{n}"))
                return in_use[-1]
            return [new(n) if isinstance(n, str) else [new(f"{n[0]}{j}") for j in range(n[1])] for n in names]

        def stage_ends():
            nc.clear_and_free_semaphores(in_use)
            in_use.clear()
            nc.all_engine_barrier()

        psum = ctx.enter_context(nc.psum_tensor("psum", [P, 8, 512], F32))
        cols_t = ctx.enter_context(nc.sbuf_tensor("cols_sb", [P, N_COLS], F32))
        ident_t = ctx.enter_context(nc.sbuf_tensor("ident_sb", [P, P], F32))
        decay_t = ctx.enter_context(nc.sbuf_tensor("chunk_decay", [P, PAIRS, CHUNKS], F32))
        cols, ident, decay = cols_t[:], ident_t[:], decay_t[:]
        consts_loaded, = sems("main", ["consts_loaded"])
        with nc.Block() as block:
            @block.sync
            def _(sp):
                sp.dma_start(cols, ins["columns"]).then_inc(consts_loaded, 16)
                sp.dma_start(ident, ins["identity"]).then_inc(consts_loaded, 16)
                sp.wait_ge(consts_loaded, 32)

        def normed_part(name, stack):
            return stack.enter_context(nc.sbuf_tensor(name, [P, KD, T], F32R))

        with ExitStack() as inner:
            x_hi, x_lo = normed_part("x_hi", inner), normed_part("x_lo", inner)
            norm_transpose(nc, "pre", sems, psum, ins["h0"], x_hi, x_lo, cols[:, COL["mix_pre"]:COL["mix_pre"] + KD], ident)
            in_projection(nc, "proj", sems, psum, x_hi, x_lo, ins["w_in_tiles"], cols[:, COL["mu"]:COL["mu"] + M_RWKV], rwkv_proj, gates)
            s5_inputs(nc, "s5in", sems, psum, x_hi, x_lo, ins["w_in_s5"], s5_u, ident)
        stage_ends()
        rwkv_prepare(nc, "prep", sems, psum, rwkv_proj, ins["lora"], cols, roles, bonus, rwkv_gate, decay)
        rwkv_chunks(nc, "chunk", sems, psum, roles, rwkv_proj[2 * PAIRS:3 * PAIRS], decay, ins["chunk_masks"], bonus, rwkv_gate, cols, rwkv_y, ident)
        stage_ends()
        s5_scan(nc, "s5", sems, psum, ins, s5_u, s5_y, ident)
        branch_mix(nc, "mix", sems, psum, rwkv_y, s5_y, ins["w_mix_tiles"], gates, mixed)
        with ExitStack() as inner:
            h_normed = inner.enter_context(nc.sbuf_tensor("h_normed", [P, KD, T], F32))[:]
            token_projection(nc, "mixout", sems, psum, mixed, N_META, ins["w_out"], KD, 1, ins["mix_post"], ins["h0"], h1, N_META, True,
                             (h_normed, cols[:, COL["ffn_pre"]:COL["ffn_pre"] + KD], ident))
            stage_ends()
        with ExitStack() as inner:
            h_lo, h_hi = normed_part("h_lo", inner), normed_part("h_hi", inner)
            ffn_up(nc, "up", sems, psum, h_normed, h_hi, h_lo, ins["w_up_tiles"], cols[:, COL["conv_w"]:COL["conv_w"] + CONV_W * M_FF],
                   cols[:, COL["conv_b"]:COL["conv_b"] + M_FF], hidden)
        token_projection(nc, "down", sems, psum, hidden, 0, ins["w_down"], M_FF // 2, 2, ins["ffn_post"], h1, out, 0, False)
        stage_ends()


def lay_out(np, i):
    i = {name: np.asarray(a) for name, a in i.items()}
    one = {name: a[0] for name, a in i.items() if name != "meta_tokens"}
    channels = lambda a: a.reshape(-1, P).T

    def k_tiles(w, width):
        k, m = w.shape
        return w.reshape(k // P, P, m // width, width).transpose(2, 1, 0, 3)

    columns = {"mu": "rwkv_shift_mu", "w0": "rwkv_w0", "a0": "rwkv_a0", "k_k": "rwkv_k_k", "k_a": "rwkv_k_a", "r_k": "rwkv_r_k",
               "ln_g": "rwkv_ln_gain", "ln_b": "rwkv_ln_bias", "mix_pre": "norm_mix_pre", "ffn_pre": "norm_ffn_pre",
               "conv_w": "ffn_conv_w", "conv_b": "ffn_conv_b"}
    w_in = one["w_in"]
    s5_at = RWKV_PROJ
    gates_at = s5_at + D_MODEL // 2
    glu, up = one["s5_w_glu"], one["ffn_w_up"]
    twice = lambda a: np.concatenate([a, a], axis=0)
    rows = lambda a: np.broadcast_to(a[None], (P, *a.shape))
    index = np.arange(P)
    head, token = index // CHUNK, index % CHUNK
    same = head[:, None] == head[None, :]
    r, c = token[:, None], token[None, :]
    masks = [same & (r < c), same & (r <= c), same & (c == r + 1) & (r % 2 == 0)]
    masks += [same & (r // b % 2 == 1) & (c // b == r // b - 1) for b in (2, 4, 8, 16, 32)]
    arrays = {
        "h0": np.concatenate([i["meta_tokens"], one["x"]], axis=0),
        "columns": np.concatenate([channels(one[columns[name]]) for name, _ in COLUMNS], axis=1),
        "identity": np.eye(P, dtype=np.float32),
        "chunk_masks": np.stack(masks, axis=1).astype(np.float32),
        "w_in_tiles": np.concatenate([k_tiles(w_in[:, :s5_at], P), k_tiles(w_in[:, gates_at:], P)], axis=0),
        "w_in_s5": k_tiles(w_in[:, s5_at:gates_at], S5_GROUPS * S5_GROUP // 2),
        "lora": np.stack([np.concatenate([one["rwkv_w_up"], one["rwkv_a_up"]], axis=0), one["rwkv_g_up"]], axis=1),
        "w_mix_tiles": np.stack([k_tiles(w, P) for w in (one["rwkv_w_branch"], glu[:, :D_MODEL], glu[:, D_MODEL:])], axis=2),
        "w_out": one["w_out"].reshape(KD, P, D_MODEL),
        "mix_post": rows(one["norm_mix_post"]),
        "w_up_tiles": np.stack([k_tiles(up[:, :D_FF], P), k_tiles(up[:, D_FF:], P)], axis=2),
        "w_down": one["ffn_w_down"].reshape(M_FF, P, D_MODEL),
        "ffn_post": rows(one["norm_ffn_post"]),
        "lam_re": twice(one["s5_lambda_re"].T),
        "lam_im": twice(one["s5_lambda_im"].T),
        "log_dt": rows(one["s5_log_dt"]),
        "skip": np.tile(one["s5_d"].reshape(S5_GROUPS, S5_GROUP).T, (S5_CHUNK, 1)),
        "b_re": twice(one["s5_b_re"].transpose(1, 0, 2)),
        "b_im": twice(one["s5_b_im"].transpose(1, 0, 2)),
        "c_re": twice(one["s5_c_re"].transpose(2, 0, 1)),
        "c_im": twice(one["s5_c_im"].transpose(2, 0, 1)),
    }
    return {name: np.ascontiguousarray(a) for name, a in arrays.items()}


def kernel(**inputs):
    import numpy as np
    import concourse.bacc as bacc
    from concourse.bass_utils import run_bass_kernel_spmd

    arrays = lay_out(np, inputs)
    nc = bacc.Bacc("TRN2", target_bir_lowering=False, num_devices=1)
    ins = {name: nc.dram_tensor(f"in_{name}", a.shape, F32, kind="ExternalInput").ap() for name, a in arrays.items()}
    out = nc.dram_tensor("out_h", [SEQ, D_MODEL], F32, kind="ExternalOutput").ap()
    hybrid_block(nc, ins, out)
    r = run_bass_kernel_spmd(nc, [{f"in_{name}": a for name, a in arrays.items()}], core_ids=[0])
    return r.results[0]["out_h"].reshape(1, SEQ, D_MODEL)
```
